# Optimizing a Trainium2 kernel written in Bass

```python
import math
import jax, jax.numpy as jnp
from jax import lax
import numpy as np

D_MODEL = 2048
BATCH = 1
SEQ = 256
DEPTH = 1

DIFF_HEADS = 8
DIFF_D = 64
NSA_HEADS = 8
NSA_KV = 2
NSA_GROUP = NSA_HEADS // NSA_KV
NSA_DK = 128
NSA_DV = 128
CMP_LEN = 32
CMP_STRIDE = 16
CMP_HIDDEN = 256
SLC_LEN = 64
SLC_TOPK = 16
WINDOW = 512
N_BUCKETS = 32
MAX_DISTANCE = 128
D_FF = 5632
CONV_W = 3
Q_BLOCK = 128
EPS = 1e-6
NEG = -1e30
FORCE = 1e30
TINY = 1e-30

DIFF_QK = DIFF_HEADS * 2 * DIFF_D
DIFF_V = DIFF_HEADS * 2 * DIFF_D
NSA_Q = NSA_HEADS * NSA_DK
NSA_K = NSA_KV * NSA_DK
NSA_V = NSA_KV * NSA_DV
N_GATES = NSA_HEADS * 3
SPLIT_SIZES = (DIFF_QK, DIFF_QK, DIFF_V, NSA_Q, NSA_K, NSA_V, NSA_K, NSA_V, NSA_K, NSA_V, N_GATES)
IN_COLS = 2 * DIFF_QK + DIFF_V + NSA_Q + 3 * (NSA_K + NSA_V) + N_GATES
MIX_WIDTH = DIFF_HEADS * 2 * DIFF_D + NSA_HEADS * NSA_DV


def rms_norm(x, g):
    xf = x.astype(jnp.float32)
    y = xf * lax.rsqrt(jnp.mean(xf * xf, axis=-1, keepdims=True) + EPS)
    return (y * g.astype(jnp.float32)).astype(x.dtype)

def rel_bucket(delta):
    n = jnp.maximum(delta, 0)
    max_exact = N_BUCKETS // 2
    nf = jnp.maximum(n, 1).astype(jnp.float32)
    large = max_exact + (jnp.log(nf / max_exact) / math.log(MAX_DISTANCE / max_exact)
                         * (N_BUCKETS - max_exact)).astype(jnp.int32)
    large = jnp.minimum(large, N_BUCKETS - 1)
    return jnp.where(n < max_exact, n, large)

def masked_softmax(s, mask):
    s = jnp.where(mask, s, NEG)
    m = jnp.max(s, axis=-1, keepdims=True)
    p = jnp.exp(s - m) * mask
    return p / jnp.maximum(jnp.sum(p, axis=-1, keepdims=True), TINY)

def selection_map(nb, nc):
    r = SLC_LEN // CMP_STRIDE
    j = np.arange(nb)[:, None, None]
    m = np.arange(r)[None, :, None]
    n = np.arange(CMP_LEN // CMP_STRIDE)[None, None, :]
    c = r * j - m - n
    jj = np.broadcast_to(j, c.shape)
    valid = (c >= 0) & (c < nc)
    out = np.zeros((nb, nc), np.float32)
    np.add.at(out, (jj[valid], c[valid]), 1.0)
    return out

def compress(k, pos_emb, w1, w2):
    B, S, G, d = k.shape
    nc = (S - CMP_LEN) // CMP_STRIDE + 1
    idx = jnp.arange(nc)[:, None] * CMP_STRIDE + jnp.arange(CMP_LEN)[None, :]
    blocks = k[:, idx] + pos_emb[:, None, :]
    blocks = jnp.transpose(blocks, (0, 3, 1, 2, 4)).reshape(B, G, nc, CMP_LEN * d)
    return jax.nn.gelu(blocks @ w1, approximate=True) @ w2

def diff_attention(q, k, v, lam, lam_init, subln, bias_tab):
    B, H, S, _, d = q.shape
    nblk = S // Q_BLOCK
    kpos = jnp.arange(S)
    scale = d ** -0.5

    def block(i):
        s0 = i * Q_BLOCK
        qb = lax.dynamic_slice_in_dim(q, s0, Q_BLOCK, axis=2)
        qpos = s0 + jnp.arange(Q_BLOCK)
        delta = qpos[:, None] - kpos[None, :]
        bias = jnp.transpose(bias_tab[rel_bucket(delta)], (2, 0, 1))
        logits = jnp.einsum('bhqmd,bhkmd->bhmqk', qb, k).astype(jnp.float32) * scale + bias[None, :, None]
        p = masked_softmax(logits, (delta >= 0)[None, None, None])
        a = p[:, :, 0] - lam * p[:, :, 1]
        return jnp.einsum('bhqk,bhke->bhqe', a.astype(v.dtype), v)

    o = lax.map(block, jnp.arange(nblk))
    o = jnp.transpose(o, (1, 2, 0, 3, 4)).reshape(B, H, S, 2 * d)
    return rms_norm(o, subln) * (1.0 - lam_init)

def nsa_attention(q, k_cmp, v_cmp, k_slc, v_slc, k_win, v_win, gates, bias_nsa):
    B, G, Hg, S, dk = q.shape
    nc = k_cmp.shape[2]
    nb = S // SLC_LEN
    topk = min(SLC_TOPK, nb)
    nsel = topk * SLC_LEN
    scale = dk ** -0.5
    sel_map = jnp.asarray(selection_map(nb, nc))
    cmp_end = jnp.arange(nc) * CMP_STRIDE + (CMP_LEN - 1)
    ks_blk = k_slc.reshape(B, G, nb, SLC_LEN, dk)
    vs_blk = v_slc.reshape(B, G, nb, SLC_LEN, -1)
    pad = ((0, 0), (0, 0), (WINDOW, 0), (0, 0))
    kw_pad = jnp.pad(k_win, pad)
    vw_pad = jnp.pad(v_win, pad)
    table_g = jnp.transpose(bias_nsa, (1, 0, 2))
    bi = jnp.arange(B)[:, None, None, None]
    gi = jnp.arange(G)[None, :, None, None]
    blk = jnp.arange(nb)

    def block(i):
        s0 = i * Q_BLOCK
        qb = lax.dynamic_slice_in_dim(q, s0, Q_BLOCK, axis=3)
        gb = lax.dynamic_slice_in_dim(gates, s0, Q_BLOCK, axis=3)
        qpos = s0 + jnp.arange(Q_BLOCK)
        lc = jnp.einsum('bghqd,bgcd->bghqc', qb, k_cmp).astype(jnp.float32) * scale
        pc = masked_softmax(lc, cmp_end[None, :] <= qpos[:, None])
        o_cmp = jnp.einsum('bghqc,bgcd->bghqd', pc.astype(v_cmp.dtype), v_cmp)
        imp = jnp.einsum('bgqc,jc->bgqj', jnp.sum(pc, axis=2), sel_map)
        cur = (qpos // SLC_LEN)[:, None]
        forced = (blk[None] == 0) | (blk[None] == cur) | (blk[None] == cur - 1)
        imp = jnp.where(forced, FORCE, jnp.where(blk[None] <= cur, imp, NEG))
        _, idx = lax.top_k(imp, topk)
        k_sel = ks_blk[bi, gi, idx].reshape(B, G, Q_BLOCK, nsel, dk)
        v_sel = vs_blk[bi, gi, idx].reshape(B, G, Q_BLOCK, nsel, -1)
        kpos_sel = (idx[..., None] * SLC_LEN + jnp.arange(SLC_LEN)).reshape(B, G, Q_BLOCK, nsel)
        d_sel = qpos[:, None] - kpos_sel
        b_sel = jnp.transpose(table_g[gi, rel_bucket(d_sel)], (0, 1, 4, 2, 3))
        ls = jnp.einsum('bghqd,bgqkd->bghqk', qb, k_sel).astype(jnp.float32) * scale + b_sel
        ps = masked_softmax(ls, (d_sel >= 0)[:, :, None])
        o_slc = jnp.einsum('bghqk,bgqkd->bghqd', ps.astype(v_sel.dtype), v_sel)
        kwb = lax.dynamic_slice_in_dim(kw_pad, s0, Q_BLOCK + WINDOW, axis=2)
        vwb = lax.dynamic_slice_in_dim(vw_pad, s0, Q_BLOCK + WINDOW, axis=2)
        kpos_w = s0 - WINDOW + jnp.arange(Q_BLOCK + WINDOW)
        d_w = qpos[:, None] - kpos_w[None, :]
        wmask = (d_w >= 0) & (d_w < WINDOW) & (kpos_w[None, :] >= 0)
        b_w = jnp.transpose(bias_nsa[rel_bucket(d_w)], (2, 3, 0, 1))
        lw = jnp.einsum('bghqd,bgkd->bghqk', qb, kwb).astype(jnp.float32) * scale + b_w
        pw = masked_softmax(lw, wmask)
        o_win = jnp.einsum('bghqk,bgkd->bghqd', pw.astype(vwb.dtype), vwb)
        return gb[..., 0:1] * o_cmp + gb[..., 1:2] * o_slc + gb[..., 2:3] * o_win

    o = lax.map(block, jnp.arange(S // Q_BLOCK))
    return jnp.transpose(o, (1, 2, 3, 0, 4, 5)).reshape(B, G, Hg, S, -1)

def causal_dwconv(u, w, b):
    S = u.shape[1]
    up = jnp.pad(u, ((0, 0), (CONV_W - 1, 0), (0, 0)))
    y = b
    for j in range(CONV_W):
        y = y + w[j] * up[:, j:j + S]
    return y

def first_inputs(seed: int = 0) -> dict:
    key = jax.random.key(seed)
    ks = jax.random.split(key, 24)
    f32 = jnp.float32

    def nrm(k, shape, scale):
        return jax.random.normal(k, shape, f32) * scale

    def gain(k, shape):
        return 1.0 + 0.05 * jax.random.normal(k, shape, f32)

    return {
        'x': nrm(ks[0], (BATCH, SEQ, D_MODEL), 1.0),
        'pre_mix_norm': gain(ks[1], (DEPTH, D_MODEL)),
        'w_in': nrm(ks[2], (DEPTH, D_MODEL, IN_COLS), D_MODEL ** -0.5),
        'lambda_q1': nrm(ks[3], (DEPTH, DIFF_D), 0.1),
        'lambda_k1': nrm(ks[4], (DEPTH, DIFF_D), 0.1),
        'lambda_q2': nrm(ks[5], (DEPTH, DIFF_D), 0.1),
        'lambda_k2': nrm(ks[6], (DEPTH, DIFF_D), 0.1),
        'diff_subln': gain(ks[7], (DEPTH, 2 * DIFF_D)),
        'cmp_pos_k': nrm(ks[8], (DEPTH, CMP_LEN, NSA_DK), 0.1),
        'cmp_pos_v': nrm(ks[9], (DEPTH, CMP_LEN, NSA_DV), 0.1),
        'cmp_k_w1': nrm(ks[10], (DEPTH, CMP_LEN * NSA_DK, CMP_HIDDEN), (CMP_LEN * NSA_DK) ** -0.5),
        'cmp_k_w2': nrm(ks[11], (DEPTH, CMP_HIDDEN, NSA_DK), CMP_HIDDEN ** -0.5),
        'cmp_v_w1': nrm(ks[12], (DEPTH, CMP_LEN * NSA_DV, CMP_HIDDEN), (CMP_LEN * NSA_DV) ** -0.5),
        'cmp_v_w2': nrm(ks[13], (DEPTH, CMP_HIDDEN, NSA_DV), CMP_HIDDEN ** -0.5),
        'rel_bias': nrm(ks[14], (N_BUCKETS, DIFF_HEADS + NSA_HEADS), 0.5),
        'w_out': nrm(ks[15], (DEPTH, MIX_WIDTH, D_MODEL), MIX_WIDTH ** -0.5),
        'post_mix_norm': gain(ks[16], (DEPTH, D_MODEL)),
        'pre_ffn_norm': gain(ks[17], (DEPTH, D_MODEL)),
        'w_up': nrm(ks[18], (DEPTH, D_MODEL, 2 * D_FF), D_MODEL ** -0.5),
        'conv_w': nrm(ks[19], (DEPTH, CONV_W, 2 * D_FF), CONV_W ** -0.5),
        'conv_b': nrm(ks[20], (DEPTH, 2 * D_FF), 0.01),
        'w_down': nrm(ks[21], (DEPTH, D_FF, D_MODEL), D_FF ** -0.5),
        'post_ffn_norm': gain(ks[22], (DEPTH, D_MODEL)),
    }

def first_block(x, pre_mix_norm, w_in, lambda_q1, lambda_k1, lambda_q2, lambda_k2, diff_subln,
              cmp_pos_k, cmp_pos_v, cmp_k_w1, cmp_k_w2, cmp_v_w1, cmp_v_w2, rel_bias, w_out,
              post_mix_norm, pre_ffn_norm, w_up, conv_w, conv_b, w_down, post_ffn_norm):
    B, S, _ = x.shape
    f32 = jnp.float32
    offsets = np.cumsum(SPLIT_SIZES)[:-1].tolist()
    bias_diff = rel_bias[:, :DIFF_HEADS]
    bias_nsa = rel_bias[:, DIFF_HEADS:].reshape(N_BUCKETS, NSA_KV, NSA_GROUP)
    for l in range(DEPTH):
        h = rms_norm(x, pre_mix_norm[l])
        proj = h @ w_in[l]
        (dq, dk, dv, nq, kc, vc, ksl, vsl, kwn, vwn, g) = jnp.split(proj, offsets, axis=-1)
        q_d = dq.reshape(B, S, DIFF_HEADS, 2, DIFF_D).transpose(0, 2, 1, 3, 4)
        k_d = dk.reshape(B, S, DIFF_HEADS, 2, DIFF_D).transpose(0, 2, 1, 3, 4)
        v_d = dv.reshape(B, S, DIFF_HEADS, 2 * DIFF_D).transpose(0, 2, 1, 3)
        lam_init = 0.8 - 0.6 * math.exp(-0.3 * l)
        lam = (jnp.exp(jnp.sum(lambda_q1[l].astype(f32) * lambda_k1[l].astype(f32)))
               - jnp.exp(jnp.sum(lambda_q2[l].astype(f32) * lambda_k2[l].astype(f32))) + lam_init)
        o_diff = diff_attention(q_d, k_d, v_d, lam, lam_init, diff_subln[l], bias_diff)
        q_n = nq.reshape(B, S, NSA_KV, NSA_GROUP, NSA_DK).transpose(0, 2, 3, 1, 4)
        k_c = compress(kc.reshape(B, S, NSA_KV, NSA_DK), cmp_pos_k[l], cmp_k_w1[l], cmp_k_w2[l])
        v_c = compress(vc.reshape(B, S, NSA_KV, NSA_DV), cmp_pos_v[l], cmp_v_w1[l], cmp_v_w2[l])
        k_s = ksl.reshape(B, S, NSA_KV, NSA_DK).transpose(0, 2, 1, 3)
        v_s = vsl.reshape(B, S, NSA_KV, NSA_DV).transpose(0, 2, 1, 3)
        k_w = kwn.reshape(B, S, NSA_KV, NSA_DK).transpose(0, 2, 1, 3)
        v_w = vwn.reshape(B, S, NSA_KV, NSA_DV).transpose(0, 2, 1, 3)
        gates = jax.nn.sigmoid(g.reshape(B, S, NSA_KV, NSA_GROUP, 3)).transpose(0, 2, 3, 1, 4)
        o_nsa = nsa_attention(q_n, k_c, v_c, k_s, v_s, k_w, v_w, gates, bias_nsa)
        mix = jnp.concatenate([o_diff.transpose(0, 2, 1, 3).reshape(B, S, -1),
                               o_nsa.transpose(0, 3, 1, 2, 4).reshape(B, S, -1)], axis=-1)
        x = x + rms_norm(mix @ w_out[l], post_mix_norm[l])
        h = rms_norm(x, pre_ffn_norm[l])
        u = causal_dwconv(h @ w_up[l], conv_w[l], conv_b[l])
        gate, up = jnp.split(u, 2, axis=-1)
        y = (jax.nn.gelu(gate, approximate=True) * up) @ w_down[l]
        x = x + rms_norm(y, post_ffn_norm[l])
    return x


HEAD_DIM = 128
MOBA_HEADS = 8
MOBA_BLOCK = 256
MOBA_TOPK = 3
MOBA_Q_CHUNK = 32
SB_HEADS = 8
SB_Q_BLOCK = 128
POOL_WINDOWS = (2, 4, 8, 16)
POOL_GROUPS = len(POOL_WINDOWS)
POOL_GROUP = 256
POOL_WIDTH = POOL_GROUP * POOL_GROUPS
MOBA_WIDTH = MOBA_HEADS * HEAD_DIM
SB_WIDTH = SB_HEADS * HEAD_DIM
N_BRANCH = 3
IN_WIDTH = 3 * MOBA_WIDTH + POOL_WIDTH + 3 * SB_WIDTH + N_BRANCH * D_MODEL
D_FF_2 = -(-8 * D_MODEL // (3 * 256)) * 256
REL_BUCKETS = 32
REL_MAX_EXACT = 16
REL_MAX_DIST = 2048
NEG_2 = -1e30


def rms_norm_2(x, g):
    xf = x.astype(jnp.float32)
    y = xf * lax.rsqrt(jnp.mean(xf * xf, axis=-1, keepdims=True) + EPS)
    return (y * g.astype(jnp.float32)).astype(x.dtype)

def rel_bucket_2(dist):
    n = jnp.maximum(dist, 0)
    nf = jnp.maximum(n, 1).astype(jnp.float32)
    large = REL_MAX_EXACT + (jnp.log(nf / REL_MAX_EXACT) / math.log(REL_MAX_DIST / REL_MAX_EXACT)
                             * (REL_BUCKETS - REL_MAX_EXACT)).astype(jnp.int32)
    large = jnp.minimum(large, REL_BUCKETS - 1)
    return jnp.where(n < REL_MAX_EXACT, n, large)

def moba_attention(q, k, v, rel_table):
    B, H, S, Dh = q.shape
    nb = -(-S // MOBA_BLOCK)
    pad = nb * MOBA_BLOCK - S
    kb = jnp.pad(k, ((0, 0), (0, 0), (0, pad), (0, 0))).reshape(B, H, nb, MOBA_BLOCK, Dh)
    vb = jnp.pad(v, ((0, 0), (0, 0), (0, pad), (0, 0))).reshape(B, H, nb, MOBA_BLOCK, Dh)
    kbar = jnp.mean(kb.astype(jnp.float32), axis=3)
    topk = min(MOBA_TOPK, nb)
    scale = Dh ** -0.5
    bi = jnp.arange(B)[:, None, None, None]
    hi = jnp.arange(H)[None, :, None, None]
    hi5 = jnp.arange(H)[None, :, None, None, None]
    blk_off = jnp.arange(MOBA_BLOCK)
    Q = MOBA_Q_CHUNK

    def chunk(c):
        t0 = c * Q
        qc = lax.dynamic_slice_in_dim(q, t0, Q, axis=2).astype(jnp.float32)
        pos = t0 + jnp.arange(Q)
        own = t0 // MOBA_BLOCK
        gate = jnp.einsum('bhqd,bhnd->bhqn', qc, kbar)
        gate = jnp.where(jnp.arange(nb) < own, gate, -jnp.inf)
        _, idx = lax.top_k(gate, topk)
        valid = jnp.arange(topk) < own
        ksel = kb[bi, hi, idx].astype(jnp.float32)
        vsel = vb[bi, hi, idx].astype(jnp.float32)
        s_sel = jnp.einsum('bhqd,bhqnkd->bhqnk', qc, ksel) * scale
        key_pos = idx[..., None] * MOBA_BLOCK + blk_off
        bias_sel = rel_table[hi5, rel_bucket_2(pos[:, None, None] - key_pos)].astype(jnp.float32)
        s_sel = jnp.where(valid[:, None], s_sel + bias_sel, NEG_2)
        k_own = lax.dynamic_index_in_dim(kb, own, axis=2, keepdims=False).astype(jnp.float32)
        v_own = lax.dynamic_index_in_dim(vb, own, axis=2, keepdims=False).astype(jnp.float32)
        d_own = pos[:, None] - (own * MOBA_BLOCK + blk_off)[None, :]
        s_own = jnp.einsum('bhqd,bhkd->bhqk', qc, k_own) * scale
        s_own = jnp.where(d_own >= 0, s_own + rel_table[:, rel_bucket_2(d_own)].astype(jnp.float32)[None], NEG_2)
        logits = jnp.concatenate([s_sel.reshape(B, H, Q, topk * MOBA_BLOCK), s_own], axis=-1)
        p = jax.nn.softmax(logits, axis=-1)
        p_sel = p[..., :topk * MOBA_BLOCK].reshape(B, H, Q, topk, MOBA_BLOCK)
        p_own = p[..., topk * MOBA_BLOCK:]
        return (jnp.einsum('bhqnk,bhqnkd->bhqd', p_sel, vsel)
                + jnp.einsum('bhqk,bhkd->bhqd', p_own, v_own))

    out = lax.map(chunk, jnp.arange(S // Q))
    return jnp.moveaxis(out, 0, 2).reshape(B, H, S, Dh).astype(q.dtype)

def stick_breaking_attention(q, k, v):
    B, H, S, Dh = q.shape
    scale = Dh ** -0.5
    outs = []
    for t0 in range(0, S, SB_Q_BLOCK):
        t1 = t0 + SB_Q_BLOCK
        qc = q[:, :, t0:t1].astype(jnp.float32)
        kc = k[:, :, :t1].astype(jnp.float32)
        vc = v[:, :, :t1].astype(jnp.float32)
        z = jnp.einsum('bhqd,bhkd->bhqk', qc, kc) * scale
        causal = jnp.arange(t1)[None, :] < jnp.arange(t0, t1)[:, None]
        log_beta = jax.nn.log_sigmoid(z)
        log_1m = jnp.where(causal, jax.nn.log_sigmoid(-z), 0.0)
        after = lax.cumsum(log_1m, axis=3, reverse=True) - log_1m
        a = jnp.where(causal, jnp.exp(log_beta + after), 0.0)
        outs.append(jnp.einsum('bhqk,bhkd->bhqd', a, vc))
    return jnp.concatenate(outs, axis=2).astype(q.dtype)

def multiscale_pool(u, w_grp, scale):
    B, S, _ = u.shape
    ug = u.astype(jnp.float32).reshape(B, S, POOL_GROUPS, POOL_GROUP)
    cs = jnp.concatenate([jnp.zeros((B, 1, POOL_GROUPS, POOL_GROUP), jnp.float32),
                          jnp.cumsum(ug, axis=1)], axis=1)
    t = jnp.arange(S)
    pooled = []
    for gi, w in enumerate(POOL_WINDOWS):
        lo = jnp.maximum(t + 1 - w, 0)
        cnt = (t + 1 - lo).astype(jnp.float32)
        mean = (cs[:, 1:, gi] - cs[:, lo, gi]) / cnt[:, None]
        pooled.append(mean - ug[:, :, gi])
    p = jnp.stack(pooled, axis=2)
    y = jnp.einsum('bsgc,gcd->bsgd', p, w_grp.astype(jnp.float32)).reshape(B, S, POOL_WIDTH)
    return (y * scale.astype(jnp.float32)).astype(u.dtype)

def hybrid_mixer(h, w_in, w_pool, pool_scale, w_br_a, w_br_b, w_br_c, w_out, rel_table):
    B, S, _ = h.shape
    proj = h @ w_in
    offs = np.cumsum([MOBA_WIDTH, MOBA_WIDTH, MOBA_WIDTH, POOL_WIDTH, SB_WIDTH, SB_WIDTH, SB_WIDTH]).tolist()
    qa, ka, va, u, qs, ks, vs, gates = jnp.split(proj, offs, axis=-1)
    to_heads = lambda t, nh: t.reshape(B, S, nh, HEAD_DIM).transpose(0, 2, 1, 3)
    from_heads = lambda t: t.transpose(0, 2, 1, 3).reshape(B, S, -1)
    ya = from_heads(moba_attention(to_heads(qa, MOBA_HEADS), to_heads(ka, MOBA_HEADS),
                                   to_heads(va, MOBA_HEADS), rel_table))
    yb = multiscale_pool(u, w_pool, pool_scale)
    yc = from_heads(stick_breaking_attention(to_heads(qs, SB_HEADS), to_heads(ks, SB_HEADS),
                                             to_heads(vs, SB_HEADS)))
    g = jax.nn.sigmoid(gates.astype(jnp.float32)).reshape(B, S, N_BRANCH, D_MODEL)
    m = (g[:, :, 0] * (ya @ w_br_a).astype(jnp.float32)
         + g[:, :, 1] * (yb @ w_br_b).astype(jnp.float32)
         + g[:, :, 2] * (yc @ w_br_c).astype(jnp.float32))
    return m.astype(h.dtype) @ w_out

def swiglu(h, w_gate, w_up, w_down):
    return (jax.nn.silu(h @ w_gate) * (h @ w_up)) @ w_down

def second_inputs(seed: int = 0) -> dict:
    key = jax.random.key(seed)
    ks = jax.random.split(key, 16)
    nrm = lambda k, shape, fan: jax.random.normal(k, shape, jnp.float32) * (fan ** -0.5)
    return {
        "x": jax.random.normal(ks[0], (BATCH, SEQ, D_MODEL), jnp.float32),
        "norm_mix": 1.0 + 0.02 * jax.random.normal(ks[1], (DEPTH, D_MODEL), jnp.float32),
        "norm_ffn": 1.0 + 0.02 * jax.random.normal(ks[2], (DEPTH, D_MODEL), jnp.float32),
        "w_in": nrm(ks[3], (DEPTH, D_MODEL, IN_WIDTH), D_MODEL),
        "w_pool": nrm(ks[4], (DEPTH, POOL_GROUPS, POOL_GROUP, POOL_GROUP), POOL_GROUP),
        "pool_scale": 1.0 + 0.02 * jax.random.normal(ks[5], (DEPTH, POOL_WIDTH), jnp.float32),
        "w_br_a": nrm(ks[6], (DEPTH, MOBA_WIDTH, D_MODEL), MOBA_WIDTH),
        "w_br_b": nrm(ks[7], (DEPTH, POOL_WIDTH, D_MODEL), POOL_WIDTH),
        "w_br_c": nrm(ks[8], (DEPTH, SB_WIDTH, D_MODEL), SB_WIDTH),
        "w_out": nrm(ks[9], (DEPTH, D_MODEL, D_MODEL), D_MODEL),
        "w_gate": nrm(ks[10], (DEPTH, D_MODEL, D_FF_2), D_MODEL),
        "w_up": nrm(ks[11], (DEPTH, D_MODEL, D_FF_2), D_MODEL),
        "w_down": nrm(ks[12], (DEPTH, D_FF_2, D_MODEL), D_FF_2),
        "rel_bias": 0.5 * jax.random.normal(ks[13], (MOBA_HEADS, REL_BUCKETS), jnp.float32),
        "norm_final": 1.0 + 0.02 * jax.random.normal(ks[14], (D_MODEL,), jnp.float32),
    }

def second_block(x, norm_mix, norm_ffn, w_in, w_pool, pool_scale, w_br_a, w_br_b, w_br_c,
              w_out, w_gate, w_up, w_down, rel_bias, norm_final):
    h = x
    for l in range(DEPTH):
        h = h + hybrid_mixer(rms_norm_2(h, norm_mix[l]), w_in[l], w_pool[l], pool_scale[l],
                             w_br_a[l], w_br_b[l], w_br_c[l], w_out[l], rel_bias)
        h = h + swiglu(rms_norm_2(h, norm_ffn[l]), w_gate[l], w_up[l], w_down[l])
    return rms_norm_2(h, norm_final)


def setup_inputs(seed=0):
    out = dict(first_inputs(seed))
    for name, value in second_inputs(seed + 1).items():
        if name != "x":
            out[name + "_2"] = value
    return out


def reference(
    x, pre_mix_norm, w_in, lambda_q1, lambda_k1, lambda_q2, lambda_k2, diff_subln, cmp_pos_k,
    cmp_pos_v, cmp_k_w1, cmp_k_w2, cmp_v_w1, cmp_v_w2, rel_bias, w_out, post_mix_norm,
    pre_ffn_norm, w_up, conv_w, conv_b, w_down, post_ffn_norm, norm_mix_2, norm_ffn_2, w_in_2,
    w_pool_2, pool_scale_2, w_br_a_2, w_br_b_2, w_br_c_2, w_out_2, w_gate_2, w_up_2, w_down_2,
    rel_bias_2, norm_final_2,
):
    x = first_block(
        x, pre_mix_norm, w_in, lambda_q1, lambda_k1, lambda_q2, lambda_k2, diff_subln,
        cmp_pos_k, cmp_pos_v, cmp_k_w1, cmp_k_w2, cmp_v_w1, cmp_v_w2, rel_bias, w_out,
        post_mix_norm, pre_ffn_norm, w_up, conv_w, conv_b, w_down, post_ffn_norm,
    )
    return second_block(
        x, norm_mix_2, norm_ffn_2, w_in_2, w_pool_2, pool_scale_2, w_br_a_2, w_br_b_2, w_br_c_2,
        w_out_2, w_gate_2, w_up_2, w_down_2, rel_bias_2, norm_final_2,
    )


_drawn_inputs = setup_inputs


def setup_inputs(seed=0):
    import zlib

    import numpy as np

    out = dict(_drawn_inputs(seed))
    spreads = {}
    factors = {'lambda_q2': 42.662,
     'cmp_pos_k': 8.0,
     'conv_b': 6.469,
     'norm_mix_2': 7.006,
     'norm_ffn_2': 19.254,
     'pool_scale_2': 8.0,
     'norm_final_2': 7.915,
     'rel_bias_2': 5.895}
    for name, (base, spread) in spreads.items():
        noise = np.random.default_rng([zlib.crc32(name.encode()), seed]).standard_normal(out[name].shape)
        drawn = base * np.exp(spread * noise) if base else spread * noise
        out[name] = __import__('jax').numpy.asarray(drawn.astype(out[name].dtype))
    for name, factor in factors.items():
        out[name] = (out[name] * factor).astype(out[name].dtype)
    return out
```

```python
import math
from contextlib import ExitStack

import numpy as np

import concourse.bass as bass
from concourse import mybir

F32 = mybir.dt.float32
F32R = mybir.dt.float32r
ACT = mybir.ActivationFunctionType
ALU = mybir.AluOpType
AX = mybir.AxisListType

P = 128
T = 256
D = 2048
NK = D // P
F = 5632
NF = F // P
NB = 256
FB = F // NB
KC = 4
RAW = 8
SPL = 4
HEADS = 8
NC = (T - 32) // 16 + 1
NEG = -1e30
TINY = 1e-30
EPS = 1e-6
LAM_INIT = 0.8 - 0.6 * math.exp(0.0)
COLS, TOKS = 0, 1
LAG = 3
KB = 1024

IDENT, FLIP, LOWER, ONES, SBMASK, CNT, CNEG, CONE, HOT1, HOT2 = np.cumsum([0, 128, 128, 128, 128, 384, 64, 2 * NC, 2 * NC, 256]).tolist()
NCONST = HOT2 + 256

VECS = [("pre_mix_norm", 16), ("pre_ffn_norm", 16), ("norm_mix_2", 16), ("norm_ffn_2", 16), ("pool_scale_2", 8),
        ("diff_subln", 1), ("conv_b", 88), ("conv_w0", 88), ("conv_w1", 88), ("conv_w2", 88), ("cmp_pos_k", 32), ("cmp_pos_v", 32)]
VEC_TILES = [[0, 1, 2, 3, 4, 5], [6], [7], [8], [9], [10, 11]]
VAT = dict(zip([n for n, _ in VECS], np.cumsum([0] + [n for _, n in VECS]).tolist()))
NVEC = sum(n for _, n in VECS)


def shape_constants():
    c = np.zeros((P, NCONST), np.float32)
    r = np.arange(P)
    c[r, IDENT + r] = 1
    c[r, FLIP + P - 1 - r] = 1
    c[:, LOWER:LOWER + P] = -(r[:, None] >= r[None, :]).astype(np.float32)
    c[:, ONES:ONES + P] = -1
    strict = np.where(r[:, None] < r[None, :], 0, NEG)
    c[:, SBMASK:SBMASK + P] = strict
    c[:, SBMASK + 2 * P:SBMASK + 3 * P] = strict
    for g in range(4):
        c[:, CNT + 16 * g:CNT + 16 * (g + 1)] = 1.0 / np.minimum(np.arange(16) + 1, 2 << g)
    for a in range(2):
        ok = (np.arange(NC) * 16 + 31)[None, :] <= (r + a * P)[:, None]
        c[:, CNEG + a * NC:CNEG + (a + 1) * NC] = np.where(ok, 0, NEG)
        c[:, CONE + a * NC:CONE + (a + 1) * NC] = ok
    for at, far in ((HOT1, 128), (HOT2, 2048)):
        d = T - 1 - np.arange(T)
        large = 16 + (np.log(np.maximum(d, 1) / 16) / math.log(far / 16) * 16).astype(np.int32)
        bucket = np.where(d < 16, d, np.minimum(large, 31))
        c[bucket, at + np.arange(T)] = 1
    return c


class Phase:

    unit = block = slot = 0
    loads = [0] * RAW

    @classmethod
    def reset(cls):
        cls.unit = cls.block = cls.slot = 0
        cls.loads = [0] * RAW

    def __init__(self, iters, blocks, nblocks=None):
        self.iters, self.blocks = iters, blocks
        self.n = sum(blocks)
        self.nb = nblocks or len(blocks)
        self.u0, self.b0, self.rot = Phase.unit, Phase.block, Phase.slot
        self.loads0 = list(Phase.loads)
        Phase.unit += iters * self.n
        Phase.block += iters * self.nb
        Phase.slot = (self.rot + self.n) % RAW
        self.per = [sum(self.slot_of(c) == s for c in range(self.n)) for s in range(RAW)]
        Phase.loads = [a + iters * b for a, b in zip(Phase.loads, self.per)]

    def slot_of(self, c):
        return (self.rot + c) % RAW

    def units(self, i, c):
        return self.u0 + i * self.n + c + 1

    def blocks_(self, i, b):
        return self.b0 + i * self.nb + b + 1

    def before(self, i, c, ring):
        if c >= ring or self.iters == 1:
            prev = c - ring
        else:
            prev = c + (self.n - 1 - c) // ring * ring - self.n
        return self.units(i, prev)

    def loaded(self, i, c):
        s = self.slot_of(c)
        nth = sum(self.slot_of(x) == s for x in range(c + 1))
        return 16 * (self.loads0[s] + i * self.per[s] + nth)

    def where(self, c):
        for b, k in enumerate(self.blocks):
            if c < k:
                return b, c
            c -= k

    def ends(self):
        out, e = [], -1
        for b, k in enumerate(self.blocks):
            e += k
            out.append(((e + LAG) % self.n if self.n > LAG else 0, b, e + LAG >= self.n))
        return out


def two_blocks(nc, w, out):
    Phase.reset()
    diff_qk = Phase(4, [4, 4])
    diff_v = Phase(2, [4, 4])
    nsa_q = Phase(3, [4, 4])
    nsa_k = Phase(1, [4, 4])
    nsa_v = Phase(1, [4, 4])
    squeeze = Phase(1, [8, 8])
    out_a = Phase(2, [2, 2, 2, 2])
    out_b = Phase(2, [2, 2, 2, 2])
    up1 = Phase(FB, [4, 4])
    down1 = Phase(4, [11, 11])
    sb_qk = Phase(4, [4, 4])
    sb_v = Phase(2, [4, 4])
    moba_qk = Phase(4, [4, 4])
    moba_v = Phase(2, [4, 4])
    pool_u = Phase(2, [4, 4])
    pool_w = Phase(1, [1, 1], nblocks=4)
    merge = Phase(8, [4, 2, 4, 2, 4, 2])
    out_2 = Phase(4, [4, 4])
    up2 = Phase(FB, [4, 4])
    down2 = Phase(4, [11, 11])

    with ExitStack() as ctx:
        def sem(name):
            return ctx.enter_context(nc.semaphore(name))

        BASE = (nc.sbuf_base + 31) // 32 * 32
        at = [BASE]

        def fixed(name, shape, dt=F32):
            t = nc.alloc_sbuf_tensor_at(name, shape, dt, offset=at[0])
            at[0] += (int(np.prod(shape[1:])) * 4 + 31) // 32 * 32
            return t.ap() if hasattr(t, "ap") and callable(t.ap) else t

        raw = fixed("raw", [P, RAW, KC, NB])
        spl = fixed("spl", [P, SPL, KC, 2, NB], F32R)
        HA0 = at[0]
        HA = fixed("HA", [P, NK, 2, T], F32R)
        k1 = fixed("k1", [P, CNEG])
        vec = fixed("vec", [P, NVEC])
        st = fixed("st", [P, 128])
        gates = fixed("gates", [P, 2, 24])
        neg_lam = fixed("neg_lam", [P, 1])
        lsum = fixed("lsum", [P, 4])
        G0 = at[0]

        def inG(name, kb, shape, dt=F32, base=G0):
            t = nc.alloc_sbuf_tensor_at(name, shape, dt, offset=int(base + kb * KB))
            assert base != G0 or kb * KB + int(np.prod(shape[1:])) * 4 <= 104 * KB, name
            return t.ap() if hasattr(t, "ap") and callable(t.ap) else t

        def inH(name, kb, shape, dt=F32):
            assert kb * KB + int(np.prod(shape[1:])) * 4 <= 32 * KB, name
            return inG(name, kb, shape, dt, HA0)

        x0 = inG("x0", 0, [P, 2, D])
        xn0 = inG("xn0", 16, [P, 2, D])
        rows = inG("rows", 32, [P, 6, P])
        k2 = inG("k2", 36, [P, NCONST - CNEG])
        tab1 = inG("tab1", 42, [P, 16])
        tab2 = inG("tab2", 42.25, [P, 8])
        rbias = inG("rbias", 42.5, [P, 2, 384])
        lamv = inG("lamv", 46, [P, 4, 64])
        lamp = inG("lamp", 47, [P, 2, 64])
        gw = inG("gw", 48, [P, NK, 24])
        gws = inG("gws", 50, [P, NK, 2, 24], F32R)
        hank1 = inG("hank1", 54, [P, 16, T])
        QK = inG("QK", 0, [P, 16, T])
        DV = inG("DV", 16, [P, 2, 1024])
        NQ = inG("NQ", 24, [P, 12, T])
        NKs = inG("NKs", 36, [P, 4, T])
        NVs = inG("NVs", 40, [P, 2, 2, T])
        MIX = inG("MIX", 44, [P, NK, 2, T], F32R)
        OD = inG("OD", 60, [P, 2, HEADS, P])
        bias1 = inG("bias1", 76, [P, 16, T])
        LG = inG("LG", 92, [P, 2, 2, 384])
        PT = inG("PT", 98, [P, 2, 2, 384])
        kblk = inG("kblk", 92, [P, 32, 2 * NC])
        vblk = inG("vblk", 96, [P, 32, 2 * NC])
        ksp = inG("ksp", 0, [P, 32, 2, 2 * NC], F32R)
        vsp = inG("vsp", 8, [P, 32, 2, 2 * NC], F32R)
        w2 = inH("w2", 22.5, [P, 2, 2, P])
        hid = inH("hid", 24.5, [P, 2, 2, 2 * NC])
        kcT = inH("kcT", 25, [P, 2 * NC])
        vcr = inH("vcr", 25.25, [P, 2, P])
        PC = inH("PC", 26.25, [P, 2, HEADS, 32])
        cl = inH("cl", 28.25, [P, 2, HEADS, NC])
        PcT = inH("PcT", 29.25, [P, 2, T])
        cmk = inH("cmk", 31.25, [P, 4, NC])
        Y1 = inG("Y1", 0, [P, 2, D])
        gain1 = inG("gain1", 32, [P, D])
        X1 = inG("X1", 88, [P, 2, D])
        xn1 = inG("xn1", 16, [P, 2, D])
        ya_tmp = inG("ya_tmp", 40, [P, 2, 2, NB])
        FF = inG("FF", 0, [P, NF, 2, T], F32R)
        U = inG("U", 88, [P, 2, T])
        CV = inG("CV", 90, [P, 2, T])
        GL = inG("GL", 92, [P, 2, T])
        HF = inG("HF", 94, [P, 2, T])
        Yd = inH("Yd", 0, [P, 2, D])
        Xd = inH("Xd", 16, [P, 2, D])
        gain2 = inG("gain2", 96, [P, D])
        X2 = inG("X2", 48, [P, 2, D])
        xn2 = inG("xn2", 64, [P, 2, D])
        hank2 = inG("hank2", 88, [P, 8, T])
        SQK = inG("SQK", 0, [P, 16, T])
        SV = inG("SV", 16, [P, 2, 1024])
        MQK = inG("MQK", 24, [P, 16, T])
        MV = inG("MV", 40, [P, 2, 1024])
        YA = inG("YA", 48, [P, 8, 2, T], F32R)
        YC = inG("YC", 64, [P, 8, 2, T], F32R)
        bias2 = inG("bias2", 80, [P, 8, T])
        SZ = inG("SZ", 88, [P, 2, 4, 384])
        UP = inG("UP", 88, [P, 8, T])
        LM = inG("LM", 96, [P, 2, 384])
        PM = inG("PM", 99, [P, 2, 384])
        PS = inG("PS", 24, [P, 8, 2, T], F32R)
        PW = inG("PW", 40, [P, 2, T])
        PX = inG("PX", 42, [P, 2, T])
        YB = inG("YB", 0, [P, 8, 2, T], F32R)
        MM = inG("MM", 16, [P, NK, 2, T], F32R)
        GT = inG("GT", 88, [P, 2, T])
        GS = inG("GS", 90, [P, 2, T])
        BR = inG("BR", 92, [P, 2, T])
        MA = inG("MA", 94, [P, 2, T])
        Y3 = inG("Y3", 48, [P, 2, D])
        X3 = inG("X3", 64, [P, 2, D])
        xn3 = inG("xn3", 0, [P, 2, D])
        fin = inG("fin", 0, [P, 2, D])

        ps = ctx.enter_context(nc.psum_tensor("ps", [P, 8, 512], F32))
        table = nc.dram_tensor("table", [24, 384], F32, kind="Internal").ap()
        spill = nc.dram_tensor("spill", [3, T, D], F32, kind="Internal").ap()

        loaded = [sem(f"loaded{s}") for s in range(RAW)]
        hi_done = sem("hi_done")
        split = sem("split")
        used = sem("used")
        emptied = sem("emptied")

        x_in = sem("x_in")
        const_in = sem("const_in")
        vec_in = sem("vec_in")
        vec_turned = sem("vec_turned")
        vec_ready = sem("vec_ready")
        lam_sums = sem("lam_sums")
        lam_exps = sem("lam_exps")
        gw_hi = sem("gw_hi")
        gw_split = sem("gw_split")
        gate_psum = sem("gate_psum")
        gate_sum = sem("gate_sum")
        gate_ready = sem("gate_ready")
        table_psum = sem("table_psum")
        table_sb = sem("table_sb")
        table_out = sem("table_out")
        hank_in = [sem(f"hank_in{b}") for b in range(2)]
        flipped = [sem(f"flipped{b}") for b in range(2)]
        bias_ready = [sem(f"bias_ready{b}") for b in range(2)]
        NORM = ["sq", "var", "root", "rstd", "scaled_a", "scaled_d", "turned", "round", "done"]
        norm = {s: sem(f"norm_{s}") for s in NORM}
        x_reloaded = [sem(f"x_reloaded{n}") for n in range(4)]
        gain_in = [sem(f"gain_in{n}") for n in range(3)]
        spilled = [sem(f"spilled{n}") for n in range(3)]
        x_ready = [sem(f"x_ready{n}") for n in range(3)]
        y_ready = [sem(f"y_ready{n}") for n in range(4)]
        scores = sem("scores")
        logits = sem("logits")
        exps = sem("exps")
        probs = sem("probs")
        probs_turned = sem("probs_turned")
        probs_copied = sem("probs_copied")
        head_out = sem("head_out")
        head_hi = sem("head_hi")
        head_free = sem("head_free")
        dn = {s: sem(f"dn_{s}") for s in ("var", "root", "scaled", "turned", "round", "done")}
        w2_in = sem("w2_in")
        blk_sum = sem("blk_sum")
        blk_hi = sem("blk_hi")
        blk_split = sem("blk_split")
        hid_sum = sem("hid_sum")
        hid_ready = sem("hid_ready")
        cmp_psum = sem("cmp_psum")
        cmp_sb = sem("cmp_sb")
        cs_psum = sem("cs_psum")
        cs_logit = sem("cs_logit")
        cs_exp = sem("cs_exp")
        cs_prob = sem("cs_prob")
        cs_turned = sem("cs_turned")
        cs_ready = sem("cs_ready")
        nsa_done = sem("nsa_done")
        ff_u = sem("ff_u")
        ff_c = sem("ff_c")
        ff_conv = sem("ff_conv")
        ff_gelu = sem("ff_gelu")
        ff_h = sem("ff_h")
        ff_hi = sem("ff_hi")
        ff_done = sem("ff_done")
        sz = {s: sem(f"sb_{s}") for s in ("z", "zm", "ln", "sp", "aft", "e", "a", "out", "hi", "free")}
        pool_p = sem("pool_p")
        pool_hi = sem("pool_hi")
        pool_split = sem("pool_split")
        pooled = sem("pooled")
        pool_done = sem("pool_done")
        mg_logit = sem("mg_logit")
        mg_gate = sem("mg_gate")
        mg_m = sem("mg_m")
        mg_hi = sem("mg_hi")
        mg_done = sem("mg_done")
        stored = sem("stored")

        def chunks(name):
            return w[name][0].rearrange("(k p) n -> p k n", p=P)

        def halves(b):
            return ps[:, 2 * (b % 2):2 * (b % 2) + 2].rearrange("p h (a n) -> p h n a", a=2)

        ident = k1[:, IDENT:IDENT + P]

        def ident_rows(n):
            return k1[0:n, IDENT:IDENT + n]

        def v(name, j=0, n=1):
            return vec[:, VAT[name] + j:VAT[name] + j + n]

        def vdyn(name, j):
            return vec[:, bass.ds(VAT[name] + j, 1)] if not isinstance(j, int) else v(name, j)

        def ds(a, n=1):
            return slice(a, a + n) if isinstance(a, int) else bass.ds(a, n)

        def flat(t):
            return t.rearrange("p a n -> p (a n)")

        NORMS = {0: (x0, xn0, "pre_mix_norm"), 2: (X1, xn1, "pre_ffn_norm"), 4: (X2, xn2, "norm_mix_2"), 5: (X3, xn3, "norm_ffn_2")}

        TURN = {0: 0, 2: 1, 4: 2, 5: 3}

        block = ctx.enter_context(nc.Block())

        @block.sync
        def _(sp):
            def load(ph, i, c, src):
                sp.wait_ge(split, RAW + ph.before(i, c, RAW))
                sp.dma_start(raw[:, ph.slot_of(c)], src).then_inc(loaded[ph.slot_of(c)], 16)

            def stream(ph, src):
                if ph.iters == 1:
                    for c in range(ph.n):
                        load(ph, 0, c, src(0, *ph.where(c)))
                else:
                    with sp.Fori(0, ph.iters) as i:
                        for c in range(ph.n):
                            load(ph, i, c, src(i, *ph.where(c)))

            def cols(name, block_of, k0=0):
                wv = chunks(name)
                return lambda i, b, k: wv[:, k0 + KC * k:k0 + KC * (k + 1), ds(NB * block_of(i, b), NB)]

            sp.dma_start(x0, w["x"][0].rearrange("(a p) d -> p a d", p=P)).then_inc(x_in, 16)
            stream(diff_qk, cols("w_in", lambda i, b: 2 * i + b))
            stream(diff_v, cols("w_in", lambda i, b: 8 + 2 * i + b))
            stream(nsa_q, cols("w_in", lambda i, b: 12 + 2 * i + b))
            stream(nsa_k, cols("w_in", lambda i, b: 18 + 2 * b))
            stream(nsa_v, cols("w_in", lambda i, b: 19 + 2 * b))
            squeezers = [chunks("cmp_k_w1"), chunks("cmp_v_w1")]
            stream(squeeze, lambda i, b, k: squeezers[b][:, KC * k:KC * (k + 1), :])
            stream(out_a, cols("w_out", lambda i, b: 4 * i + b))
            stream(out_b, cols("w_out", lambda i, b: 4 * i + b, 8))
            stream(up1, cols("w_up", lambda i, b: i + FB * b))
            stream(down1, cols("w_down", lambda i, b: 2 * i + b))
            stream(sb_qk, cols("w_in_2", lambda i, b: 16 + 2 * i + b))
            stream(sb_v, cols("w_in_2", lambda i, b: 24 + 2 * i + b))
            stream(moba_qk, cols("w_in_2", lambda i, b: 2 * i + b))
            stream(moba_v, cols("w_in_2", lambda i, b: 8 + 2 * i + b))
            stream(pool_u, cols("w_in_2", lambda i, b: 12 + 2 * i + b))
            wp = w["w_pool_2"][0].rearrange("(c g) (k p) n -> c p (g k) n", p=P, g=2)
            stream(pool_w, lambda i, b, k: wp[b])
            gate = chunks("w_in_2")
            branch = [chunks(n) for n in ("w_br_a_2", "w_br_b_2", "w_br_c_2")]

            def merge_src(i, b, k):
                if b % 2 == 0:
                    return gate[:, KC * k:KC * (k + 1), ds(NB * (28 + 8 * (b // 2) + i), NB)]
                return branch[b // 2][:, KC * k:KC * (k + 1), ds(NB * i, NB)]

            stream(merge, merge_src)
            stream(out_2, cols("w_out_2", lambda i, b: 2 * i + b))
            gu = [chunks("w_gate_2"), chunks("w_up_2")]
            stream(up2, lambda i, b, k: gu[b][:, KC * k:KC * (k + 1), ds(NB * i, NB)])
            stream(down2, cols("w_down_2", lambda i, b: 2 * i + b))

        @block.gpsimd
        def _(pool):
            def rows_of(name, dst, src):
                pool.dma_start(dst, src).then_inc(vec_in, 16)

            pool.dma_start(k1, w["consts"][:, 0:CNEG]).then_inc(const_in, 16)
            r = 0
            for name, n in VECS[:6]:
                rows_of(name, rows[r:r + n, 0, :], w[name][0].rearrange("(r p) -> r p", p=P))
                r += n
            rows_of("conv_b", rows[0:88, 1, :], w["conv_b"][0].rearrange("(r p) -> r p", p=P))
            for j in range(3):
                rows_of("conv_w", rows[0:88, 2 + j, :], w["conv_w"][0, j].rearrange("(r p) -> r p", p=P))
            rows_of("pos", rows[0:32, 5, :], w["cmp_pos_k"][0])
            rows_of("pos", rows[32:64, 5, :], w["cmp_pos_v"][0])
            pool.dma_start(gw, chunks("w_in")[:, :, 5632:5656]).then_inc(const_in, 16)
            pool.dma_start(k2, w["consts"][:, CNEG:]).then_inc(const_in, 16)
            pool.dma_start(tab1[0:32, :], w["rel_bias"]).then_inc(const_in, 16)
            pool.dma_start(tab2[0:32, :], w["rel_bias_2"].rearrange("h b -> b h"), allow_slow_non_contiguous=True).then_inc(const_in, 16)
            for j, name in enumerate(("lambda_q1", "lambda_k1", "lambda_q2", "lambda_k2")):
                pool.dma_start(lamv[:, j, :], w[name].to_broadcast([P, 64])).then_inc(const_in, 16)

            pool.wait_ge(table_sb, 1)
            pool.dma_start(table[0:16], rbias[0:16, 0, :]).then_inc(table_out, 16)
            pool.dma_start(table[16:24], rbias[0:8, 1, :]).then_inc(table_out, 16)
            pool.wait_ge(table_out, 32)
            window = lambda h0, n: bass.AP(table.tensor, h0 * 384, [[1, P], [384, n], [1, T]])
            pool.dma_start(hank1, window(0, 16)).then_inc(hank_in[0], 16)

            pool.wait_ge(used, SPL + nsa_v.units(0, nsa_v.n - 1))
            for j, name in enumerate(("cmp_k_w2", "cmp_v_w2")):
                pool.dma_start(w2[:, j], w[name][0].rearrange("(k p) n -> p k n", p=P)).then_inc(w2_in, 16)
            cm = w["consts"][:, CNEG:CNEG + 4 * NC].rearrange("p (a c) -> p a c", c=NC)
            pool.dma_start(cmk, cm).then_inc(w2_in, 16)

            pool.wait_ge(nsa_done, 1)
            pool.dma_start(X1, w["x"][0].rearrange("(a p) d -> p a d", p=P)).then_inc(x_reloaded[0], 16)
            pool.dma_start(gain1, w["post_mix_norm"].to_broadcast([P, D])).then_inc(gain_in[0], 16)

            def keep(n, x):
                pool.wait_ge(x_ready[n], 1)
                pool.dma_start(spill[n].rearrange("(a p) d -> p a d", p=P), x).then_inc(spilled[n], 16)

            def reload(n, x, r):
                pool.dma_start(x, spill[n].rearrange("(a p) d -> p a d", p=P)).then_inc(x_reloaded[r], 16)

            keep(0, X1)
            pool.wait_ge(used, SPL + up1.units(FB - 1, up1.n - 1))
            pool.wait_ge(spilled[0], 16)
            reload(0, Xd, 1)
            pool.dma_start(gain2, w["post_ffn_norm"].to_broadcast([P, D])).then_inc(gain_in[1], 16)
            keep(1, X2)
            pool.wait_ge(y_ready[1], 1)
            pool.dma_start(hank2, window(16, 8)).then_inc(hank_in[1], 16)
            pool.wait_ge(used, SPL + merge.units(7, merge.n - 1))
            pool.wait_ge(spilled[1], 16)
            reload(1, X3, 2)
            keep(2, X3)
            pool.wait_ge(used, SPL + up2.units(FB - 1, up2.n - 1))
            pool.wait_ge(spilled[2], 16)
            reload(2, Xd, 3)
            pool.dma_start(gain2, w["norm_final_2"].rearrange("(a d) -> a d", a=1).to_broadcast([P, D])).then_inc(gain_in[2], 16)
            oview = out[0].rearrange("(a p) d -> a p d", p=P)
            for a in range(2):
                pool.wait_ge(y_ready[3], a + 1)
                pool.dma_start(oview[a], fin[:, a]).then_inc(stored, 16)
            pool.wait_ge(stored, 32)

        @block.tensor
        def _(pe):
            def unit(ph, i, c, kinds, acts):
                b, k = ph.where(c)
                pe.wait_ge(split, RAW + ph.units(i, c))
                if k == 0:
                    pe.wait_ge(emptied, ph.blocks_(i, b))
                s = ph.slot_of(c) % SPL
                last_k = ph.blocks[b] * KC - 1
                for kk in range(KC):
                    act = acts(b, KC * k + kk)
                    wt = spl[:, s, kk]
                    n = act.shape[-1]
                    for h in range(2):
                        o = ps[:, 2 * (b % 2) + h]
                        first, last = KC * k + kk == 0, KC * k + kk == last_k
                        part = slice(h * P, (h + 1) * P)

                        def whole():
                            if kinds[b] == COLS:
                                return nc.tensor.matmul(o[:, 0:2 * n], wt[:, 0, part], flat(act), start=first, stop=last)
                            return nc.tensor.matmul(o, act[:, 0, part], flat(wt), start=first, stop=last)

                        def cross():
                            if kinds[b] == COLS:
                                return nc.tensor.matmul(o[:, n:2 * n], wt[:, 1, part], act[:, 0], start=False, stop=False)
                            return nc.tensor.matmul(o[:, NB:], act[:, 1, part], wt[:, 0], start=False, stop=False)

                        if first:
                            whole()
                            m = cross()
                        else:
                            cross()
                            m = whole()
                m.then_inc(used, 1)

            def stream(ph, kinds, acts, before=None, heads=False):
                if ph.iters == 1 or heads:
                    for i in range(ph.iters):
                        for c in range(ph.n):
                            if before:
                                before(i, c)
                            unit(ph, i, c, kinds, acts)
                else:
                    with pe.Fori(0, ph.iters) as i:
                        for c in range(ph.n):
                            if before:
                                before(i, c)
                            unit(ph, i, c, kinds, acts)

            def turn_norm(n):
                src = NORMS[n][1]
                s, nth = norm, TURN[n]
                pe.wait_ge(s["scaled_a"], nth + 1)
                pe.wait_ge(s["scaled_d"], nth + 1)
                for q in range(8):
                    if q >= 4:
                        pe.wait_ge(s["done"], 8 * nth + q - 3)
                    for c in range(2):
                        for a in range(2):
                            at_ = (c * 2 + a) * P
                            m = nc.tensor.transpose(ps[:, 4 + q % 4, at_:at_ + P], src[:, a, (2 * q + c) * P:(2 * q + c + 1) * P], ident)
                    m.then_inc(s["turned"], 1)
                pe.wait_ge(s["done"], 8 * nth + 8)

            def head_scores(h, q, k, g, bank, rows_=None):
                S = ps[:, bank]
                nc.tensor.matmul(S[:, 0:P], q[:, 0:P], k[:, 0:P], start=True, stop=True)
                return nc.tensor.matmul(S[:, P:3 * P], q[:, P:T], k, start=True, stop=True)

            def turn(src, bank):
                for j in range(3):
                    m = nc.tensor.transpose(ps[:, bank, j * P:(j + 1) * P], src[:, j * P:(j + 1) * P], ident)
                return m

            def free_bank(h):
                pe.wait_ge(head_free, h + 1)

            def diff_scores(i, j):
                h = 2 * i + j
                free_bank(h)
                for m in range(2):
                    r = slice(64 * m, 64 * m + 64)
                    q = QK[r, ds(h)].rearrange("p a t -> p (a t)")
                    k = QK[r, ds(h + 8)].rearrange("p a t -> p (a t)")
                    last = head_scores(h, q, k, 0, 4 + 2 * j + m)
                last.then_inc(scores, 1)

            def diff_turn(i, j):
                h = 2 * i + j
                pe.wait_ge(probs, h + 1)
                turn(LG[:, j, 0], 4 + 2 * j).then_inc(probs_turned, 1)

            def diff_out(i, j):
                h = 2 * i + j
                pe.wait_ge(probs_copied, h + 1)
                pe.wait_ge(emptied, 2 + diff_v.blocks_(1, 1))
                O = ps[:, 5 + 2 * j]
                vh = [DV[:, a, ds(P * h, P)] for a in range(2)]
                pt = PT[:, j, 0]
                nc.tensor.matmul(O[:, 0:P], pt[:, 0:P], vh[0], start=True, stop=True)
                nc.tensor.matmul(O[:, P:T], pt[:, P:T], vh[0], start=True, stop=False)
                nc.tensor.matmul(O[:, P:T], pt[:, T:3 * P], vh[1], start=False, stop=True).then_inc(head_out, 1)

            def diff_before(i, c):
                for j in range(2):
                    if c == 0:
                        diff_scores(i, j)
                    if c == 3 + j:
                        diff_turn(i, j)
                    if c == 5 + j:
                        diff_out(i, j)

            def diff_finish(c):
                if c == 3:
                    pe.wait_ge(dn["scaled"], 1)
                    for q in range(4):
                        for c_ in range(2):
                            for a in range(2):
                                at_ = (c_ * 2 + a) * P
                                m = nc.tensor.transpose(ps[:, 4 + q, at_:at_ + P], OD[:, a, 2 * q + c_], ident)
                        m.then_inc(dn["turned"], 1)

            def nsa_before(g, c):
                pair, c = c // 4, c % 4
                for j in range(2):
                    hg = 2 * pair + j
                    nh = 4 * g + hg
                    if c == 0:
                        free_bank(HEADS + nh)
                        q = NQ[:, ds(nh)].rearrange("p a t -> p (a t)")
                        for m in range(2):
                            k = NKs[:, ds(2 * m + g)].rearrange("p a t -> p (a t)")
                            last = head_scores(nh, q, k, 0, 4 + 2 * j + m)
                        last.then_inc(scores, 1)
                    if c == 2:
                        pe.wait_ge(probs, HEADS + nh + 1)
                        turn(LG[:, j, 0], 4 + 2 * j)
                        turn(LG[:, j, 1], 5 + 2 * j).then_inc(probs_turned, 1)
                    if c == 3:
                        pe.wait_ge(probs_copied, HEADS + nh + 1)
                        O = ps[:, 4 + 2 * j, 0:T]
                        for m in range(2):
                            for a in range(2):
                                vh = NVs[:, a, m, ds(P * g, P)]
                                o, pt = (O, PT[:, j, m, 0:T]) if a == 0 else (O[:, P:T], PT[:, j, m, T:3 * P])
                                nc.tensor.matmul(o, vh, pt, start=(m == 0 and a == 0), stop=False)
                        r = slice(32 * hg, 32 * hg + NC)
                        nc.tensor.matmul(O, vcr[r, ds(g)].rearrange("p a e -> p (a e)"), PcT[r, ds(g)].rearrange("p a t -> p (a t)"),
                                         start=False, stop=True).then_inc(head_out, 1)

            def sb_before(i, c):
                for j in range(2):
                    h = 2 * i + j
                    X, Yb = ps[:, 4 + 2 * j], ps[:, 5 + 2 * j]
                    if c == 0:
                        pe.wait_ge(sz["free"], h + 1)
                        q = SQK[:, ds(h)].rearrange("p a t -> p (a t)")
                        k = SQK[:, ds(h + 8)].rearrange("p a t -> p (a t)")
                        nc.tensor.matmul(X[:, 0:T], k[:, 0:P], q, start=True, stop=True)
                        nc.tensor.matmul(X[:, T:3 * P], k[:, P:T], q[:, P:T], start=True, stop=True).then_inc(sz["z"], 1)
                    if c == 3 + j:
                        pe.wait_ge(sz["sp"], h + 1)
                        sp_ = SZ[:, j, 2]
                        low, one = k1[:, LOWER:LOWER + P], k1[:, ONES:ONES + P]
                        nc.tensor.matmul(Yb[:, 0:T], low, sp_[:, 0:T], start=True, stop=False)
                        nc.tensor.matmul(Yb[:, P:T], one, sp_[:, T:3 * P], start=False, stop=True)
                        nc.tensor.matmul(Yb[:, T:3 * P], low, sp_[:, T:3 * P], start=True, stop=True).then_inc(sz["aft"], 1)
                    if c == 5 + j:
                        pe.wait_ge(sz["a"], h + 1)
                        pe.wait_ge(emptied, 2 + sb_v.blocks_(1, 1))
                        a_ = SZ[:, j, 3]
                        nc.tensor.matmul(X[:, 0:T], SV[:, 0, ds(P * h, P)], a_[:, 0:T], start=True, stop=False)
                        nc.tensor.matmul(X[:, P:T], SV[:, 1, ds(P * h, P)], a_[:, T:3 * P], start=False, stop=True).then_inc(sz["out"], 1)

            def moba_before(i, c):
                pair, c = c // 4, c % 4
                for j in range(2):
                    h = 4 * i + 2 * pair + j
                    n = 2 * HEADS + h
                    X, Yb = 4 + 2 * j, 5 + 2 * j
                    if c == 0:
                        free_bank(n)
                        q = MQK[:, ds(h)].rearrange("p a t -> p (a t)")
                        k = MQK[:, ds(h + 8)].rearrange("p a t -> p (a t)")
                        head_scores(h, q, k, 0, X).then_inc(scores, 1)
                    if c == 2:
                        pe.wait_ge(probs, n + 1)
                        turn(LM[:, j], Yb).then_inc(probs_turned, 1)
                    if c == 3:
                        pe.wait_ge(probs_copied, n + 1)
                        pe.wait_ge(emptied, 2 + moba_v.blocks_(1, 1))
                        O = ps[:, X]
                        nc.tensor.matmul(O[:, 0:T], MV[:, 0, ds(P * h, P)], PM[:, j, 0:T], start=True, stop=False)
                        nc.tensor.matmul(O[:, P:T], MV[:, 1, ds(P * h, P)], PM[:, j, T:3 * P], start=False, stop=True).then_inc(head_out, 1)

            nc.tensor.sem_inc(used, SPL)
            nc.tensor.sem_inc(bias_ready[0], 4)

            pe.wait_ge(const_in, 16 * 9)
            pe.wait_ge(vec_in, 16 * 12)
            for j, members in enumerate(VEC_TILES):
                n = sum(VECS[m][1] for m in members)
                a = VAT[VECS[members[0]][0]]
                m = nc.tensor.transpose(ps[:, 0, a:a + n], rows[0:n, j], ident_rows(n))
            m.then_inc(vec_turned, 1)
            nc.tensor.matmul(ps[0:16, 2, 0:T], tab1[0:32], k2[0:32, HOT1 - CNEG:HOT1 - CNEG + T], start=True, stop=True)
            nc.tensor.matmul(ps[0:8, 3, 0:T], tab2[0:32], k2[0:32, HOT2 - CNEG:HOT2 - CNEG + T], start=True, stop=True).then_inc(table_psum, 1)
            turn_norm(0)
            pe.wait_ge(gw_split, 1)
            pe.wait_ge(vec_ready, 1)
            for a in range(2):
                o = ps[:, a]
                for k in range(NK):
                    x_hi, x_lo = HA[:, k, 0, a * P:(a + 1) * P], HA[:, k, 1, a * P:(a + 1) * P]
                    if k:
                        nc.tensor.matmul(o[:, 24:48], x_lo, gws[:, k, 0], start=False, stop=False)
                    m = nc.tensor.matmul(o[:, 0:48], x_hi, flat(gws[:, k]), start=k == 0, stop=k == NK - 1)
                    if k == 0:
                        m = nc.tensor.matmul(o[:, 24:48], x_lo, gws[:, k, 0], start=False, stop=False)
            m.then_inc(gate_psum, 1)
            pe.wait_ge(gate_sum, 1)
            pe.wait_ge(table_sb, 1)

            HAc = lambda b, k: HA[:, k]
            stream(diff_qk, [COLS, COLS], HAc)
            pe.wait_ge(hank_in[0], 16)

            def bias_before(i, c):
                if c == 0:
                    pe.wait_ge(bias_ready[0], 4 * i + 4)
                    for q in range(4):
                        nc.tensor.matmul(ps[:, 4 + q], k1[:, FLIP:FLIP + P], hank1[:, ds(8 * i + 2 * q, 2)].rearrange("p h t -> p (h t)"),
                                         start=True, stop=True).then_inc(flipped[0], 1)

            stream(diff_v, [TOKS, TOKS], HAc, bias_before)
            pe.wait_ge(bias_ready[0], 12)
            stream(nsa_q, [COLS, COLS], HAc, diff_before, heads=True)
            stream(nsa_k, [COLS, COLS], HAc, lambda i, c: diff_before(3, c))
            stream(nsa_v, [TOKS, TOKS], HAc, lambda i, c: diff_finish(c))
            pe.wait_ge(blk_split, 2)
            sq = [ksp, vsp]
            stream(squeeze, [COLS, COLS], lambda b, k: sq[b][:, k])
            pe.wait_ge(hid_ready, 2)
            pe.wait_ge(dn["done"], 4)
            pe.wait_ge(w2_in, 48)
            for k in range(2):
                nc.tensor.matmul(ps[:, 4, 0:2 * NC], w2[:, 0, k], hid[:, 0, k], start=k == 0, stop=k == 1)
            for j in range(4):
                for g in range(2):
                    for k in range(2):
                        m = nc.tensor.matmul(ps[32 * j:32 * j + NC, 5, g * P:(g + 1) * P], hid[:, 1, k, g * NC:(g + 1) * NC],
                                             w2[:, 1, k], start=k == 0, stop=k == 1)
            m.then_inc(cmp_psum, 1)
            pe.wait_ge(cmp_sb, 1)
            for a in range(2):
                for h in range(HEADS):
                    m = nc.tensor.matmul(ps[:, 6 + a, h * NC:(h + 1) * NC], NQ[:, h, a * P:(a + 1) * P],
                                         kcT[:, (h // 4) * NC:(h // 4 + 1) * NC], start=True, stop=True)
            m.then_inc(cs_psum, 1)
            pe.wait_ge(cs_prob, 1)
            for g in range(2):
                for a in range(2):
                    m = nc.tensor.transpose(ps[:, 4, (g * 2 + a) * P:(g * 2 + a + 1) * P],
                                            PC[:, a, 4 * g:4 * g + 4].rearrange("p h c -> p (h c)"), ident)
            m.then_inc(cs_turned, 1)
            pe.wait_ge(cs_ready, 1)
            MIXc = lambda b, k: MIX[:, k]
            stream(out_a, [TOKS] * 4, MIXc, nsa_before, heads=True)
            pe.wait_ge(head_free, 2 + 2 * HEADS)
            stream(out_b, [TOKS] * 4, lambda b, k: MIX[:, 8 + k])
            turn_norm(2)
            stream(up1, [COLS, COLS], HAc)
            pe.wait_ge(ff_done, FB)
            FFc = lambda b, k: FF[:, k]
            stream(down1, [TOKS, TOKS], FFc)
            turn_norm(4)
            stream(sb_qk, [COLS, COLS], HAc)
            pe.wait_ge(hank_in[1], 16)
            for q in range(4):
                nc.tensor.matmul(ps[:, 4 + q], k1[:, FLIP:FLIP + P], hank2[:, 2 * q:2 * q + 2].rearrange("p h t -> p (h t)"),
                                 start=True, stop=True).then_inc(flipped[1], 1)
            stream(sb_v, [TOKS, TOKS], HAc)
            pe.wait_ge(bias_ready[1], 4)
            stream(moba_qk, [COLS, COLS], HAc, sb_before, heads=True)
            stream(moba_v, [TOKS, TOKS], HAc)
            pe.wait_ge(sz["free"], 2 + HEADS)
            stream(pool_u, [COLS, COLS], HAc, moba_before, heads=True)
            pe.wait_ge(pool_split, 4)
            for c in range(2):
                pe.wait_ge(split, RAW + pool_w.units(0, c))
                s = pool_w.slot_of(c) % SPL
                for g in range(2):
                    b = 2 * c + g
                    pe.wait_ge(emptied, pool_w.blocks_(0, b))
                    for h in range(2):
                        o = ps[:, 2 * (b % 2) + h]
                        for k in range(2):
                            wt, act = spl[:, s, 2 * g + k], PS[:, 2 * b + k]
                            part = slice(h * P, (h + 1) * P)
                            if k:
                                nc.tensor.matmul(o[:, T:], wt[:, 1, part], act[:, 0], start=False, stop=False)
                            m = nc.tensor.matmul(o, wt[:, 0, part], flat(act), start=k == 0, stop=k == 1)
                            if not k:
                                nc.tensor.matmul(o[:, T:], wt[:, 1, part], act[:, 0], start=False, stop=False)
                    if g == 1:
                        m.then_inc(used, 1)
                    else:
                        m.then_inc(pool_p, 1)
            pe.wait_ge(pool_done, 4)
            pe.wait_ge(head_free, 2 + 3 * HEADS)
            ys = [YA, YB, YC]
            stream(merge, [COLS] * 6, lambda b, k: HA[:, k] if b % 2 == 0 else ys[b // 2][:, k])
            pe.wait_ge(mg_done, 8)
            stream(out_2, [TOKS, TOKS], lambda b, k: MM[:, k])
            turn_norm(5)
            stream(up2, [COLS, COLS], HAc)
            pe.wait_ge(ff_done, 2 * FB)
            stream(down2, [TOKS, TOKS], FFc)

        @block.scalar
        def _(act):
            def round_unit(ph, i, c):
                s = ph.slot_of(c)
                act.wait_ge(loaded[s], ph.loaded(i, c))
                act.wait_ge(used, SPL + ph.before(i, c, SPL))
                nc.scalar.activation(spl[:, s % SPL, :, 0], raw[:, s], ACT.Copy).then_inc(hi_done, 1)

            def stream(ph, after=None, carried=None):
                def body(i, first):
                    for c in range(ph.n):
                        round_unit(ph, i, c)
                        if first and carried:
                            carried(c)
                        if after:
                            after(i, c, first)
                body(0, True)
                if ph.iters > 1:
                    with act.Fori(1, ph.iters) as i:
                        body(i, False)

            def norm_act(n, src, dst, scaled=True):
                s = norm
                nc.scalar.activation(dst[:, 0], src[:, 0], ACT.Square, accum_out=st[:, 4 * n:4 * n + 1]).then_inc(s["sq"], 1)
                act.wait_ge(s["var"], n + 1)
                nc.scalar.activation(st[:, 4 * n + 2:4 * n + 4], st[:, 4 * n:4 * n + 2], ACT.Sqrt).then_inc(s["root"], 1)
                if not scaled:
                    return
                act.wait_ge(s["rstd"], n + 1)
                nc.scalar.activation(dst[:, 0], src[:, 0], ACT.Copy, scale=st[:, 4 * n:4 * n + 1]).then_inc(s["scaled_a"], 1)

            def turn_act(n):
                s, name = norm, NORMS[n][2]
                for q in range(8):
                    act.wait_ge(s["turned"], 8 * TURN[n] + q + 1)
                    for c in range(2):
                        m = nc.scalar.activation(HA[:, 2 * q + c, 0], ps[:, 4 + q % 4, c * T:(c + 1) * T], ACT.Copy, scale=v(name, 2 * q + c))
                    m.then_inc(s["round"], 1)

            def softmax_exp(n, j, buf, maps):
                act.wait_ge(logits, n + 1)
                for a in range(2):
                    sl = slice(0, P) if a == 0 else slice(P, 3 * P)
                    for m in range(maps):
                        at_ = 32 + 16 * j + 2 * a + m
                        e = nc.scalar.activation(buf[:, m, sl], buf[:, m, sl], ACT.Exp, bias=st[:, at_:at_ + 1], accum_out=st[:, at_ + 4:at_ + 5])
                e.then_inc(exps, 1)

            def copy_turned(n, j, dst, bank, maps):
                act.wait_ge(probs_turned, n + 1)
                for m in range(maps):
                    cp = nc.scalar.activation(dst[:, m], ps[:, bank + m, 0:3 * P], ACT.Copy)
                cp.then_inc(probs_copied, 1)

            def head_round(n, j, dst, bank, ready=None, done=None):
                act.wait_ge(ready or head_out, n + 1)
                nc.scalar.activation(dst, ps[:, bank, 0:T], ACT.Copy).then_inc(done or head_hi, 1)

            def diff_after(i, c):
                for j in range(2):
                    h = 2 * i + j
                    if c == 2:
                        softmax_exp(h, j, LG[:, j], 2)
                    if c == 5 + j:
                        copy_turned(h, j, PT[:, j], 4 + 2 * j, 1)
                    if c == 7:
                        act.wait_ge(head_out, h + 1)
                        for a in range(2):
                            at_ = 64 + a * 8 + h
                            nc.scalar.activation(PT[:, j, 1, a * P:(a + 1) * P], ps[:, 5 + 2 * j, a * P:(a + 1) * P], ACT.Square, accum_out=st[:, ds(at_)])
                        nc.scalar.activation(OD[:, :, ds(h)].rearrange("p a h e -> p (a h) e"), ps[:, 5 + 2 * j, 0:T].rearrange("p (a e) -> p a e", a=2), ACT.Copy).then_inc(head_free, 1)

            def nsa_after(g, c, first):
                pair, c = c // 4, c % 4
                for j in range(2):
                    h = 4 * g + 2 * pair + j
                    if c == 1:
                        softmax_exp(HEADS + h, j, LG[:, j], 2)
                    if c == 2:
                        copy_turned(HEADS + h, j, PT[:, j], 4 + 2 * j, 2)
                    if c == 3:
                        head_round(HEADS + h, j, MIX[:, ds(8 + h), 0].rearrange("p a t -> p (a t)"), 4 + 2 * j)

            def moba_after(i, c, first):
                pair, c = c // 4, c % 4
                for j in range(2):
                    h = 4 * i + 2 * pair + j
                    n = 2 * HEADS + h
                    if c == 1:
                        softmax_exp(n, j, LM[:, j:j + 1], 1)
                    if c == 2:
                        copy_turned(n, j, PM[:, j:j + 1], 5 + 2 * j, 1)
                    if c == 3:
                        head_round(n, j, YA[:, ds(h), 0].rearrange("p a t -> p (a t)"), 4 + 2 * j)

            def sb_after(i, c, first):
                for j in range(2):
                    h = 2 * i + j
                    z, e, sp_, a_ = (SZ[:, j, k] for k in range(4))
                    if c == 2:
                        act.wait_ge(sz["zm"], h + 1)
                        nc.scalar.activation(e, z, ACT.Abs)
                        act.drain()
                        nc.scalar.activation(e, e, ACT.Exp, scale=-1.0)
                        act.drain()
                        nc.scalar.activation(e, e, ACT.Ln, bias=1.0).then_inc(sz["ln"], 1)
                    if c == 4 + j:
                        act.wait_ge(sz["e"], h + 1)
                        nc.scalar.activation(a_, a_, ACT.Exp).then_inc(sz["a"], 1)
                    if c == 7:
                        head_round(h, j, YC[:, ds(h), 0].rearrange("p a t -> p (a t)"), 4 + 2 * j, sz["out"], sz["hi"])

            def ff1_empty(i, b):
                n = 2 * i + b
                act.wait_ge(ff_u, n + 1)
                for t in range(2):
                    j = 2 * i + 44 * b + t
                    m = nc.scalar.activation(CV[:, t], U[:, t], ACT.Identity, bias=vdyn("conv_b", j), scale=vdyn("conv_w2", j))
                m.then_inc(ff_c, 1)
                if b == 0:
                    act.wait_ge(ff_conv, i + 1)
                    nc.scalar.activation(GL, CV, ACT.Gelu_apprx_tanh).then_inc(ff_gelu, 1)
                else:
                    act.wait_ge(ff_h, i + 1)
                    nc.scalar.activation(FF[:, ds(2 * i, 2), 0], HF, ACT.Copy).then_inc(ff_hi, 1)

            def ff2_empty(i, b):
                if b == 0:
                    act.wait_ge(ff_u, 2 * FB + i + 1)
                    nc.scalar.activation(GL, U, ACT.Silu).then_inc(ff_gelu, 1)
                else:
                    act.wait_ge(ff_h, FB + i + 1)
                    nc.scalar.activation(FF[:, ds(2 * i, 2), 0], HF, ACT.Copy).then_inc(ff_hi, 1)

            def emptier(ph, empty):
                def after(i, c, first):
                    for e, b, late in ph.ends():
                        if c == e and not late:
                            empty(i, b)
                        if c == e and late and not first:
                            empty(i - 1, b)
                return after

            def late(ph, empty):
                def carried(c):
                    for e, b, is_late in ph.ends():
                        if is_late and c == e:
                            empty(ph.iters - 1, b)
                return carried

            def merge_empty(i, b):
                if b % 2 == 0:
                    act.wait_ge(mg_logit, 3 * i + b // 2 + 1)
                    nc.scalar.activation(GS, GT, ACT.Sigmoid).then_inc(mg_gate, 1)
                if b == 5:
                    act.wait_ge(mg_m, i + 1)
                    nc.scalar.activation(MM[:, ds(2 * i, 2), 0], MA, ACT.Copy).then_inc(mg_hi, 1)


            act.wait_ge(x_in, 16)
            norm_act(0, x0, xn0)
            act.wait_ge(lam_sums, 1)
            nc.scalar.activation(lsum[:, 2:4], lsum[:, 0:2], ACT.Exp).then_inc(lam_exps, 1)
            act.wait_ge(const_in, 16 * 9)
            nc.scalar.activation(gws[:, :, 0], gw, ACT.Copy).then_inc(gw_hi, 1)
            act.wait_ge(vec_ready, 1)
            turn_act(0)
            act.wait_ge(gate_sum, 1)
            nc.scalar.activation(gates, gates, ACT.Sigmoid).then_inc(gate_ready, 1)

            def bias_after(i, c, first):
                if c == 3:
                    for q in range(4):
                        act.wait_ge(flipped[0], 4 * i + q + 1)
                        nc.scalar.activation(bias1[:, ds(8 * i + 2 * q, 2)].rearrange("p h t -> p (h t)"), ps[:, 4 + q],
                                             ACT.Copy).then_inc(bias_ready[0], 1)

            stream(diff_qk)
            stream(diff_v, bias_after)
            stream(nsa_q, lambda i, c, first: diff_after(i, c))
            stream(nsa_k, lambda i, c, first: diff_after(3, c))

            def finish_diff(i, c, first):
                if c == 1:
                    act.wait_ge(dn["var"], 1)
                    nc.scalar.activation(st[:, 80:96], st[:, 64:80], ACT.Sqrt).then_inc(dn["root"], 1)
                if c == 4:
                    for b, (src, dst) in enumerate(((kblk, ksp), (vblk, vsp))):
                        act.wait_ge(blk_sum, b + 1)
                        nc.scalar.activation(dst[:, :, 0], src, ACT.Copy).then_inc(blk_hi, 1)
                if c == 6:
                    for q in range(4):
                        act.wait_ge(dn["turned"], q + 1)
                        nc.scalar.activation(MIX[:, 2 * q:2 * q + 2, 0], ps[:, 4 + q].rearrange("p (c t) -> p c t", c=2), ACT.Copy,
                                             scale=st[:, 96:97]).then_inc(dn["round"], 1)

            stream(nsa_v, finish_diff)
            def squeeze_empty(b):
                act.wait_ge(hid_sum, b + 1)
                nc.scalar.activation(hid[:, b], hid[:, b], ACT.Gelu_apprx_tanh).then_inc(hid_ready, 1)

            stream(squeeze, lambda i, c, first: squeeze_empty(0) if c == 11 else None)
            squeeze_empty(1)
            act.wait_ge(cmp_psum, 1)
            nc.scalar.activation(kcT, ps[:, 4, 0:2 * NC], ACT.Copy)
            for j in range(4):
                r = slice(32 * j, 32 * j + NC)
                m = nc.scalar.activation(vcr[r].rearrange("p g e -> p (g e)"), ps[r, 5, 0:T], ACT.Copy)
            m.then_inc(cmp_sb, 1)
            act.wait_ge(cs_logit, 1)
            nc.scalar.activation(cl, cl, ACT.Exp).then_inc(cs_exp, 1)
            act.wait_ge(cs_turned, 1)
            nc.scalar.activation(PcT.rearrange("p g t -> p (g t)"), ps[:, 4], ACT.Copy).then_inc(cs_ready, 1)
            stream(out_a, nsa_after)
            stream(out_b)
            act.wait_ge(y_ready[0], 1)
            norm_act(1, Y1, xn1, scaled=False)
            act.wait_ge(x_ready[0], 1)
            norm_act(2, X1, xn1)
            turn_act(2)
            act.wait_ge(spilled[0], 16)
            stream(up1, emptier(up1, ff1_empty))
            stream(down1, None, late(up1, ff1_empty))
            act.wait_ge(y_ready[1], 1)
            norm_act(3, Yd, xn2, scaled=False)
            act.wait_ge(x_ready[1], 1)
            norm_act(4, X2, xn2)
            turn_act(4)

            def bias2_after(c):
                if c == 5:
                    for q in range(4):
                        act.wait_ge(flipped[1], q + 1)
                        nc.scalar.activation(bias2[:, 2 * q:2 * q + 2].rearrange("p h t -> p (h t)"), ps[:, 4 + q], ACT.Copy).then_inc(bias_ready[1], 1)

            stream(sb_qk)
            stream(sb_v, None, bias2_after)
            stream(moba_qk, sb_after)
            stream(moba_v)
            act.wait_ge(spilled[1], 16)
            stream(pool_u, moba_after)
            for g in range(4):
                act.wait_ge(pooled, g + 1)
                nc.scalar.activation(PS[:, 2 * g:2 * g + 2, 0], (PX, PW)[g % 2], ACT.Copy).then_inc(pool_hi, 1)
            stream(pool_w)
            for g in range(4):
                act.wait_ge(pooled, 4 + g + 1)
                nc.scalar.activation(YB[:, 2 * g:2 * g + 2, 0], (PX, PW)[g % 2], ACT.Copy).then_inc(pool_hi, 1)
            stream(merge, emptier(merge, merge_empty))
            for e, b, is_late in merge.ends():
                if is_late:
                    merge_empty(7, b)
            stream(out_2)
            act.wait_ge(x_ready[2], 1)
            norm_act(5, X3, xn3)
            turn_act(5)
            act.wait_ge(spilled[2], 16)
            stream(up2, emptier(up2, ff2_empty))
            stream(down2, None, late(up2, ff2_empty))
            act.wait_ge(y_ready[2], 1)
            norm_act(6, Xd, fin, scaled=False)

        @block.vector
        def _(dve):
            def split_unit(ph, i, c):
                s = ph.slot_of(c)
                dve.wait_ge(hi_done, ph.units(i, c))
                nc.vector.tensor_tensor(spl[:, s % SPL, :, 1], raw[:, s], spl[:, s % SPL, :, 0].bitcast(F32),
                                        ALU.subtract).then_inc(split, 1)

            def empty(ph, i, b, dst, n=NB):
                dve.wait_ge(used, SPL + ph.units(i, sum(ph.blocks[:b + 1]) - 1))
                src = ps[:, 2 * (b % 2):2 * (b % 2) + 2, 0:2 * n].rearrange("p h (a n) -> p h n a", a=2)
                nc.vector.tensor_reduce(dst, src, AX.X, ALU.add).then_inc(emptied, 1)

            def stream(ph, emptyb=None, after=None, carried=None):
                def body(i, first):
                    for c in range(ph.n):
                        split_unit(ph, i, c)
                        if first and carried:
                            carried(c)
                        for e, b, is_late in ph.ends():
                            if emptyb and c == e and not is_late:
                                emptyb(i, b)
                            if emptyb and c == e and is_late and not first:
                                emptyb(i - 1, b)
                        if after:
                            after(i, c)
                body(0, True)
                if ph.iters > 1:
                    with dve.Fori(1, ph.iters) as i:
                        body(i, False)

            def late(ph, emptyb):
                def carried(c):
                    for e, b, is_late in ph.ends():
                        if is_late and c == e:
                            emptyb(ph.iters - 1, b)
                return carried

            def finish(ph, emptyb):
                for e, b, is_late in ph.ends():
                    if is_late:
                        emptyb(ph.iters - 1, b)

            def tiles(ph, dst):
                return lambda i, b: empty(ph, i, b, dst[:, ds(ph.nb * 2 * i + 2 * b, 2)])

            def columns(ph, dst):
                return lambda i, b: empty(ph, i, b, dst[:, :, ds(NB * (ph.nb * i + b), NB)])

            def norm_dve(n, src, dst):
                s, q = norm, 4 * n
                nc.vector.tensor_tensor_reduce(out=dst[:, 1], in0=src[:, 1], in1=src[:, 1], scale=1.0, scalar=0.0,
                                               op0=ALU.mult, op1=ALU.add, accum_out=st[:, q + 1:q + 2])
                dve.wait_ge(s["sq"], n + 1)
                dve.drain()
                nc.vector.tensor_scalar(st[:, q:q + 2], st[:, q:q + 2], 1.0 / D, EPS, ALU.mult, ALU.add).then_inc(s["var"], 1)
                dve.wait_ge(s["root"], n + 1)
                nc.vector.reciprocal(st[:, q:q + 2], st[:, q + 2:q + 4]).then_inc(s["rstd"], 1)
                dve.drain()

            def scale_dve(n, src, dst):
                nc.vector.tensor_scalar(dst[:, 1], src[:, 1], st[:, 4 * n + 1:4 * n + 2], None, ALU.mult).then_inc(norm["scaled_d"], 1)

            def turn_dve(n):
                s, name = norm, NORMS[n][2]
                for q in range(8):
                    dve.wait_ge(s["round"], 8 * TURN[n] + q + 1)
                    for c in range(2):
                        k = 2 * q + c
                        m = nc.vector.scalar_tensor_tensor(HA[:, k, 1], ps[:, 4 + q % 4, c * T:(c + 1) * T], v(name, k),
                                                           HA[:, k, 0].bitcast(F32), ALU.mult, ALU.subtract)
                    m.then_inc(s["done"], 1)

            def add_normed(n, y, x, gain, tmp, dst):
                for a in range(2):
                    nc.vector.scalar_tensor_tensor(tmp[:, a], y[:, a], st[:, 4 * n + a:4 * n + a + 1], gain, ALU.mult, ALU.mult)
                dve.drain()
                return nc.vector.tensor_tensor(dst, tmp, x, ALU.add)

            TILE = [slice(0, P), slice(P, 3 * P)]

            def softmax_logits(n, j, bank, maps, buf, scale, bias, h):
                dve.wait_ge(scores, n + 1)
                for a in range(2):
                    w_ = P * (a + 1)
                    bt = bias[:, ds(h), T - w_:T].to_broadcast([P, maps, w_]) if maps > 1 else bias[:, ds(h), T - w_:T]
                    nc.vector.scalar_tensor_tensor(buf[:, 0:maps, TILE[a]], ps[:, bank:bank + maps, TILE[a]], scale, bt, ALU.mult, ALU.add)
                dve.drain()
                for a in range(2):
                    at_ = 32 + 16 * j + 2 * a
                    m = nc.vector.tensor_reduce(st[:, at_:at_ + maps], buf[:, 0:maps, TILE[a]], AX.X, ALU.max, negate=True)
                m.then_inc(logits, 1)

            def softmax_sums(n, j, maps, guard=True):
                dve.wait_ge(exps, n + 1)
                sv = st[:, 36 + 16 * j:40 + 16 * j].rearrange("p (a m) -> p a m", m=2)[:, :, 0:maps]
                r = st[:, 40 + 16 * j:44 + 16 * j].rearrange("p (a m) -> p a m", m=2)[:, :, 0:maps]
                if guard:
                    nc.vector.tensor_scalar(sv, sv, TINY, None, ALU.max)
                    dve.drain()
                nc.vector.reciprocal(r, sv)
                dve.drain()
                return r

            def scale_probs(buf, r, maps):
                for a in range(2):
                    for m in range(maps):
                        t = nc.vector.tensor_scalar(buf[:, m, TILE[a]], buf[:, m, TILE[a]], r[:, a, m:m + 1], None, ALU.mult)
                return t

            def diff_after(i, c):
                if c != 2:
                    return
                for j in range(2):
                    softmax_logits(2 * i + j, j, 4 + 2 * j, 2, LG[:, j], 64 ** -0.5, bias1, 2 * i + j)
                for j in range(2):
                    r = softmax_sums(2 * i + j, j, 2)
                    nc.vector.tensor_scalar(r[:, :, 1], r[:, :, 1], neg_lam, None, ALU.mult)
                    dve.drain()
                    for a in range(2):
                        nc.vector.tensor_scalar(LG[:, j, 1, TILE[a]], LG[:, j, 1, TILE[a]], r[:, a, 1:2], None, ALU.mult)
                    dve.drain()
                    for a in range(2):
                        m = nc.vector.scalar_tensor_tensor(LG[:, j, 0, TILE[a]], LG[:, j, 0, TILE[a]], r[:, a, 0:1], LG[:, j, 1, TILE[a]],
                                                           ALU.mult, ALU.add)
                    m.then_inc(probs, 1)

            def head_split(n, j, dst):
                dve.wait_ge(head_hi, n - HEADS + 1)
                nc.vector.tensor_tensor(dst[1], ps[:, 4 + 2 * j, 0:T], dst[0].bitcast(F32), ALU.subtract).then_inc(head_free, 1)

            def parts(t, h):
                return [t[:, ds(h), k].rearrange("p a t -> p (a t)") for k in range(2)]

            def nsa_after(g, c):
                pair, c = c // 4, c % 4
                hs = [4 * g + 2 * pair + j for j in range(2)]
                if c == 1:
                    for j, h in enumerate(hs):
                        softmax_logits(HEADS + h, j, 4 + 2 * j, 2, LG[:, j], 128 ** -0.5, bias1, 8 + h)
                    for j, h in enumerate(hs):
                        r = softmax_sums(HEADS + h, j, 2)
                        nc.vector.tensor_tensor(r, r, gates[:, :, ds(3 * h + 1, 2)], ALU.mult)
                        dve.drain()
                        scale_probs(LG[:, j], r, 2).then_inc(probs, 1)
                if c == 3:
                    for j, h in enumerate(hs):
                        head_split(HEADS + h, j, parts(MIX, 8 + h))

            def moba_after(i, c):
                pair, c = c // 4, c % 4
                hs = [4 * i + 2 * pair + j for j in range(2)]
                if c == 1:
                    for j, h in enumerate(hs):
                        softmax_logits(2 * HEADS + h, j, 4 + 2 * j, 1, LM[:, j:j + 1], 128 ** -0.5, bias2, h)
                    for j, h in enumerate(hs):
                        r = softmax_sums(2 * HEADS + h, j, 1, guard=False)
                        scale_probs(LM[:, j:j + 1], r, 1).then_inc(probs, 1)
                if c == 3:
                    for j, h in enumerate(hs):
                        head_split(2 * HEADS + h, j, parts(YA, h))

            def sb_after(i, c):
                for j in range(2):
                    h = 2 * i + j
                    if c == 2:
                        dve.wait_ge(sz["z"], h + 1)
                        nc.vector.scalar_tensor_tensor(SZ[:, j, 0], ps[:, 4 + 2 * j, 0:3 * P], 128 ** -0.5, k1[:, SBMASK:SBMASK + 3 * P],
                                                       ALU.mult, ALU.add).then_inc(sz["zm"], 1)
                for j in range(2):
                    h = 2 * i + j
                    if c == 2:
                        dve.wait_ge(sz["ln"], h + 1)
                        nc.vector.scalar_tensor_tensor(SZ[:, j, 2], SZ[:, j, 0], 0.0, SZ[:, j, 1], ALU.max, ALU.add).then_inc(sz["sp"], 1)
                    if c == 4 + j:
                        dve.wait_ge(sz["aft"], h + 1)
                        nc.vector.tensor_tensor(SZ[:, j, 3], SZ[:, j, 0], ps[:, 5 + 2 * j, 0:3 * P], ALU.add).then_inc(sz["e"], 1)
                    if c == 7:
                        dve.wait_ge(sz["hi"], h + 1)
                        d = parts(YC, h)
                        nc.vector.tensor_tensor(d[1], ps[:, 4 + 2 * j, 0:T], d[0].bitcast(F32), ALU.subtract).then_inc(sz["free"], 1)

            def split_hidden(i):
                dve.wait_ge(ff_hi, i + 1)
                return lambda ii: nc.vector.tensor_tensor(FF[:, ds(2 * ii, 2), 1], HF, FF[:, ds(2 * ii, 2), 0].bitcast(F32),
                                                          ALU.subtract).then_inc(ff_done, 1)

            def ff1_empty(i, b):
                dve.drain()
                empty(up1, i, b, U)
                dve.drain()
                dve.sem_inc(ff_u, 1)
                dve.wait_ge(ff_c, 2 * i + b + 1)
                for back in (1, 2):
                    for t in range(2):
                        cw = vdyn(f"conv_w{2 - back}", 2 * i + 44 * b + t)
                        m = nc.vector.scalar_tensor_tensor(CV[:, t, back:], U[:, t, 0:T - back], cw, CV[:, t, back:], ALU.mult, ALU.add)
                    if back == 1:
                        dve.drain()
                if b == 0:
                    m.then_inc(ff_conv, 1)
                else:
                    dve.drain()
                    dve.wait_ge(ff_gelu, i + 1)
                    nc.vector.tensor_tensor(HF, GL, CV, ALU.mult).then_inc(ff_h, 1)
                    split_hidden(i)(i)

            def ff2_empty(i, b):
                dve.drain()
                if b == 0:
                    empty(up2, i, b, U)
                    dve.drain()
                    dve.sem_inc(ff_u, 1)
                else:
                    empty(up2, i, b, CV)
                    dve.drain()
                    dve.wait_ge(ff_gelu, FB + i + 1)
                    nc.vector.tensor_tensor(HF, GL, CV, ALU.mult).then_inc(ff_h, 1)
                    split_hidden(FB + i)(i)

            nc.vector.sem_inc(split, RAW)
            nc.vector.sem_inc(emptied, 2)
            nc.vector.sem_inc(head_free, 2)
            nc.vector.sem_inc(sz["free"], 2)
            dve.wait_ge(x_in, 16)
            norm_dve(0, x0, xn0)
            scale_dve(0, x0, xn0)
            dve.wait_ge(const_in, 16 * 9)
            lv = lamv.rearrange("p (a b) n -> p a b n", b=2)
            nc.vector.tensor_tensor(lamp, lv[:, :, 0], lv[:, :, 1], ALU.mult)
            dve.drain()
            nc.vector.tensor_reduce(lsum[:, 0:2], lamp, AX.X, ALU.add).then_inc(lam_sums, 1)
            dve.wait_ge(lam_exps, 1)
            nc.vector.scalar_tensor_tensor(neg_lam, lsum[:, 3:4], -LAM_INIT, lsum[:, 2:3], ALU.add, ALU.subtract)
            dve.wait_ge(vec_turned, 1)
            nc.vector.tensor_copy(vec, ps[:, 0, 0:NVEC])
            dve.drain()
            nc.vector.tensor_scalar(st[:, 96:97], v("diff_subln"), 1.0 - LAM_INIT, None, ALU.mult).then_inc(vec_ready, 1)
            dve.wait_ge(gw_hi, 1)
            nc.vector.tensor_tensor(gws[:, :, 1], gw, gws[:, :, 0].bitcast(F32), ALU.subtract).then_inc(gw_split, 1)
            dve.wait_ge(table_psum, 1)
            nc.vector.tensor_copy(rbias[0:16, 0, 0:T], ps[0:16, 2, 0:T])
            nc.vector.tensor_copy(rbias[0:8, 1, 0:T], ps[0:8, 3, 0:T])
            nc.vector.memset(rbias[0:16, :, T:384], NEG).then_inc(table_sb, 1)
            turn_dve(0)
            dve.wait_ge(gate_psum, 1)
            nc.vector.tensor_reduce(gates, ps[:, 0:2, 0:48].rearrange("p h (a n) -> p h n a", a=2), AX.X, ALU.add).then_inc(gate_sum, 1)

            e_qk, e_v, e_q = tiles(diff_qk, QK), columns(diff_v, DV), tiles(nsa_q, NQ)
            stream(diff_qk, e_qk)
            stream(diff_v, e_v, carried=late(diff_qk, e_qk))
            dve.wait_ge(bias_ready[0], 12)
            dve.wait_ge(gate_ready, 1)
            stream(nsa_q, e_q, diff_after, late(diff_v, e_v))
            e_k = lambda i, b: empty(nsa_k, i, b, NKs[:, 2 * b:2 * b + 2])
            e_nv = lambda i, b: empty(nsa_v, i, b, NVs[:, :, b])
            stream(nsa_k, e_k, lambda i, c: diff_after(3, c), late(nsa_q, e_q))

            def between(i, c):
                if c == 0:
                    dve.wait_ge(head_free, 2 + HEADS)
                    nc.vector.tensor_scalar(st[:, 64:80], st[:, 64:80], 1.0 / P, EPS, ALU.mult, ALU.add).then_inc(dn["var"], 1)
                if c == 1:
                    dve.wait_ge(dn["root"], 1)
                    nc.vector.reciprocal(st[:, 64:80], st[:, 80:96])
                    dve.drain()
                    od = OD.rearrange("p a h e -> p (a h) e")
                    nc.vector.tensor_tensor(od, od, st[:, 64:80].unsqueeze(2).to_broadcast([P, 16, P]), ALU.mult).then_inc(dn["scaled"], 1)
                if c == 3:
                    for b, (dst, name) in enumerate(((kblk, "cmp_pos_k"), (vblk, "cmp_pos_v"))):
                        pos = v(name, 0, 32).unsqueeze(2).to_broadcast([P, 32, NC])
                        for g in range(2):
                            src = NQ[:, 8 + 2 * b + g]
                            win = bass.AP(src.tensor, src.offset, [src.ap[0], [1, 32], [16, NC]])
                            m = nc.vector.tensor_tensor(dst[:, :, g * NC:(g + 1) * NC], win, pos, ALU.add)
                        m.then_inc(blk_sum, 1)
                if c == 5:
                    for b, (src, dst) in enumerate(((kblk, ksp), (vblk, vsp))):
                        dve.wait_ge(blk_hi, b + 1)
                        nc.vector.tensor_tensor(dst[:, :, 1], src, dst[:, :, 0].bitcast(F32), ALU.subtract).then_inc(blk_split, 1)
                if c == 6:
                    for q in range(4):
                        dve.wait_ge(dn["round"], q + 1)
                        nc.vector.scalar_tensor_tensor(MIX[:, 2 * q:2 * q + 2, 1], ps[:, 4 + q].rearrange("p (c t) -> p c t", c=2),
                                                       st[:, 96:97], MIX[:, 2 * q:2 * q + 2, 0].bitcast(F32), ALU.mult,
                                                       ALU.subtract).then_inc(dn["done"], 1)

            stream(nsa_v, e_nv, between, late(nsa_k, e_k))

            def e_sq(i, b):
                empty(squeeze, i, b, hid[:, b], 2 * NC)
                dve.drain()
                dve.sem_inc(hid_sum, 1)

            stream(squeeze, e_sq, carried=late(nsa_v, e_nv))
            finish(squeeze, e_sq)
            dve.wait_ge(w2_in, 48)
            dve.wait_ge(cs_psum, 1)
            for a in range(2):
                nc.vector.scalar_tensor_tensor(cl[:, a], ps[:, 6 + a, 0:HEADS * NC].rearrange("p (h c) -> p h c", c=NC), 128 ** -0.5,
                                               cmk[:, a:a + 1].to_broadcast([P, HEADS, NC]), ALU.mult, ALU.add)
            dve.drain()
            ah = cl.rearrange("p a h c -> p (a h) c")
            cm = st[:, 100:116]
            cmb = cm.unsqueeze(2).to_broadcast([P, 16, NC])
            nc.vector.tensor_reduce(cm, ah, AX.X, ALU.max)
            dve.drain()
            nc.vector.tensor_tensor(ah, ah, cmb, ALU.subtract).then_inc(cs_logit, 1)
            dve.wait_ge(cs_exp, 1)
            for a in range(2):
                nc.vector.tensor_tensor(cl[:, a], cl[:, a], cmk[:, 2 + a:3 + a].to_broadcast([P, HEADS, NC]), ALU.mult)
            nc.vector.memset(PC, 0.0)
            dve.drain()
            nc.vector.tensor_reduce(cm, ah, AX.X, ALU.add)
            dve.drain()
            nc.vector.tensor_scalar(cm, cm, TINY, None, ALU.max)
            dve.drain()
            nc.vector.reciprocal(cm, cm)
            dve.drain()
            cm2 = cm.rearrange("p (a h) -> p a h", a=2)
            nc.vector.tensor_tensor(cm2, cm2, gates.rearrange("p a (h c) -> p a h c", c=3)[:, :, :, 0], ALU.mult)
            dve.drain()
            nc.vector.tensor_tensor(PC.rearrange("p a h c -> p (a h) c")[:, :, 0:NC], ah, cmb, ALU.mult).then_inc(cs_prob, 1)

            e_oa = columns(out_a, Y1)

            def e_ob(i, b):
                empty(out_b, i, b, ya_tmp[:, b % 2])
                dve.drain()
                y = Y1[:, :, ds(NB * (4 * i + b), NB)]
                nc.vector.tensor_tensor(y, y, ya_tmp[:, b % 2], ALU.add)

            stream(out_a, e_oa, nsa_after)
            dve.drain()
            dve.sem_inc(nsa_done, 1)
            stream(out_b, e_ob, carried=late(out_a, e_oa))
            finish(out_b, e_ob)
            dve.drain()
            dve.sem_inc(y_ready[0], 1)
            norm_dve(1, Y1, xn1)
            dve.wait_ge(x_reloaded[0], 16)
            dve.wait_ge(gain_in[0], 16)
            add_normed(1, Y1, X1, gain1, xn1, X1).then_inc(x_ready[0], 1)
            dve.drain()
            norm_dve(2, X1, xn1)
            scale_dve(2, X1, xn1)
            turn_dve(2)
            dve.wait_ge(spilled[0], 16)
            stream(up1, ff1_empty)
            e_d1 = columns(down1, Yd)
            stream(down1, e_d1, carried=late(up1, ff1_empty))
            finish(down1, e_d1)
            dve.drain()
            dve.sem_inc(y_ready[1], 1)
            norm_dve(3, Yd, xn2)
            dve.wait_ge(x_reloaded[1], 16)
            dve.wait_ge(gain_in[1], 16)
            add_normed(3, Yd, Xd, gain2, xn2, X2).then_inc(x_ready[1], 1)
            dve.drain()
            norm_dve(4, X2, xn2)
            scale_dve(4, X2, xn2)
            turn_dve(4)
            e_sqk, e_sv = tiles(sb_qk, SQK), columns(sb_v, SV)
            e_mqk, e_mv, e_pu = tiles(moba_qk, MQK), columns(moba_v, MV), tiles(pool_u, UP)
            stream(sb_qk, e_sqk)
            stream(sb_v, e_sv, carried=late(sb_qk, e_sqk))
            stream(moba_qk, e_mqk, sb_after, late(sb_v, e_sv))
            stream(moba_v, e_mv, carried=late(moba_qk, e_mqk))
            dve.wait_ge(bias_ready[1], 4)
            dve.wait_ge(spilled[1], 16)
            stream(pool_u, e_pu, moba_after, late(moba_v, e_mv))
            finish(pool_u, e_pu)
            dve.drain()
            for g in range(4):
                u = UP[:, 2 * g:2 * g + 2]
                src = u
                dve.drain()
                for s in range(g + 1):
                    dst, back = (PW, PX)[s % 2], 1 << s
                    nc.vector.tensor_copy(dst[:, :, 0:back], src[:, :, 0:back])
                    nc.vector.tensor_tensor(dst[:, :, back:], src[:, :, back:], src[:, :, 0:T - back], ALU.add)
                    dve.drain()
                    src = dst
                q = (PX, PW)[g % 2]
                cnt = k1[:, CNT + 16 * g:CNT + 16 * (g + 1)].unsqueeze(1).to_broadcast([P, 2, 16])
                nc.vector.tensor_tensor(q[:, :, 0:16], src[:, :, 0:16], cnt, ALU.mult)
                nc.vector.tensor_scalar(q[:, :, 16:], src[:, :, 16:], 1.0 / (2 << g), None, ALU.mult)
                dve.drain()
                nc.vector.tensor_tensor(q, q, u, ALU.subtract).then_inc(pooled, 1)
                dve.wait_ge(pool_hi, g + 1)
                nc.vector.tensor_tensor(PS[:, 2 * g:2 * g + 2, 1], q, PS[:, 2 * g:2 * g + 2, 0].bitcast(F32), ALU.subtract).then_inc(pool_split, 1)
            stream(pool_w)
            for g in range(4):
                q = (PX, PW)[g % 2]
                if g % 2 == 0:
                    dve.wait_ge(pool_p, g // 2 + 1)
                else:
                    dve.wait_ge(used, SPL + pool_w.units(0, g // 2))
                dve.drain()
                nc.vector.tensor_reduce(q, halves(g), AX.X, ALU.add).then_inc(emptied, 1)
                dve.drain()
                for t in range(2):
                    m = nc.vector.tensor_scalar(q[:, t], q[:, t], v("pool_scale_2", 2 * g + t), None, ALU.mult)
                m.then_inc(pooled, 1)
                dve.drain()
                dve.wait_ge(pool_hi, 4 + g + 1)
                nc.vector.tensor_tensor(YB[:, 2 * g:2 * g + 2, 1], q, YB[:, 2 * g:2 * g + 2, 0].bitcast(F32), ALU.subtract).then_inc(pool_done, 1)

            def merge_empty(i, b):
                dve.drain()
                if b % 2 == 0:
                    empty(merge, i, b, GT)
                    dve.drain()
                    dve.sem_inc(mg_logit, 1)
                    return
                empty(merge, i, b, BR)
                dve.drain()
                dve.wait_ge(mg_gate, 3 * i + b // 2 + 1)
                if b == 1:
                    nc.vector.tensor_tensor(MA, BR, GS, ALU.mult)
                    return
                nc.vector.tensor_tensor(BR, BR, GS, ALU.mult)
                dve.drain()
                m = nc.vector.tensor_tensor(MA, MA, BR, ALU.add)
                if b == 5:
                    m.then_inc(mg_m, 1)
                    dve.drain()
                    dve.wait_ge(mg_hi, i + 1)
                    nc.vector.tensor_tensor(MM[:, ds(2 * i, 2), 1], MA, MM[:, ds(2 * i, 2), 0].bitcast(F32), ALU.subtract).then_inc(mg_done, 1)

            stream(merge, merge_empty)
            finish(merge, merge_empty)
            e_o2 = columns(out_2, Y3)
            stream(out_2, e_o2)
            finish(out_2, e_o2)
            dve.drain()
            dve.wait_ge(x_reloaded[2], 16)
            nc.vector.tensor_tensor(X3, X3, Y3, ALU.add).then_inc(x_ready[2], 1)
            dve.drain()
            norm_dve(5, X3, xn3)
            scale_dve(5, X3, xn3)
            turn_dve(5)
            dve.wait_ge(spilled[2], 16)
            stream(up2, ff2_empty)
            e_d2 = columns(down2, Yd)
            stream(down2, e_d2, carried=late(up2, ff2_empty))
            finish(down2, e_d2)
            dve.drain()
            dve.wait_ge(x_reloaded[3], 16)
            dve.wait_ge(gain_in[2], 16)
            nc.vector.tensor_tensor(Xd, Xd, Yd, ALU.add).then_inc(y_ready[2], 1)
            dve.drain()
            norm_dve(6, Xd, fin)
            for a in range(2):
                nc.vector.scalar_tensor_tensor(fin[:, a], Xd[:, a], st[:, 24 + a:25 + a], gain2, ALU.mult, ALU.mult).then_inc(y_ready[3], 1)


_INS = ["x", "pre_mix_norm", "w_in", "lambda_q1", "lambda_k1", "lambda_q2", "lambda_k2", "diff_subln", "cmp_pos_k",
        "cmp_pos_v", "cmp_k_w1", "cmp_k_w2", "cmp_v_w1", "cmp_v_w2", "rel_bias", "w_out", "post_mix_norm",
        "pre_ffn_norm", "w_up", "conv_w", "conv_b", "w_down", "post_ffn_norm", "norm_mix_2", "norm_ffn_2", "w_in_2",
        "w_pool_2", "pool_scale_2", "w_br_a_2", "w_br_b_2", "w_br_c_2", "w_out_2", "w_gate_2", "w_up_2", "w_down_2",
        "rel_bias_2", "norm_final_2"]


def kernel(**inputs):
    import concourse.bacc as bacc
    from concourse.bass_utils import run_bass_kernel_spmd

    nc = bacc.Bacc("TRN2", target_bir_lowering=False, num_devices=1)
    arrays, w = {}, {}
    for name in _INS + ["consts"]:
        a = np.ascontiguousarray(shape_constants() if name == "consts" else inputs[name])
        arrays[f"in_{name}_dram"] = a
        w[name] = nc.dram_tensor(f"in_{name}_dram", a.shape, mybir.dt.from_np(a.dtype), kind="ExternalInput").ap()
    out = nc.dram_tensor("out_0_dram", (1, T, D), F32, kind="ExternalOutput").ap()
    two_blocks(nc, w, out)
    r = run_bass_kernel_spmd(nc, [arrays], core_ids=[0])
    return r.results[0]["out_0_dram"]
```

```python
import math
from contextlib import ExitStack

import numpy as np

import concourse.bass as bass
from concourse import mybir

F32 = mybir.dt.float32
F32R = mybir.dt.float32r
ACT = mybir.ActivationFunctionType
ALU = mybir.AluOpType
AX = mybir.AxisListType

P = 128
T = 256
D = 2048
NK = D // P
F = 5632
NF = F // P
NB = 256
FB = F // NB
KC = 4
RAW = 8
SPL = 4
HEADS = 8
NC = (T - 32) // 16 + 1
NEG = -1e30
TINY = 1e-30
EPS = 1e-6
LAM_INIT = 0.8 - 0.6 * math.exp(0.0)
COLS, TOKS = 0, 1
LAG = 3
KB = 1024

IDENT, FLIP, LOWER, ONES, SBMASK, CNT, CNEG, CONE, HOT1, HOT2 = np.cumsum([0, 128, 128, 128, 128, 384, 64, 2 * NC, 2 * NC, 256]).tolist()
NCONST = HOT2 + 256

VECS = [("pre_mix_norm", 16), ("pre_ffn_norm", 16), ("norm_mix_2", 16), ("norm_ffn_2", 16), ("pool_scale_2", 8),
        ("diff_subln", 1), ("conv_b", 88), ("conv_w0", 88), ("conv_w1", 88), ("conv_w2", 88), ("cmp_pos_k", 32), ("cmp_pos_v", 32)]
VEC_TILES = [[0, 1, 2, 3, 4, 5], [6], [7], [8], [9], [10, 11]]
VAT = dict(zip([n for n, _ in VECS], np.cumsum([0] + [n for _, n in VECS]).tolist()))
NVEC = sum(n for _, n in VECS)


def shape_constants():
    c = np.zeros((P, NCONST), np.float32)
    r = np.arange(P)
    c[r, IDENT + r] = 1
    c[r, FLIP + P - 1 - r] = 1
    c[:, LOWER:LOWER + P] = -(r[:, None] >= r[None, :]).astype(np.float32)
    c[:, ONES:ONES + P] = -1
    strict = np.where(r[:, None] < r[None, :], 0, NEG)
    c[:, SBMASK:SBMASK + P] = strict
    c[:, SBMASK + 2 * P:SBMASK + 3 * P] = strict
    for g in range(4):
        c[:, CNT + 16 * g:CNT + 16 * (g + 1)] = 1.0 / np.minimum(np.arange(16) + 1, 2 << g)
    for a in range(2):
        ok = (np.arange(NC) * 16 + 31)[None, :] <= (r + a * P)[:, None]
        c[:, CNEG + a * NC:CNEG + (a + 1) * NC] = np.where(ok, 0, NEG)
        c[:, CONE + a * NC:CONE + (a + 1) * NC] = ok
    for at, far in ((HOT1, 128), (HOT2, 2048)):
        d = T - 1 - np.arange(T)
        large = 16 + (np.log(np.maximum(d, 1) / 16) / math.log(far / 16) * 16).astype(np.int32)
        bucket = np.where(d < 16, d, np.minimum(large, 31))
        c[bucket, at + np.arange(T)] = 1
    return c


class Phase:

    unit = block = slot = 0
    loads = [0] * RAW

    @classmethod
    def reset(cls):
        cls.unit = cls.block = cls.slot = 0
        cls.loads = [0] * RAW

    def __init__(self, iters, blocks, nblocks=None):
        self.iters, self.blocks = iters, blocks
        self.n = sum(blocks)
        self.nb = nblocks or len(blocks)
        self.u0, self.b0, self.rot = Phase.unit, Phase.block, Phase.slot
        self.loads0 = list(Phase.loads)
        Phase.unit += iters * self.n
        Phase.block += iters * self.nb
        Phase.slot = (self.rot + self.n) % RAW
        self.per = [sum(self.slot_of(c) == s for c in range(self.n)) for s in range(RAW)]
        Phase.loads = [a + iters * b for a, b in zip(Phase.loads, self.per)]

    def slot_of(self, c):
        return (self.rot + c) % RAW

    def units(self, i, c):
        return self.u0 + i * self.n + c + 1

    def blocks_(self, i, b):
        return self.b0 + i * self.nb + b + 1

    def before(self, i, c, ring):
        if c >= ring or self.iters == 1:
            prev = c - ring
        else:
            prev = c + (self.n - 1 - c) // ring * ring - self.n
        return self.units(i, prev)

    def loaded(self, i, c):
        s = self.slot_of(c)
        nth = sum(self.slot_of(x) == s for x in range(c + 1))
        return 16 * (self.loads0[s] + i * self.per[s] + nth)

    def where(self, c):
        for b, k in enumerate(self.blocks):
            if c < k:
                return b, c
            c -= k

    def ends(self):
        out, e = [], -1
        for b, k in enumerate(self.blocks):
            e += k
            out.append(((e + LAG) % self.n if self.n > LAG else 0, b, e + LAG >= self.n))
        return out


def two_blocks(nc, w, out):
    Phase.reset()
    diff_qk = Phase(4, [4, 4])
    diff_v = Phase(2, [4, 4])
    nsa_q = Phase(3, [4, 4])
    nsa_k = Phase(1, [4, 4])
    squeeze = Phase(1, [8, 8])
    nsa_v = Phase(1, [4, 4])
    out_a = Phase(2, [2, 2, 2, 2])
    out_b = Phase(2, [2, 2, 2, 2])
    up1 = Phase(FB, [4, 4])
    down1 = Phase(4, [11, 11])
    sb_qk = Phase(4, [4, 4])
    sb_v = Phase(2, [4, 4])
    pool_u = Phase(2, [4, 4])
    moba_v = Phase(2, [4, 4])
    pool_w = Phase(1, [1, 1])
    moba_qk = Phase(4, [4, 4])
    merge = Phase(8, [4, 2, 4, 2, 4, 2])
    out_2 = Phase(4, [4, 4])
    up2 = Phase(FB, [4, 4])
    down2 = Phase(4, [11, 11])

    with ExitStack() as ctx:
        def sem(name):
            return ctx.enter_context(nc.semaphore(name))

        BASE = (nc.sbuf_base + 31) // 32 * 32
        at = [BASE]

        def fixed(name, shape, dt=F32):
            t = nc.alloc_sbuf_tensor_at(name, shape, dt, offset=at[0])
            at[0] += (int(np.prod(shape[1:])) * 4 + 31) // 32 * 32
            return t.ap() if hasattr(t, "ap") and callable(t.ap) else t

        raw = fixed("raw", [P, RAW, KC, NB])
        spl = fixed("spl", [P, SPL, KC, 2, NB], F32R)
        HA0 = at[0]
        HA = fixed("HA", [P, NK, 2, T], F32R)
        k1 = fixed("k1", [P, CNEG])
        vec = fixed("vec", [P, NVEC])
        st = fixed("st", [P, 128])
        gates = fixed("gates", [P, 2, 24])
        neg_lam = fixed("neg_lam", [P, 1])
        lsum = fixed("lsum", [P, 4])
        G0 = at[0]

        def inG(name, kb, shape, dt=F32, base=G0):
            t = nc.alloc_sbuf_tensor_at(name, shape, dt, offset=int(base + kb * KB))
            assert base != G0 or kb * KB + int(np.prod(shape[1:])) * 4 <= 104 * KB, name
            return t.ap() if hasattr(t, "ap") and callable(t.ap) else t

        def inH(name, kb, shape, dt=F32):
            assert kb * KB + int(np.prod(shape[1:])) * 4 <= 32 * KB, name
            return inG(name, kb, shape, dt, HA0)

        x0 = inG("x0", 0, [P, 2, D])
        xn0 = inG("xn0", 16, [P, 2, D])
        rows = inG("rows", 32, [P, 6, P])
        k2 = inG("k2", 36, [P, NCONST - CNEG])
        tab1 = inG("tab1", 42, [P, 16])
        tab2 = inG("tab2", 42.25, [P, 8])
        rbias = inG("rbias", 42.5, [P, 2, 384])
        lamv = inG("lamv", 46, [P, 4, 64])
        lamp = inG("lamp", 47, [P, 2, 64])
        gw = inG("gw", 48, [P, NK, 24])
        gws = inG("gws", 50, [P, NK, 2, 24], F32R)
        hank1 = inG("hank1", 54, [P, 16, T])
        QK = inG("QK", 0, [P, 16, T])
        DV = inG("DV", 16, [P, 2, 1024])
        NQ = inG("NQ", 24, [P, 12, T])
        NKs = inG("NKs", 36, [P, 4, T])
        NVs = inG("NVs", 40, [P, 2, 2, T])
        MIX = inG("MIX", 44, [P, NK, 2, T], F32R)
        OD = inG("OD", 60, [P, 2, HEADS, P])
        bias1 = inG("bias1", 76, [P, 16, T])
        LG = inG("LG", 92, [P, 2, 2, 384])
        PT = inG("PT", 98, [P, 2, 2, 384])
        kblk = inG("kblk", 68, [P, 32, 2 * NC])
        vblk = inG("vblk", 72, [P, 32, 2 * NC])
        ksp = inG("ksp", 0, [P, 32, 2, 2 * NC], F32R)
        vsp = inG("vsp", 8, [P, 32, 2, 2 * NC], F32R)
        PC = inG("PC", 16, [P, 2, HEADS, 32])
        PcT = inG("PcT", 18, [P, 2, T])
        vcr = inG("vcr", 20, [P, 2, P])
        kcT = inG("kcT", 21, [P, 2 * NC])
        hid_rows = inG("hid_rows", 21.25, [P, 2, NB])
        w2 = inG("w2", 32, [P, 2, 2, P])
        hid = inG("hid", 34, [P, 2, 2, 2 * NC])
        cmk = inG("cmk", 34.5, [P, 4, NC])
        cl = inG("cl", 34.75, [P, 2, HEADS, NC])
        Y1 = inG("Y1", 0, [P, 2, D])
        gain1 = inG("gain1", 32, [P, D])
        X1 = inG("X1", 88, [P, 2, D])
        xn1 = inG("xn1", 16, [P, 2, D])
        ya_tmp = inG("ya_tmp", 40, [P, 2, 2, NB])
        FF = inG("FF", 0, [P, NF, 2, T], F32R)
        U = inG("U", 88, [P, 2, T])
        CV = inG("CV", 90, [P, 2, T])
        GL = inG("GL", 92, [P, 2, T])
        HF = inG("HF", 94, [P, 2, T])
        Yd = inH("Yd", 0, [P, 2, D])
        Xd = inH("Xd", 16, [P, 2, D])
        gain2 = inG("gain2", 96, [P, D])
        X2 = inG("X2", 48, [P, 2, D])
        xn2 = inG("xn2", 64, [P, 2, D])
        hank2 = inG("hank2", 88, [P, 8, T])
        SQK = inG("SQK", 0, [P, 16, T])
        SV = inG("SV", 16, [P, 2, 1024])
        UP = inG("UP", 24, [P, 8, T])
        PQ = inG("PQ", 32, [P, 4, 2, T])
        PD = inG("PD", 100, [P, 2, T])
        PS = inG("PS", 48, [P, 8, 2, T], F32R)
        MQK = inG("MQK", 16, [P, 16, T])
        MV = inG("MV", 40, [P, 2, 1024])
        YA = inG("YA", 48, [P, 8, 2, T], F32R)
        YC = inG("YC", 64, [P, 8, 2, T], F32R)
        bias2 = inG("bias2", 80, [P, 8, T])
        SZ = inG("SZ", 88, [P, 2, 4, 384])
        LM = inG("LM", 96, [P, 2, 384])
        PM = inG("PM", 99, [P, 2, 384])
        YB = inG("YB", 0, [P, 8, 2, T], F32R)
        MM = inG("MM", 16, [P, NK, 2, T], F32R)
        GT = inG("GT", 88, [P, 2, T])
        GS = inG("GS", 90, [P, 2, T])
        BR = inG("BR", 92, [P, 2, T])
        MA = inG("MA", 94, [P, 2, T])
        Y3 = inG("Y3", 48, [P, 2, D])
        X3 = inG("X3", 64, [P, 2, D])
        xn3 = inG("xn3", 0, [P, 2, D])
        fin = inG("fin", 0, [P, 2, D])

        ps = ctx.enter_context(nc.psum_tensor("ps", [P, 8, 512], F32))
        table = nc.dram_tensor("table", [24, 384], F32, kind="Internal").ap()
        spill = nc.dram_tensor("spill", [3, T, D], F32, kind="Internal").ap()

        loaded = [sem(f"loaded{s}") for s in range(RAW)]
        hi_done = sem("hi_done")
        split = sem("split")
        used = sem("used")
        emptied = sem("emptied")

        x_in = sem("x_in")
        const_in = sem("const_in")
        vec_in = sem("vec_in")
        vec_turned = sem("vec_turned")
        vec_ready = sem("vec_ready")
        lam_sums = sem("lam_sums")
        lam_exps = sem("lam_exps")
        gw_hi = sem("gw_hi")
        gw_split = sem("gw_split")
        gate_psum = sem("gate_psum")
        gate_sum = sem("gate_sum")
        gate_ready = sem("gate_ready")
        table_psum = sem("table_psum")
        table_sb = sem("table_sb")
        table_out = sem("table_out")
        hank_in = [sem(f"hank_in{b}") for b in range(2)]
        flipped = [sem(f"flipped{b}") for b in range(2)]
        bias_ready = [sem(f"bias_ready{b}") for b in range(2)]
        NORM = ["sq", "var", "root", "rstd", "scaled_a", "scaled_d", "turned", "round", "done"]
        norm = {s: sem(f"norm_{s}") for s in NORM}
        x_reloaded = [sem(f"x_reloaded{n}") for n in range(4)]
        gain_in = [sem(f"gain_in{n}") for n in range(3)]
        spilled = [sem(f"spilled{n}") for n in range(3)]
        x_ready = [sem(f"x_ready{n}") for n in range(3)]
        y_ready = [sem(f"y_ready{n}") for n in range(4)]
        scores = sem("scores")
        logits = sem("logits")
        exps = sem("exps")
        probs = sem("probs")
        probs_turned = sem("probs_turned")
        probs_copied = sem("probs_copied")
        head_out = sem("head_out")
        head_hi = sem("head_hi")
        head_free = sem("head_free")
        dn = {s: sem(f"dn_{s}") for s in ("var", "root", "scaled", "turned", "round", "done")}
        w2_in = sem("w2_in")
        blk_sum = sem("blk_sum")
        blk_hi = sem("blk_hi")
        blk_split = sem("blk_split")
        hid_sum = sem("hid_sum")
        hid_turned = sem("hid_turned")
        hid_gelu = sem("hid_gelu")
        hid_ready = sem("hid_ready")
        cmp_psum = sem("cmp_psum")
        cmp_sb = sem("cmp_sb")
        cs_psum = sem("cs_psum")
        cs_logit = sem("cs_logit")
        cs_exp = sem("cs_exp")
        cs_prob = sem("cs_prob")
        cs_turned = sem("cs_turned")
        cs_ready = sem("cs_ready")
        nsa_done = sem("nsa_done")
        ff_u = sem("ff_u")
        ff_c = sem("ff_c")
        ff_conv = sem("ff_conv")
        ff_gelu = sem("ff_gelu")
        ff_h = sem("ff_h")
        ff_hi = sem("ff_hi")
        ff_done = sem("ff_done")
        sz = {s: sem(f"sb_{s}") for s in ("z", "zm", "ln", "sp", "aft", "e", "a", "out", "hi", "free")}
        pooled = sem("pooled")
        pool_hi = sem("pool_hi")
        pool_split = sem("pool_split")
        proj_sum = sem("proj_sum")
        proj_hi = sem("proj_hi")
        pool_done = sem("pool_done")
        mg_logit = sem("mg_logit")
        mg_gate = sem("mg_gate")
        mg_m = sem("mg_m")
        mg_hi = sem("mg_hi")
        mg_done = sem("mg_done")
        stored = sem("stored")

        def chunks(name):
            return w[name][0].rearrange("(k p) n -> p k n", p=P)

        def halves(b):
            return ps[:, 2 * (b % 2):2 * (b % 2) + 2].rearrange("p h (a n) -> p h n a", a=2)

        ident = k1[:, IDENT:IDENT + P]

        def ident_rows(n):
            return k1[0:n, IDENT:IDENT + n]

        def v(name, j=0, n=1):
            return vec[:, VAT[name] + j:VAT[name] + j + n]

        def vdyn(name, j):
            return vec[:, bass.ds(VAT[name] + j, 1)] if not isinstance(j, int) else v(name, j)

        def ds(a, n=1):
            return slice(a, a + n) if isinstance(a, int) else bass.ds(a, n)

        def flat(t):
            return t.rearrange("p a n -> p (a n)")

        NORMS = {0: (x0, xn0, "pre_mix_norm"), 2: (X1, xn1, "pre_ffn_norm"), 4: (X2, xn2, "norm_mix_2"), 5: (X3, xn3, "norm_ffn_2")}

        TURN = {0: 0, 2: 1, 4: 2, 5: 3}

        block = ctx.enter_context(nc.Block())

        @block.sync
        def _(sp):
            def load(ph, i, c, src):
                sp.wait_ge(split, RAW + ph.before(i, c, RAW))
                sp.dma_start(raw[:, ph.slot_of(c)], src).then_inc(loaded[ph.slot_of(c)], 16)

            def stream(ph, src):
                if ph.iters == 1:
                    for c in range(ph.n):
                        load(ph, 0, c, src(0, *ph.where(c)))
                else:
                    with sp.Fori(0, ph.iters) as i:
                        for c in range(ph.n):
                            load(ph, i, c, src(i, *ph.where(c)))

            def cols(name, block_of, k0=0):
                wv = chunks(name)
                return lambda i, b, k: wv[:, k0 + KC * k:k0 + KC * (k + 1), ds(NB * block_of(i, b), NB)]

            sp.dma_start(x0, w["x"][0].rearrange("(a p) d -> p a d", p=P)).then_inc(x_in, 16)
            stream(diff_qk, cols("w_in", lambda i, b: 2 * i + b))
            stream(diff_v, cols("w_in", lambda i, b: 8 + 2 * i + b))
            stream(nsa_q, cols("w_in", lambda i, b: 12 + 2 * i + b))
            stream(nsa_k, cols("w_in", lambda i, b: 18 + 2 * b))
            squeezers = [chunks("cmp_k_w1"), chunks("cmp_v_w1")]
            stream(squeeze, lambda i, b, k: squeezers[b][:, KC * k:KC * (k + 1), :])
            stream(nsa_v, cols("w_in", lambda i, b: 19 + 2 * b))
            stream(out_a, cols("w_out", lambda i, b: 4 * i + b))
            stream(out_b, cols("w_out", lambda i, b: 4 * i + b, 8))
            stream(up1, cols("w_up", lambda i, b: i + FB * b))
            stream(down1, cols("w_down", lambda i, b: 2 * i + b))
            stream(sb_qk, cols("w_in_2", lambda i, b: 16 + 2 * i + b))
            stream(sb_v, cols("w_in_2", lambda i, b: 24 + 2 * i + b))
            stream(pool_u, cols("w_in_2", lambda i, b: 12 + 2 * i + b))
            stream(moba_v, cols("w_in_2", lambda i, b: 8 + 2 * i + b))
            wp = w["w_pool_2"][0].rearrange("(c g) (k p) n -> c p (g k) n", p=P, g=2)
            stream(pool_w, lambda i, b, k: wp[b])
            stream(moba_qk, cols("w_in_2", lambda i, b: i + 4 * b))
            gate = chunks("w_in_2")
            branch = [chunks(n) for n in ("w_br_a_2", "w_br_b_2", "w_br_c_2")]

            def merge_src(i, b, k):
                g = 2 - b // 2
                if b % 2 == 0:
                    return gate[:, KC * k:KC * (k + 1), ds(NB * (28 + 8 * g + i), NB)]
                return branch[g][:, KC * k:KC * (k + 1), ds(NB * i, NB)]

            stream(merge, merge_src)
            stream(out_2, cols("w_out_2", lambda i, b: 2 * i + b))
            gu = [chunks("w_gate_2"), chunks("w_up_2")]
            stream(up2, lambda i, b, k: gu[b][:, KC * k:KC * (k + 1), ds(NB * i, NB)])
            stream(down2, cols("w_down_2", lambda i, b: 2 * i + b))

        @block.gpsimd
        def _(pool):
            def rows_of(name, dst, src):
                pool.dma_start(dst, src).then_inc(vec_in, 16)

            pool.dma_start(k1, w["consts"][:, 0:CNEG]).then_inc(const_in, 16)
            r = 0
            for name, n in VECS[:6]:
                rows_of(name, rows[r:r + n, 0, :], w[name][0].rearrange("(r p) -> r p", p=P))
                r += n
            rows_of("conv_b", rows[0:88, 1, :], w["conv_b"][0].rearrange("(r p) -> r p", p=P))
            for j in range(3):
                rows_of("conv_w", rows[0:88, 2 + j, :], w["conv_w"][0, j].rearrange("(r p) -> r p", p=P))
            rows_of("pos", rows[0:32, 5, :], w["cmp_pos_k"][0])
            rows_of("pos", rows[32:64, 5, :], w["cmp_pos_v"][0])
            pool.dma_start(gw, chunks("w_in")[:, :, 5632:5656]).then_inc(const_in, 16)
            pool.dma_start(k2, w["consts"][:, CNEG:]).then_inc(const_in, 16)
            pool.dma_start(tab1[0:32, :], w["rel_bias"]).then_inc(const_in, 16)
            pool.dma_start(tab2[0:32, :], w["rel_bias_2"].rearrange("h b -> b h"), allow_slow_non_contiguous=True).then_inc(const_in, 16)
            for j, name in enumerate(("lambda_q1", "lambda_k1", "lambda_q2", "lambda_k2")):
                pool.dma_start(lamv[:, j, :], w[name].to_broadcast([P, 64])).then_inc(const_in, 16)

            pool.wait_ge(table_sb, 1)
            pool.dma_start(table[0:16], rbias[0:16, 0, :]).then_inc(table_out, 16)
            pool.dma_start(table[16:24], rbias[0:8, 1, :]).then_inc(table_out, 16)
            pool.wait_ge(table_out, 32)
            window = lambda h0, n: bass.AP(table.tensor, h0 * 384, [[1, P], [384, n], [1, T]])
            pool.dma_start(hank1, window(0, 16)).then_inc(hank_in[0], 16)

            pool.wait_ge(used, SPL + nsa_k.units(0, nsa_k.n - 1))
            for j, name in enumerate(("cmp_k_w2", "cmp_v_w2")):
                pool.dma_start(w2[:, j], w[name][0].rearrange("(k p) n -> p k n", p=P)).then_inc(w2_in, 16)
            cm = w["consts"][:, CNEG:CNEG + 4 * NC].rearrange("p (a c) -> p a c", c=NC)
            pool.dma_start(cmk, cm).then_inc(w2_in, 16)

            pool.wait_ge(nsa_done, 1)
            pool.dma_start(X1, w["x"][0].rearrange("(a p) d -> p a d", p=P)).then_inc(x_reloaded[0], 16)
            pool.dma_start(gain1, w["post_mix_norm"].to_broadcast([P, D])).then_inc(gain_in[0], 16)

            def keep(n, x):
                pool.wait_ge(x_ready[n], 1)
                pool.dma_start(spill[n].rearrange("(a p) d -> p a d", p=P), x).then_inc(spilled[n], 16)

            def reload(n, x, r):
                pool.dma_start(x, spill[n].rearrange("(a p) d -> p a d", p=P)).then_inc(x_reloaded[r], 16)

            keep(0, X1)
            pool.wait_ge(used, SPL + up1.units(FB - 1, up1.n - 1))
            pool.wait_ge(spilled[0], 16)
            reload(0, Xd, 1)
            pool.dma_start(gain2, w["post_ffn_norm"].to_broadcast([P, D])).then_inc(gain_in[1], 16)
            keep(1, X2)
            pool.wait_ge(y_ready[1], 1)
            pool.dma_start(hank2, window(16, 8)).then_inc(hank_in[1], 16)
            for g in range(4):
                pool.wait_ge(emptied, 2 + pool_u.blocks_(g // 2, g % 2))
                src, q = UP[:, 2 * g:2 * g + 2], PQ[:, g]
                for n in range(g + 1):
                    dst, back = (PD, q)[(g - n) % 2], 1 << n
                    nc.gpsimd.tensor_copy(dst[:, :, 0:back], src[:, :, 0:back])
                    nc.gpsimd.tensor_tensor(dst[:, :, back:], src[:, :, back:], src[:, :, 0:T - back], ALU.add)
                    pool.drain()
                    src = dst
                cnt = k1[:, CNT + 16 * g:CNT + 16 * (g + 1)].unsqueeze(1).to_broadcast([P, 2, 16])
                nc.gpsimd.tensor_tensor(q[:, :, 0:16], src[:, :, 0:16], cnt, ALU.mult)
                nc.gpsimd.tensor_scalar(q[:, :, 16:], src[:, :, 16:], 1.0 / (2 << g), None, ALU.mult)
                pool.drain()
                nc.gpsimd.tensor_tensor(q, q, UP[:, 2 * g:2 * g + 2], ALU.subtract).then_inc(pooled, 1)
            pool.wait_ge(used, SPL + merge.units(7, merge.n - 1))
            pool.wait_ge(spilled[1], 16)
            reload(1, X3, 2)
            keep(2, X3)
            pool.wait_ge(used, SPL + up2.units(FB - 1, up2.n - 1))
            pool.wait_ge(spilled[2], 16)
            reload(2, Xd, 3)
            pool.dma_start(gain2, w["norm_final_2"].rearrange("(a d) -> a d", a=1).to_broadcast([P, D])).then_inc(gain_in[2], 16)
            oview = out[0].rearrange("(a p) d -> a p d", p=P)
            for a in range(2):
                pool.wait_ge(y_ready[3], a + 1)
                pool.dma_start(oview[a], fin[:, a]).then_inc(stored, 16)
            pool.wait_ge(stored, 32)

        @block.tensor
        def _(pe):
            def unit(ph, i, c, kinds, acts):
                b, k = ph.where(c)
                pe.wait_ge(split, RAW + ph.units(i, c))
                if k == 0:
                    pe.wait_ge(emptied, ph.blocks_(i, b))
                s = ph.slot_of(c) % SPL
                last_k = ph.blocks[b] * KC - 1
                for kk in range(KC):
                    act = acts(b, KC * k + kk)
                    wt = spl[:, s, kk]
                    n = act.shape[-1]
                    for h in range(2):
                        o = ps[:, 2 * (b % 2) + h]
                        first, last = KC * k + kk == 0, KC * k + kk == last_k
                        part = slice(h * P, (h + 1) * P)

                        def whole():
                            if kinds[b] == COLS:
                                return nc.tensor.matmul(o[:, 0:2 * n], wt[:, 0, part], flat(act), start=first, stop=last)
                            return nc.tensor.matmul(o, act[:, 0, part], flat(wt), start=first, stop=last)

                        def cross():
                            if kinds[b] == COLS:
                                return nc.tensor.matmul(o[:, n:2 * n], wt[:, 1, part], act[:, 0], start=False, stop=False)
                            return nc.tensor.matmul(o[:, NB:], act[:, 1, part], wt[:, 0], start=False, stop=False)

                        if first:
                            whole()
                            m = cross()
                        else:
                            cross()
                            m = whole()
                m.then_inc(used, 1)

            def stream(ph, kinds, acts, before=None, heads=False, ahead=None):
                peeled = ph.iters if heads else min(ph.iters, 1 if ahead or ph.iters == 1 else 0)
                for i in range(peeled):
                    for c in range(ph.n):
                        if ahead and i == 0:
                            ahead(c)
                        if before:
                            before(i, c)
                        unit(ph, i, c, kinds, acts)
                if peeled < ph.iters:
                    with pe.Fori(peeled, ph.iters) as i:
                        for c in range(ph.n):
                            if before:
                                before(i, c)
                            unit(ph, i, c, kinds, acts)

            def turn_norm(n, c):
                src, nth, s = NORMS[n][1], TURN[n], norm
                for q in {0: range(6), 1: range(6, 8)}.get(c, ()):
                    if q in (0, 4):
                        pe.wait_ge(s["scaled_a"], 2 * nth + 1 + q // 4)
                        pe.wait_ge(s["scaled_d"], 2 * nth + 1 + q // 4)
                    if q >= 4:
                        pe.wait_ge(s["done"], 8 * nth + q - 3)
                    for k in range(2):
                        for a in range(2):
                            at_ = (k * 2 + a) * P
                            m = nc.tensor.transpose(ps[:, 4 + q % 4, at_:at_ + P], src[:, a, (2 * q + k) * P:(2 * q + k + 1) * P], ident)
                    m.then_inc(s["turned"], 1)
                if c < 4:
                    pe.wait_ge(s["done"], 8 * nth + 2 * c + 2)

            def head_scores(q, k, bank):
                S = ps[:, bank]
                nc.tensor.matmul(S[:, 0:P], q[:, 0:P], k[:, 0:P], start=True, stop=True)
                return nc.tensor.matmul(S[:, P:3 * P], q[:, P:T], k, start=True, stop=True)

            def turn(src, bank):
                for j in range(3):
                    m = nc.tensor.transpose(ps[:, bank, j * P:(j + 1) * P], src[:, j * P:(j + 1) * P], ident)
                return m

            def free_bank(h):
                pe.wait_ge(head_free, h + 1)

            def diff_scores(i, j):
                h = 2 * i + j
                free_bank(h)
                for m in range(2):
                    r = slice(64 * m, 64 * m + 64)
                    q = QK[r, ds(h)].rearrange("p a t -> p (a t)")
                    k = QK[r, ds(h + 8)].rearrange("p a t -> p (a t)")
                    last = head_scores(q, k, 4 + 2 * j + m)
                last.then_inc(scores, 1)

            def diff_turn(i, j):
                h = 2 * i + j
                pe.wait_ge(probs, h + 1)
                turn(LG[:, j, 0], 4 + 2 * j).then_inc(probs_turned, 1)

            def diff_out(i, j):
                h = 2 * i + j
                pe.wait_ge(probs_copied, h + 1)
                pe.wait_ge(emptied, 2 + diff_v.blocks_(1, 1))
                O = ps[:, 5 + 2 * j]
                vh = [DV[:, a, ds(P * h, P)] for a in range(2)]
                pt = PT[:, j, 0]
                nc.tensor.matmul(O[:, 0:P], pt[:, 0:P], vh[0], start=True, stop=True)
                nc.tensor.matmul(O[:, P:T], pt[:, P:T], vh[0], start=True, stop=False)
                nc.tensor.matmul(O[:, P:T], pt[:, T:3 * P], vh[1], start=False, stop=True).then_inc(head_out, 1)

            def diff_before(i, c):
                for j in range(2):
                    if c == 0:
                        diff_scores(i, j)
                    if c == 3 + j:
                        diff_turn(i, j)
                    if c == 5 + j:
                        diff_out(i, j)

            def diff_finish(c):
                if c == 3:
                    pe.wait_ge(dn["scaled"], 1)
                    for q in range(4):
                        for c_ in range(2):
                            for a in range(2):
                                at_ = (c_ * 2 + a) * P
                                m = nc.tensor.transpose(ps[:, 4 + q, at_:at_ + P], OD[:, a, 2 * q + c_], ident)
                        m.then_inc(dn["turned"], 1)

            def nsa_before(g, c):
                pair, c = c // 4, c % 4
                for j in range(2):
                    hg = 2 * pair + j
                    nh = 4 * g + hg
                    if c == 0:
                        free_bank(HEADS + nh)
                        q = NQ[:, ds(nh)].rearrange("p a t -> p (a t)")
                        for m in range(2):
                            k = NKs[:, ds(2 * m + g)].rearrange("p a t -> p (a t)")
                            last = head_scores(q, k, 4 + 2 * j + m)
                        last.then_inc(scores, 1)
                    if c == 2:
                        pe.wait_ge(probs, HEADS + nh + 1)
                        turn(LG[:, j, 0], 4 + 2 * j)
                        turn(LG[:, j, 1], 5 + 2 * j).then_inc(probs_turned, 1)
                    if c == 3:
                        pe.wait_ge(probs_copied, HEADS + nh + 1)
                        pe.wait_ge(emptied, nsa_v.blocks_(0, 1) + 2)
                        O = ps[:, 4 + 2 * j, 0:T]
                        for m in range(2):
                            for a in range(2):
                                vh = NVs[:, a, m, ds(P * g, P)]
                                o, pt = (O, PT[:, j, m, 0:T]) if a == 0 else (O[:, P:T], PT[:, j, m, T:3 * P])
                                nc.tensor.matmul(o, vh, pt, start=(m == 0 and a == 0), stop=False)
                        r = slice(32 * hg, 32 * hg + NC)
                        nc.tensor.matmul(O, vcr[r, ds(g)].rearrange("p a e -> p (a e)"), PcT[r, ds(g)].rearrange("p a t -> p (a t)"),
                                         start=False, stop=True).then_inc(head_out, 1)

            def sb_before(i, c):
                for j in range(2):
                    h = 2 * i + j
                    X, Yb = ps[:, 4 + 2 * j], ps[:, 5 + 2 * j]
                    if c == 0:
                        pe.wait_ge(sz["free"], h + 1)
                        q = SQK[:, ds(h)].rearrange("p a t -> p (a t)")
                        k = SQK[:, ds(h + 8)].rearrange("p a t -> p (a t)")
                        nc.tensor.matmul(X[:, 0:T], k[:, 0:P], q, start=True, stop=True)
                        nc.tensor.matmul(X[:, T:3 * P], k[:, P:T], q[:, P:T], start=True, stop=True).then_inc(sz["z"], 1)
                    if c == 3 + j:
                        pe.wait_ge(sz["sp"], h + 1)
                        sp_ = SZ[:, j, 2]
                        low, one = k1[:, LOWER:LOWER + P], k1[:, ONES:ONES + P]
                        nc.tensor.matmul(Yb[:, 0:T], low, sp_[:, 0:T], start=True, stop=False)
                        nc.tensor.matmul(Yb[:, P:T], one, sp_[:, T:3 * P], start=False, stop=True)
                        nc.tensor.matmul(Yb[:, T:3 * P], low, sp_[:, T:3 * P], start=True, stop=True).then_inc(sz["aft"], 1)
                    if c == 5 + j:
                        pe.wait_ge(sz["a"], h + 1)
                        pe.wait_ge(emptied, 2 + sb_v.blocks_(1, 1))
                        a_ = SZ[:, j, 3]
                        nc.tensor.matmul(X[:, 0:T], SV[:, 0, ds(P * h, P)], a_[:, 0:T], start=True, stop=False)
                        nc.tensor.matmul(X[:, P:T], SV[:, 1, ds(P * h, P)], a_[:, T:3 * P], start=False, stop=True).then_inc(sz["out"], 1)

            def moba_before(pair, c):
                for j in range(2):
                    h = 2 * pair + j
                    n = 2 * HEADS + h
                    X, Yb = 4 + 2 * j, 5 + 2 * j
                    if c == 1:
                        free_bank(n)
                        pe.wait_ge(emptied, 2 + moba_qk.blocks_(pair, 1))
                        q = MQK[:, ds(h)].rearrange("p a t -> p (a t)")
                        k = MQK[:, ds(h + 8)].rearrange("p a t -> p (a t)")
                        head_scores(q, k, X).then_inc(scores, 1)
                    if c == 3:
                        pe.wait_ge(probs, n + 1)
                        turn(LM[:, j], Yb).then_inc(probs_turned, 1)
                    if c == 5:
                        pe.wait_ge(probs_copied, n + 1)
                        O = ps[:, X]
                        nc.tensor.matmul(O[:, 0:T], MV[:, 0, ds(P * h, P)], PM[:, j, 0:T], start=True, stop=False)
                        nc.tensor.matmul(O[:, P:T], MV[:, 1, ds(P * h, P)], PM[:, j, T:3 * P], start=False, stop=True).then_inc(head_out, 1)

            nc.tensor.sem_inc(used, SPL)
            nc.tensor.sem_inc(bias_ready[0], 4)

            pe.wait_ge(const_in, 16 * 9)
            pe.wait_ge(vec_in, 16 * 12)
            for j, members in enumerate(VEC_TILES):
                n = sum(VECS[m][1] for m in members)
                a = VAT[VECS[members[0]][0]]
                m = nc.tensor.transpose(ps[:, 0, a:a + n], rows[0:n, j], ident_rows(n))
            m.then_inc(vec_turned, 1)
            nc.tensor.matmul(ps[0:16, 2, 0:T], tab1[0:32], k2[0:32, HOT1 - CNEG:HOT1 - CNEG + T], start=True, stop=True)
            nc.tensor.matmul(ps[0:8, 3, 0:T], tab2[0:32], k2[0:32, HOT2 - CNEG:HOT2 - CNEG + T], start=True, stop=True).then_inc(table_psum, 1)

            def gate_logits(c):
                turn_norm(0, c)
                if c != 4:
                    return
                pe.wait_ge(gw_split, 1)
                for a in range(2):
                    o = ps[:, 4 + a]
                    for k in range(NK):
                        x_hi, x_lo = HA[:, k, 0, a * P:(a + 1) * P], HA[:, k, 1, a * P:(a + 1) * P]
                        if k:
                            nc.tensor.matmul(o[:, 24:48], x_lo, gws[:, k, 0], start=False, stop=False)
                        m = nc.tensor.matmul(o[:, 0:48], x_hi, flat(gws[:, k]), start=k == 0, stop=k == NK - 1)
                        if k == 0:
                            m = nc.tensor.matmul(o[:, 24:48], x_lo, gws[:, k, 0], start=False, stop=False)
                m.then_inc(gate_psum, 1)

            HAc = lambda b, k: HA[:, k]
            stream(diff_qk, [COLS, COLS], HAc, ahead=gate_logits)
            pe.wait_ge(gate_sum, 1)
            pe.wait_ge(hank_in[0], 16)

            def bias_before(i, c):
                if c == 0:
                    pe.wait_ge(bias_ready[0], 4 * i + 4)
                    for q in range(4):
                        nc.tensor.matmul(ps[:, 4 + q], k1[:, FLIP:FLIP + P], hank1[:, ds(8 * i + 2 * q, 2)].rearrange("p h t -> p (h t)"),
                                         start=True, stop=True).then_inc(flipped[0], 1)

            stream(diff_v, [TOKS, TOKS], HAc, bias_before)
            pe.wait_ge(bias_ready[0], 12)
            stream(nsa_q, [COLS, COLS], HAc, diff_before, heads=True)
            stream(nsa_k, [COLS, COLS], HAc, lambda i, c: diff_before(3, c))
            pe.wait_ge(blk_split, 2)
            for c in range(squeeze.n):
                diff_finish(c)
                b, k = squeeze.where(c)
                pe.wait_ge(split, RAW + squeeze.units(0, c))
                if k == 0:
                    pe.wait_ge(emptied, squeeze.blocks_(0, b))
                o = ps[0:2 * NC, 2 * b]
                for kk in range(KC):
                    wt, act = spl[:, squeeze.slot_of(c) % SPL, kk], (ksp, vsp)[b][:, KC * k + kk]
                    first, last = KC * k + kk == 0, KC * k + kk == 31
                    if not first:
                        nc.tensor.matmul(o[:, NB:], act[:, 1], wt[:, 0], start=False, stop=False)
                    m = nc.tensor.matmul(o, act[:, 0], flat(wt), start=first, stop=last)
                    if first:
                        nc.tensor.matmul(o[:, NB:], act[:, 1], wt[:, 0], start=False, stop=False)
                m.then_inc(used, 1)

            def compressed(c):
                if c == 1:
                    pe.wait_ge(hid_gelu, 1)
                    pe.wait_ge(dn["done"], 4)
                    for b in range(2):
                        for k in range(2):
                            at_ = (2 * b + k) * 2 * NC
                            m = nc.tensor.transpose(ps[:, 7, at_:at_ + 2 * NC], hid_rows[0:2 * NC, b, k * P:(k + 1) * P], ident_rows(2 * NC))
                    m.then_inc(hid_turned, 1)
                if c == 2:
                    pe.wait_ge(hid_ready, 1)
                    pe.wait_ge(w2_in, 48)
                    for k in range(2):
                        nc.tensor.matmul(ps[:, 4, 0:2 * NC], w2[:, 0, k], hid[:, 0, k], start=k == 0, stop=k == 1)
                    for j in range(4):
                        for g in range(2):
                            for k in range(2):
                                m = nc.tensor.matmul(ps[32 * j:32 * j + NC, 5, g * P:(g + 1) * P], hid[:, 1, k, g * NC:(g + 1) * NC],
                                                     w2[:, 1, k], start=k == 0, stop=k == 1)
                    m.then_inc(cmp_psum, 1)
                if c == 3:
                    pe.wait_ge(cmp_sb, 1)
                    for a in range(2):
                        for h in range(HEADS):
                            m = nc.tensor.matmul(ps[:, 6 + a, h * NC:(h + 1) * NC], NQ[:, h, a * P:(a + 1) * P],
                                                 kcT[:, (h // 4) * NC:(h // 4 + 1) * NC], start=True, stop=True)
                    m.then_inc(cs_psum, 1)
                if c == 7:
                    pe.wait_ge(cs_prob, 1)
                    for g in range(2):
                        for a in range(2):
                            m = nc.tensor.transpose(ps[:, 4, (g * 2 + a) * P:(g * 2 + a + 1) * P],
                                                    PC[:, a, 4 * g:4 * g + 4].rearrange("p h c -> p (h c)"), ident)
                    m.then_inc(cs_turned, 1)

            stream(nsa_v, [TOKS, TOKS], HAc, lambda i, c: compressed(c))
            pe.wait_ge(cs_ready, 1)
            MIXc = lambda b, k: MIX[:, k]
            stream(out_a, [TOKS] * 4, MIXc, nsa_before, heads=True)
            pe.wait_ge(head_free, 2 + 2 * HEADS)
            stream(out_b, [TOKS] * 4, lambda b, k: MIX[:, 8 + k])
            stream(up1, [COLS, COLS], HAc, ahead=lambda c: turn_norm(2, c))

            def hidden_ready(n):
                def ahead(c):
                    if c == 0:
                        pe.wait_ge(ff_done, n * FB - 1)
                    if c == 10:
                        pe.wait_ge(ff_done, n * FB)
                return ahead

            FFc = lambda b, k: FF[:, k]
            stream(down1, [TOKS, TOKS], FFc, ahead=hidden_ready(1))
            stream(sb_qk, [COLS, COLS], HAc, ahead=lambda c: turn_norm(4, c))
            pe.wait_ge(hank_in[1], 16)
            for q in range(4):
                nc.tensor.matmul(ps[:, 4 + q], k1[:, FLIP:FLIP + P], hank2[:, 2 * q:2 * q + 2].rearrange("p h t -> p (h t)"),
                                 start=True, stop=True).then_inc(flipped[1], 1)
            stream(sb_v, [TOKS, TOKS], HAc)
            pe.wait_ge(bias_ready[1], 4)
            stream(pool_u, [COLS, COLS], HAc, sb_before, heads=True)
            stream(moba_v, [TOKS, TOKS], HAc, lambda i, c: sb_before(i + 2, c), heads=True)
            pe.wait_ge(sz["free"], 2 + HEADS)
            for c in range(2):
                pe.wait_ge(split, RAW + pool_w.units(0, c))
                pe.wait_ge(pool_split, 2 * c + 2)
                for g in (2 * c, 2 * c + 1):
                    if c == 0:
                        pe.wait_ge(emptied, pool_w.blocks_(0, g))
                    for h in range(2):
                        o = ps[:, 2 * g + h]
                        for k in range(2):
                            wt, act = spl[:, pool_w.slot_of(c) % SPL, 2 * (g % 2) + k], PS[:, 2 * g + k]
                            part = slice(h * P, (h + 1) * P)
                            if k:
                                nc.tensor.matmul(o[:, T:], wt[:, 1, part], act[:, 0], start=False, stop=False)
                            m = nc.tensor.matmul(o, wt[:, 0, part], flat(act), start=k == 0, stop=k == 1)
                            if not k:
                                nc.tensor.matmul(o[:, T:], wt[:, 1, part], act[:, 0], start=False, stop=False)
                m.then_inc(used, 1)

            def moba_heads(i, c):
                if i == 1 and c == 0:
                    pe.wait_ge(pool_done, 4)
                if i > 0:
                    moba_before(i - 1, c)

            stream(moba_qk, [COLS, COLS], HAc, moba_heads, heads=True)
            ys = [YC, YB, YA]

            def last_heads(c):
                moba_before(3, c)
                if c == 16:
                    pe.wait_ge(head_free, 2 + 3 * HEADS)

            stream(merge, [COLS] * 6, lambda b, k: HA[:, k] if b % 2 == 0 else ys[b // 2][:, k], ahead=last_heads)
            stream(out_2, [TOKS, TOKS], lambda b, k: MM[:, k], ahead=lambda c: pe.wait_ge(mg_done, 2 * c + 2) if c < 4 else None)
            stream(up2, [COLS, COLS], HAc, ahead=lambda c: turn_norm(5, c))
            stream(down2, [TOKS, TOKS], FFc, ahead=hidden_ready(2))

        @block.scalar
        def _(act):
            def round_unit(ph, i, c):
                s = ph.slot_of(c)
                act.wait_ge(loaded[s], ph.loaded(i, c))
                act.wait_ge(used, SPL + ph.before(i, c, SPL))
                nc.scalar.activation(spl[:, s % SPL, :, 0], raw[:, s], ACT.Copy).then_inc(hi_done, 1)

            def stream(ph, after=None, carried=None):
                def body(i, first):
                    for c in range(ph.n):
                        round_unit(ph, i, c)
                        if first and carried:
                            carried(c)
                        if after:
                            after(i, c, first)
                body(0, True)
                if ph.iters > 1:
                    with act.Fori(1, ph.iters) as i:
                        body(i, False)

            def norm_act(n, src, dst, scaled=True):
                s = norm
                nc.scalar.activation(dst[:, 0], src[:, 0], ACT.Square, accum_out=st[:, 4 * n:4 * n + 1]).then_inc(s["sq"], 1)
                act.wait_ge(s["var"], n + 1)
                nc.scalar.activation(st[:, 4 * n + 2:4 * n + 4], st[:, 4 * n:4 * n + 2], ACT.Sqrt).then_inc(s["root"], 1)
                if not scaled:
                    return
                act.wait_ge(s["rstd"], n + 1)
                for half in (slice(0, D // 2), slice(D // 2, D)):
                    nc.scalar.activation(dst[:, 0, half], src[:, 0, half], ACT.Copy, scale=st[:, 4 * n:4 * n + 1]).then_inc(s["scaled_a"], 1)

            def turn_act(n, qs=range(8)):
                s, name = norm, NORMS[n][2]
                for q in qs:
                    act.wait_ge(s["turned"], 8 * TURN[n] + q + 1)
                    for c in range(2):
                        m = nc.scalar.activation(HA[:, 2 * q + c, 0], ps[:, 4 + q % 4, c * T:(c + 1) * T], ACT.Copy, scale=v(name, 2 * q + c))
                    m.then_inc(s["round"], 1)

            def softmax_exp(n, j, buf, maps):
                act.wait_ge(logits, n + 1)
                for a in range(2):
                    sl = slice(0, P) if a == 0 else slice(P, 3 * P)
                    for m in range(maps):
                        at_ = 32 + 16 * j + 2 * a + m
                        e = nc.scalar.activation(buf[:, m, sl], buf[:, m, sl], ACT.Exp, bias=st[:, at_:at_ + 1], accum_out=st[:, at_ + 4:at_ + 5])
                e.then_inc(exps, 1)

            def copy_turned(n, j, dst, bank, maps):
                act.wait_ge(probs_turned, n + 1)
                for m in range(maps):
                    cp = nc.scalar.activation(dst[:, m], ps[:, bank + m, 0:3 * P], ACT.Copy)
                cp.then_inc(probs_copied, 1)

            def head_round(n, j, dst, bank, ready=None, done=None):
                act.wait_ge(ready or head_out, n + 1)
                nc.scalar.activation(dst, ps[:, bank, 0:T], ACT.Copy).then_inc(done or head_hi, 1)

            def diff_after(i, c):
                for j in range(2):
                    h = 2 * i + j
                    if c == 2:
                        softmax_exp(h, j, LG[:, j], 2)
                    if c == 5 + j:
                        copy_turned(h, j, PT[:, j], 4 + 2 * j, 1)
                    if c == 7:
                        act.wait_ge(head_out, h + 1)
                        for a in range(2):
                            at_ = 64 + a * 8 + h
                            nc.scalar.activation(PT[:, j, 1, a * P:(a + 1) * P], ps[:, 5 + 2 * j, a * P:(a + 1) * P], ACT.Square, accum_out=st[:, ds(at_)])
                        nc.scalar.activation(OD[:, :, ds(h)].rearrange("p a h e -> p (a h) e"), ps[:, 5 + 2 * j, 0:T].rearrange("p (a e) -> p a e", a=2), ACT.Copy).then_inc(head_free, 1)

            def nsa_after(g, c, first):
                pair, c = c // 4, c % 4
                for j in range(2):
                    h = 4 * g + 2 * pair + j
                    if c == 1:
                        softmax_exp(HEADS + h, j, LG[:, j], 2)
                    if c == 2:
                        copy_turned(HEADS + h, j, PT[:, j], 4 + 2 * j, 2)
                    if c == 3:
                        head_round(HEADS + h, j, MIX[:, ds(8 + h), 0].rearrange("p a t -> p (a t)"), 4 + 2 * j)

            def moba_after(pair, c):
                for j in range(2):
                    h = 2 * pair + j
                    n = 2 * HEADS + h
                    if c == 4:
                        softmax_exp(n, j, LM[:, j:j + 1], 1)
                    if c == 6:
                        copy_turned(n, j, PM[:, j:j + 1], 5 + 2 * j, 1)
                    if c == 7:
                        head_round(n, j, YA[:, ds(h), 0].rearrange("p a t -> p (a t)"), 4 + 2 * j)

            def sb_after(i, c, first):
                for j in range(2):
                    h = 2 * i + j
                    z, e, sp_, a_ = (SZ[:, j, k] for k in range(4))
                    if c == 2:
                        act.wait_ge(sz["zm"], h + 1)
                        nc.scalar.activation(e, z, ACT.Abs)
                        act.drain()
                        nc.scalar.activation(e, e, ACT.Exp, scale=-1.0)
                        act.drain()
                        nc.scalar.activation(e, e, ACT.Ln, bias=1.0).then_inc(sz["ln"], 1)
                    if c == 4 + j:
                        act.wait_ge(sz["e"], h + 1)
                        nc.scalar.activation(a_, a_, ACT.Exp).then_inc(sz["a"], 1)
                    if c == 7:
                        head_round(h, j, YC[:, ds(h), 0].rearrange("p a t -> p (a t)"), 4 + 2 * j, sz["out"], sz["hi"])

            def ff1_after(i, c, first=False, tail=False):
                def tap(i, b):
                    act.wait_ge(ff_u, 2 * i + b + 1)
                    for t in range(2):
                        j = 2 * i + 44 * b + t
                        m = nc.scalar.activation(CV[:, t], U[:, t], ACT.Identity, bias=vdyn("conv_b", j), scale=vdyn("conv_w2", j))
                    m.then_inc(ff_c, 1)
                if not first:
                    if c == 0:
                        act.wait_ge(ff_conv, i)
                        nc.scalar.activation(GL, CV, ACT.Gelu_apprx_tanh).then_inc(ff_gelu, 1)
                    if c == 3:
                        tap(i - 1, 1)
                    if c == 5:
                        act.wait_ge(ff_h, i)
                        nc.scalar.activation(FF[:, ds(2 * (i - 1), 2), 0], HF, ACT.Copy).then_inc(ff_hi, 1)
                if not tail and c == 7:
                    tap(i, 0)

            def ff2_after(i, c, first=False, tail=False):
                if not first:
                    if c == 4:
                        act.wait_ge(ff_h, FB + i)
                        nc.scalar.activation(FF[:, ds(2 * (i - 1), 2), 0], HF, ACT.Copy).then_inc(ff_hi, 1)
                if not tail and c == 7:
                    act.wait_ge(ff_u, 2 * FB + i + 1)
                    nc.scalar.activation(GL, U, ACT.Silu).then_inc(ff_gelu, 1)

            def merge_after(i, c, first=False, tail=False):
                def gate(i, g):
                    act.wait_ge(mg_logit, 3 * i + g + 1)
                    nc.scalar.activation(GS, GT, ACT.Sigmoid).then_inc(mg_gate, 1)
                if not first:
                    if c == 1:
                        gate(i - 1, 2)
                    if c == 4:
                        act.wait_ge(mg_m, i)
                        nc.scalar.activation(MM[:, ds(2 * (i - 1), 2), 0], MA, ACT.Copy).then_inc(mg_hi, 1)
                if not tail:
                    if c == 7:
                        gate(i, 0)
                    if c == 13:
                        gate(i, 1)

            act.wait_ge(x_in, 16)
            norm_act(0, x0, xn0)
            act.wait_ge(lam_sums, 1)
            nc.scalar.activation(lsum[:, 2:4], lsum[:, 0:2], ACT.Exp).then_inc(lam_exps, 1)

            def first_turn(c):
                if c == 0:
                    act.wait_ge(vec_ready, 1)
                if c < 4:
                    turn_act(0, (2 * c, 2 * c + 1))
                if c == 3:
                    act.wait_ge(const_in, 16 * 9)
                    nc.scalar.activation(gws[:, :, 0], gw, ACT.Copy).then_inc(gw_hi, 1)
                if c == 7:
                    act.wait_ge(gate_sum, 1)
                    nc.scalar.activation(gates, gates, ACT.Sigmoid).then_inc(gate_ready, 1)

            def bias_after(i, c, first):
                if c == 3:
                    for q in range(4):
                        act.wait_ge(flipped[0], 4 * i + q + 1)
                        nc.scalar.activation(bias1[:, ds(8 * i + 2 * q, 2)].rearrange("p h t -> p (h t)"), ps[:, 4 + q],
                                             ACT.Copy).then_inc(bias_ready[0], 1)

            stream(diff_qk, None, first_turn)
            stream(diff_v, bias_after)
            stream(nsa_q, lambda i, c, first: diff_after(i, c))

            def last_diff(i, c, first):
                diff_after(3, c)
                if c == 6:
                    for b, (src, dst) in enumerate(((kblk, ksp), (vblk, vsp))):
                        act.wait_ge(blk_sum, b + 1)
                        nc.scalar.activation(dst[:, :, 0], src, ACT.Copy).then_inc(blk_hi, 1)

            stream(nsa_k, last_diff)

            def finish_diff(i, c, first):
                if c == 1:
                    act.wait_ge(dn["var"], 1)
                    nc.scalar.activation(st[:, 80:96], st[:, 64:80], ACT.Sqrt).then_inc(dn["root"], 1)
                if c == 6:
                    for q in range(4):
                        act.wait_ge(dn["turned"], q + 1)
                        nc.scalar.activation(MIX[:, 2 * q:2 * q + 2, 0], ps[:, 4 + q].rearrange("p (c t) -> p c t", c=2), ACT.Copy,
                                             scale=st[:, 96:97]).then_inc(dn["round"], 1)

            stream(squeeze, finish_diff)

            def compressed(i, c, first):
                if c == 2:
                    act.wait_ge(hid_sum, 2)
                    nc.scalar.activation(hid_rows[0:2 * NC], hid_rows[0:2 * NC], ACT.Gelu_apprx_tanh).then_inc(hid_gelu, 1)
                if c == 4:
                    act.wait_ge(hid_turned, 1)
                    nc.scalar.activation(hid.rearrange("p b k n -> p (b k n)"), ps[:, 7, 0:8 * NC], ACT.Copy).then_inc(hid_ready, 1)
                if c == 5:
                    act.wait_ge(cmp_psum, 1)
                    nc.scalar.activation(kcT, ps[:, 4, 0:2 * NC], ACT.Copy)
                    for j in range(4):
                        r = slice(32 * j, 32 * j + NC)
                        m = nc.scalar.activation(vcr[r].rearrange("p g e -> p (g e)"), ps[r, 5, 0:T], ACT.Copy)
                    m.then_inc(cmp_sb, 1)
                if c == 6:
                    act.wait_ge(cs_logit, 1)
                    nc.scalar.activation(cl, cl, ACT.Exp).then_inc(cs_exp, 1)

            def turned_copy(c):
                if c == 0:
                    act.wait_ge(cs_turned, 1)
                    nc.scalar.activation(PcT.rearrange("p g t -> p (g t)"), ps[:, 4], ACT.Copy).then_inc(cs_ready, 1)

            stream(nsa_v, compressed)
            stream(out_a, nsa_after, turned_copy)
            stream(out_b)

            def second_norm(n, y, x, xn, c):
                if c == 2:
                    act.wait_ge(y_ready[n // 2], 1)
                    norm_act(n, y, xn, scaled=False)
                    act.wait_ge(x_ready[n // 2], 1)
                    norm_act(n + 1, x, xn)
                    turn_act(n + 1)

            stream(up1, ff1_after, lambda c: second_norm(1, Y1, X1, xn1, c))
            stream(down1, None, lambda c: ff1_after(FB, c, tail=True))

            def bias2_after(c):
                if c == 5:
                    for q in range(4):
                        act.wait_ge(flipped[1], q + 1)
                        nc.scalar.activation(bias2[:, 2 * q:2 * q + 2].rearrange("p h t -> p (h t)"), ps[:, 4 + q], ACT.Copy).then_inc(bias_ready[1], 1)

            stream(sb_qk, None, lambda c: second_norm(3, Yd, X2, xn2, c))
            stream(sb_v, None, bias2_after)
            stream(pool_u, sb_after)
            act.wait_ge(spilled[1], 16)

            def pool_round(*groups):
                for g in groups:
                    act.wait_ge(pooled, g + 1)
                    nc.scalar.activation(PS[:, 2 * g:2 * g + 2, 0], PQ[:, g], ACT.Copy).then_inc(pool_hi, 1)

            def moba_v_after(i, c, first):
                sb_after(i + 2, c, first)
                if first and c == 7:
                    pool_round(0, 1)
                if not first and c in (3, 6):
                    pool_round(2 if c == 3 else 3)

            stream(moba_v, moba_v_after)
            stream(pool_w)

            def proj_round(c):
                if 1 <= c <= 4:
                    g = c - 1
                    act.wait_ge(proj_sum, g + 1)
                    for t in range(2):
                        m = nc.scalar.activation(YB[:, 2 * g + t, 0], PQ[:, g, t], ACT.Copy, scale=v("pool_scale_2", 2 * g + t))
                    m.then_inc(proj_hi, 1)

            stream(moba_qk, lambda i, c, first: None if first else moba_after(i - 1, c), proj_round)
            stream(merge, merge_after, lambda c: moba_after(3, c))
            stream(out_2, None, lambda c: merge_after(8, c, tail=True))

            def third_norm(c):
                if c == 2:
                    act.wait_ge(x_ready[2], 1)
                    norm_act(5, X3, xn3)
                    turn_act(5)

            stream(up2, ff2_after, third_norm)
            stream(down2, None, lambda c: ff2_after(FB, c, tail=True))
            act.wait_ge(y_ready[2], 1)
            norm_act(6, Xd, fin, scaled=False)

        @block.vector
        def _(dve):
            def split_unit(ph, i, c):
                s = ph.slot_of(c)
                dve.wait_ge(hi_done, ph.units(i, c))
                nc.vector.tensor_tensor(spl[:, s % SPL, :, 1], raw[:, s], spl[:, s % SPL, :, 0].bitcast(F32),
                                        ALU.subtract).then_inc(split, 1)

            def empty(ph, i, b, dst, n=NB):
                dve.wait_ge(used, SPL + ph.units(i, sum(ph.blocks[:b + 1]) - 1))
                src = ps[:, 2 * (b % 2):2 * (b % 2) + 2, 0:2 * n].rearrange("p h (a n) -> p h n a", a=2)
                nc.vector.tensor_reduce(dst, src, AX.X, ALU.add).then_inc(emptied, 1)

            def stream(ph, emptyb=None, after=None, carried=None, steps=None):
                def body(i, first):
                    for c in range(ph.n):
                        split_unit(ph, i, c)
                        if first and carried:
                            carried(c)
                        for e, b, is_late in ph.ends():
                            if emptyb and c == e and not is_late:
                                emptyb(i, b)
                            if emptyb and c == e and is_late and not first:
                                emptyb(i - 1, b)
                        if after:
                            after(i, c)
                        if steps:
                            steps(i, c, first)
                body(0, True)
                if ph.iters > 1:
                    with dve.Fori(1, ph.iters) as i:
                        body(i, False)

            def late(ph, emptyb):
                def carried(c):
                    for e, b, is_late in ph.ends():
                        if is_late and c == e:
                            emptyb(ph.iters - 1, b)
                return carried

            def finish(ph, emptyb):
                for e, b, is_late in ph.ends():
                    if is_late:
                        emptyb(ph.iters - 1, b)

            def tiles(ph, dst):
                return lambda i, b: empty(ph, i, b, dst[:, ds(ph.nb * 2 * i + 2 * b, 2)])

            def columns(ph, dst):
                return lambda i, b: empty(ph, i, b, dst[:, :, ds(NB * (ph.nb * i + b), NB)])

            def norm_dve(n, src, dst):
                s, q = norm, 4 * n
                nc.vector.tensor_tensor_reduce(out=dst[:, 1], in0=src[:, 1], in1=src[:, 1], scale=1.0, scalar=0.0,
                                               op0=ALU.mult, op1=ALU.add, accum_out=st[:, q + 1:q + 2])
                dve.wait_ge(s["sq"], n + 1)
                dve.drain()
                nc.vector.tensor_scalar(st[:, q:q + 2], st[:, q:q + 2], 1.0 / D, EPS, ALU.mult, ALU.add).then_inc(s["var"], 1)
                dve.wait_ge(s["root"], n + 1)
                nc.vector.reciprocal(st[:, q:q + 2], st[:, q + 2:q + 4]).then_inc(s["rstd"], 1)
                dve.drain()

            def scale_dve(n, src, dst):
                for half in (slice(0, D // 2), slice(D // 2, D)):
                    nc.vector.tensor_scalar(dst[:, 1, half], src[:, 1, half], st[:, 4 * n + 1:4 * n + 2], None, ALU.mult).then_inc(norm["scaled_d"], 1)

            def turn_dve(n, qs=range(8)):
                s, name = norm, NORMS[n][2]
                for q in qs:
                    dve.wait_ge(s["round"], 8 * TURN[n] + q + 1)
                    for c in range(2):
                        k = 2 * q + c
                        m = nc.vector.scalar_tensor_tensor(HA[:, k, 1], ps[:, 4 + q % 4, c * T:(c + 1) * T], v(name, k),
                                                           HA[:, k, 0].bitcast(F32), ALU.mult, ALU.subtract)
                    m.then_inc(s["done"], 1)

            def add_normed(n, y, x, gain, tmp, dst):
                for a in range(2):
                    nc.vector.scalar_tensor_tensor(tmp[:, a], y[:, a], st[:, 4 * n + a:4 * n + a + 1], gain, ALU.mult, ALU.mult)
                dve.drain()
                return nc.vector.tensor_tensor(dst, tmp, x, ALU.add)

            TILE = [slice(0, P), slice(P, 3 * P)]

            def softmax_logits(n, j, bank, maps, buf, scale, bias, h):
                dve.wait_ge(scores, n + 1)
                for a in range(2):
                    w_ = P * (a + 1)
                    bt = bias[:, ds(h), T - w_:T].to_broadcast([P, maps, w_]) if maps > 1 else bias[:, ds(h), T - w_:T]
                    nc.vector.scalar_tensor_tensor(buf[:, 0:maps, TILE[a]], ps[:, bank:bank + maps, TILE[a]], scale, bt, ALU.mult, ALU.add)
                dve.drain()
                for a in range(2):
                    at_ = 32 + 16 * j + 2 * a
                    m = nc.vector.tensor_reduce(st[:, at_:at_ + maps], buf[:, 0:maps, TILE[a]], AX.X, ALU.max, negate=True)
                m.then_inc(logits, 1)

            def softmax_sums(n, j, maps, guard=True):
                dve.wait_ge(exps, n + 1)
                sv = st[:, 36 + 16 * j:40 + 16 * j].rearrange("p (a m) -> p a m", m=2)[:, :, 0:maps]
                r = st[:, 40 + 16 * j:44 + 16 * j].rearrange("p (a m) -> p a m", m=2)[:, :, 0:maps]
                if guard:
                    nc.vector.tensor_scalar(sv, sv, TINY, None, ALU.max)
                    dve.drain()
                nc.vector.reciprocal(r, sv)
                dve.drain()
                return r

            def scale_probs(buf, r, maps):
                for a in range(2):
                    for m in range(maps):
                        t = nc.vector.tensor_scalar(buf[:, m, TILE[a]], buf[:, m, TILE[a]], r[:, a, m:m + 1], None, ALU.mult)
                return t

            def diff_after(i, c):
                if c != 2:
                    return
                for j in range(2):
                    softmax_logits(2 * i + j, j, 4 + 2 * j, 2, LG[:, j], 64 ** -0.5, bias1, 2 * i + j)
                for j in range(2):
                    r = softmax_sums(2 * i + j, j, 2)
                    nc.vector.tensor_scalar(r[:, :, 1], r[:, :, 1], neg_lam, None, ALU.mult)
                    dve.drain()
                    for a in range(2):
                        nc.vector.tensor_scalar(LG[:, j, 1, TILE[a]], LG[:, j, 1, TILE[a]], r[:, a, 1:2], None, ALU.mult)
                    dve.drain()
                    for a in range(2):
                        m = nc.vector.scalar_tensor_tensor(LG[:, j, 0, TILE[a]], LG[:, j, 0, TILE[a]], r[:, a, 0:1], LG[:, j, 1, TILE[a]],
                                                           ALU.mult, ALU.add)
                    m.then_inc(probs, 1)

            def head_split(n, j, dst):
                dve.wait_ge(head_hi, n - HEADS + 1)
                nc.vector.tensor_tensor(dst[1], ps[:, 4 + 2 * j, 0:T], dst[0].bitcast(F32), ALU.subtract).then_inc(head_free, 1)

            def parts(t, h):
                return [t[:, ds(h), k].rearrange("p a t -> p (a t)") for k in range(2)]

            def nsa_after(g, c):
                pair, c = c // 4, c % 4
                hs = [4 * g + 2 * pair + j for j in range(2)]
                if c == 1:
                    for j, h in enumerate(hs):
                        softmax_logits(HEADS + h, j, 4 + 2 * j, 2, LG[:, j], 128 ** -0.5, bias1, 8 + h)
                    for j, h in enumerate(hs):
                        r = softmax_sums(HEADS + h, j, 2)
                        nc.vector.tensor_tensor(r, r, gates[:, :, ds(3 * h + 1, 2)], ALU.mult)
                        dve.drain()
                        scale_probs(LG[:, j], r, 2).then_inc(probs, 1)
                if c == 3:
                    for j, h in enumerate(hs):
                        head_split(HEADS + h, j, parts(MIX, 8 + h))

            def moba_after(pair, c):
                hs = [2 * pair + j for j in range(2)]
                if c == 4:
                    for j, h in enumerate(hs):
                        softmax_logits(2 * HEADS + h, j, 4 + 2 * j, 1, LM[:, j:j + 1], 128 ** -0.5, bias2, h)
                    for j, h in enumerate(hs):
                        r = softmax_sums(2 * HEADS + h, j, 1, guard=False)
                        scale_probs(LM[:, j:j + 1], r, 1).then_inc(probs, 1)
                if c == 7:
                    for j, h in enumerate(hs):
                        head_split(2 * HEADS + h, j, parts(YA, h))

            def sb_after(i, c):
                for j in range(2):
                    h = 2 * i + j
                    if c == 2:
                        dve.wait_ge(sz["z"], h + 1)
                        nc.vector.scalar_tensor_tensor(SZ[:, j, 0], ps[:, 4 + 2 * j, 0:3 * P], 128 ** -0.5, k1[:, SBMASK:SBMASK + 3 * P],
                                                       ALU.mult, ALU.add).then_inc(sz["zm"], 1)
                for j in range(2):
                    h = 2 * i + j
                    if c == 2:
                        dve.wait_ge(sz["ln"], h + 1)
                        nc.vector.scalar_tensor_tensor(SZ[:, j, 2], SZ[:, j, 0], 0.0, SZ[:, j, 1], ALU.max, ALU.add).then_inc(sz["sp"], 1)
                    if c == 4 + j:
                        dve.wait_ge(sz["aft"], h + 1)
                        nc.vector.tensor_tensor(SZ[:, j, 3], SZ[:, j, 0], ps[:, 5 + 2 * j, 0:3 * P], ALU.add).then_inc(sz["e"], 1)
                    if c == 7:
                        dve.wait_ge(sz["hi"], h + 1)
                        d = parts(YC, h)
                        nc.vector.tensor_tensor(d[1], ps[:, 4 + 2 * j, 0:T], d[0].bitcast(F32), ALU.subtract).then_inc(sz["free"], 1)

            def split_hidden(n, i):
                dve.wait_ge(ff_hi, n + 1)
                nc.vector.tensor_tensor(FF[:, ds(2 * i, 2), 1], HF, FF[:, ds(2 * i, 2), 0].bitcast(F32), ALU.subtract).then_inc(ff_done, 1)

            def empty_u(ph, i, b):
                dve.drain()
                empty(ph, i, b, U)
                dve.drain()
                dve.sem_inc(ff_u, 1)

            def ff1_after(i, c, first=False, tail=False):
                def taps(i, b):
                    dve.wait_ge(ff_c, 2 * i + b + 1)
                    for back in (1, 2):
                        for t in range(2):
                            cw = vdyn(f"conv_w{2 - back}", 2 * i + 44 * b + t)
                            m = nc.vector.scalar_tensor_tensor(CV[:, t, back:], U[:, t, 0:T - back], cw, CV[:, t, back:], ALU.mult, ALU.add)
                        if back == 1:
                            dve.drain()
                    return m
                if not first:
                    if c == 2:
                        empty_u(up1, i - 1, 1)
                    if c == 3:
                        taps(i - 1, 1)
                    if c == 4:
                        dve.drain()
                        dve.wait_ge(ff_gelu, i)
                        nc.vector.tensor_tensor(HF, GL, CV, ALU.mult).then_inc(ff_h, 1)
                    if c == 6:
                        split_hidden(i - 1, i - 1)
                if not tail:
                    if c == 6:
                        empty_u(up1, i, 0)
                    if c == 7:
                        taps(i, 0).then_inc(ff_conv, 1)

            def ff2_after(i, c, first=False, tail=False):
                if not first:
                    if c == 2:
                        dve.drain()
                        empty(up2, i - 1, 1, CV)
                    if c == 3:
                        dve.drain()
                        dve.wait_ge(ff_gelu, FB + i)
                        nc.vector.tensor_tensor(HF, GL, CV, ALU.mult).then_inc(ff_h, 1)
                    if c == 5:
                        split_hidden(FB + i - 1, i - 1)
                if not tail and c == 6:
                    empty_u(up2, i, 0)

            nc.vector.sem_inc(split, RAW)
            nc.vector.sem_inc(emptied, 2)
            nc.vector.sem_inc(head_free, 2)
            nc.vector.sem_inc(sz["free"], 2)
            dve.wait_ge(x_in, 16)
            norm_dve(0, x0, xn0)
            scale_dve(0, x0, xn0)
            dve.wait_ge(const_in, 16 * 9)
            lv = lamv.rearrange("p (a b) n -> p a b n", b=2)
            nc.vector.tensor_tensor(lamp, lv[:, :, 0], lv[:, :, 1], ALU.mult)
            dve.drain()
            nc.vector.tensor_reduce(lsum[:, 0:2], lamp, AX.X, ALU.add).then_inc(lam_sums, 1)
            dve.wait_ge(lam_exps, 1)
            nc.vector.scalar_tensor_tensor(neg_lam, lsum[:, 3:4], -LAM_INIT, lsum[:, 2:3], ALU.add, ALU.subtract)
            dve.wait_ge(vec_turned, 1)
            nc.vector.tensor_copy(vec, ps[:, 0, 0:NVEC])
            dve.drain()
            nc.vector.tensor_scalar(st[:, 96:97], v("diff_subln"), 1.0 - LAM_INIT, None, ALU.mult).then_inc(vec_ready, 1)
            dve.wait_ge(table_psum, 1)
            nc.vector.tensor_copy(rbias[0:16, 0, 0:T], ps[0:16, 2, 0:T])
            nc.vector.tensor_copy(rbias[0:8, 1, 0:T], ps[0:8, 3, 0:T])
            nc.vector.memset(rbias[0:16, :, T:384], NEG).then_inc(table_sb, 1)

            def first_turn(c):
                if c < 4:
                    turn_dve(0, (2 * c, 2 * c + 1))
                if c == 3:
                    dve.wait_ge(gw_hi, 1)
                    nc.vector.tensor_tensor(gws[:, :, 1], gw, gws[:, :, 0].bitcast(F32), ALU.subtract).then_inc(gw_split, 1)
                if c == 7:
                    dve.wait_ge(gate_psum, 1)
                    nc.vector.tensor_reduce(gates, ps[:, 4:6, 0:48].rearrange("p h (a n) -> p h n a", a=2), AX.X, ALU.add).then_inc(gate_sum, 1)

            e_qk, e_v, e_q = tiles(diff_qk, QK), columns(diff_v, DV), tiles(nsa_q, NQ)
            stream(diff_qk, e_qk, carried=first_turn)
            stream(diff_v, e_v, carried=late(diff_qk, e_qk))
            dve.wait_ge(bias_ready[0], 12)
            dve.wait_ge(gate_ready, 1)
            stream(nsa_q, e_q, diff_after, late(diff_v, e_v))
            e_k = lambda i, b: empty(nsa_k, i, b, NKs[:, 2 * b:2 * b + 2])
            e_nv = lambda i, b: empty(nsa_v, i, b, NVs[:, :, b])

            def last_diff(i, c):
                diff_after(3, c)
                if c == 4:
                    dve.drain()
                    for b, (dst, name) in enumerate(((kblk, "cmp_pos_k"), (vblk, "cmp_pos_v"))):
                        pos = v(name, 0, 32).unsqueeze(2).to_broadcast([P, 32, NC])
                        for g in range(2):
                            src = NQ[:, 8 + 2 * b + g]
                            win = bass.AP(src.tensor, src.offset, [src.ap[0], [1, 32], [16, NC]])
                            m = nc.vector.tensor_tensor(dst[:, :, g * NC:(g + 1) * NC], win, pos, ALU.add)
                        m.then_inc(blk_sum, 1)
                if c == 7:
                    for b, (src, dst) in enumerate(((kblk, ksp), (vblk, vsp))):
                        dve.wait_ge(blk_hi, b + 1)
                        nc.vector.tensor_tensor(dst[:, :, 1], src, dst[:, :, 0].bitcast(F32), ALU.subtract).then_inc(blk_split, 1)

            stream(nsa_k, e_k, last_diff, late(nsa_q, e_q))

            def between(i, c):
                if c == 0:
                    dve.wait_ge(head_free, 2 + HEADS)
                    nc.vector.tensor_scalar(st[:, 64:80], st[:, 64:80], 1.0 / P, EPS, ALU.mult, ALU.add).then_inc(dn["var"], 1)
                if c == 1:
                    dve.wait_ge(dn["root"], 1)
                    nc.vector.reciprocal(st[:, 64:80], st[:, 80:96])
                    dve.drain()
                    od = OD.rearrange("p a h e -> p (a h) e")
                    nc.vector.tensor_tensor(od, od, st[:, 64:80].unsqueeze(2).to_broadcast([P, 16, P]), ALU.mult).then_inc(dn["scaled"], 1)
                if c == 6:
                    for q in range(4):
                        dve.wait_ge(dn["round"], q + 1)
                        nc.vector.scalar_tensor_tensor(MIX[:, 2 * q:2 * q + 2, 1], ps[:, 4 + q].rearrange("p (c t) -> p c t", c=2),
                                                       st[:, 96:97], MIX[:, 2 * q:2 * q + 2, 0].bitcast(F32), ALU.mult,
                                                       ALU.subtract).then_inc(dn["done"], 1)

            def e_sq(i, b):
                dve.wait_ge(used, SPL + squeeze.units(0, 8 * b + 7))
                nc.vector.tensor_reduce(hid_rows[0:2 * NC, b], ps[0:2 * NC, 2 * b].rearrange("p (a n) -> p n a", a=2), AX.X, ALU.add).then_inc(emptied, 1)
                dve.drain()
                dve.sem_inc(hid_sum, 1)

            stream(squeeze, e_sq, between, late(nsa_k, e_k))
            ah = cl.rearrange("p a h c -> p (a h) c")
            cm = st[:, 100:116]
            cmb = cm.unsqueeze(2).to_broadcast([P, 16, NC])

            def compressed(i, c):
                if c == 6:
                    dve.wait_ge(w2_in, 48)
                    dve.wait_ge(cs_psum, 1)
                    for a in range(2):
                        nc.vector.scalar_tensor_tensor(cl[:, a], ps[:, 6 + a, 0:HEADS * NC].rearrange("p (h c) -> p h c", c=NC), 128 ** -0.5,
                                                       cmk[:, a:a + 1].to_broadcast([P, HEADS, NC]), ALU.mult, ALU.add)
                    dve.drain()
                    nc.vector.tensor_reduce(cm, ah, AX.X, ALU.max)
                    dve.drain()
                    nc.vector.tensor_tensor(ah, ah, cmb, ALU.subtract).then_inc(cs_logit, 1)
                if c == 7:
                    dve.wait_ge(cs_exp, 1)
                    for a in range(2):
                        nc.vector.tensor_tensor(cl[:, a], cl[:, a], cmk[:, 2 + a:3 + a].to_broadcast([P, HEADS, NC]), ALU.mult)
                    nc.vector.memset(PC, 0.0)
                    dve.drain()
                    nc.vector.tensor_reduce(cm, ah, AX.X, ALU.add)
                    dve.drain()
                    nc.vector.tensor_scalar(cm, cm, TINY, None, ALU.max)
                    dve.drain()
                    nc.vector.reciprocal(cm, cm)
                    dve.drain()
                    cm2 = cm.rearrange("p (a h) -> p a h", a=2)
                    nc.vector.tensor_tensor(cm2, cm2, gates.rearrange("p a (h c) -> p a h c", c=3)[:, :, :, 0], ALU.mult)
                    dve.drain()
                    nc.vector.tensor_tensor(PC.rearrange("p a h c -> p (a h) c")[:, :, 0:NC], ah, cmb, ALU.mult).then_inc(cs_prob, 1)

            stream(nsa_v, e_nv, compressed, late(squeeze, e_sq))
            e_oa = columns(out_a, Y1)

            def e_ob(i, b):
                empty(out_b, i, b, ya_tmp[:, b % 2])
                dve.drain()
                y = Y1[:, :, ds(NB * (4 * i + b), NB)]
                nc.vector.tensor_tensor(y, y, ya_tmp[:, b % 2], ALU.add)

            stream(out_a, e_oa, nsa_after, late(nsa_v, e_nv))
            dve.drain()
            dve.sem_inc(nsa_done, 1)
            stream(out_b, e_ob, carried=late(out_a, e_oa))

            def second_norm(n, ph, e, y, x, xn, c, gain, dst):
                late(ph, e)(c)
                if c == 2:
                    dve.drain()
                    dve.sem_inc(y_ready[n // 2], 1)
                    norm_dve(n, y, xn)
                    dve.wait_ge(x_reloaded[n // 2], 16)
                    dve.wait_ge(gain_in[n // 2], 16)
                    add_normed(n, y, x, gain, xn, dst).then_inc(x_ready[n // 2], 1)
                    dve.drain()
                    norm_dve(n + 1, dst, xn)
                    scale_dve(n + 1, dst, xn)
                    turn_dve(n + 1)

            def up1_carried(c):
                second_norm(1, out_b, e_ob, Y1, X1, xn1, c, gain1, X1)
                if c == 4:
                    dve.wait_ge(spilled[0], 16)

            stream(up1, carried=up1_carried, steps=ff1_after)
            e_d1 = columns(down1, Yd)
            stream(down1, e_d1, carried=lambda c: ff1_after(FB, c, tail=True))
            e_sqk, e_sv = tiles(sb_qk, SQK), columns(sb_v, SV)
            e_pu, e_mv = tiles(pool_u, UP), columns(moba_v, MV)
            stream(sb_qk, e_sqk, carried=lambda c: second_norm(3, down1, e_d1, Yd, Xd, xn2, c, gain2, X2))
            stream(sb_v, e_sv, carried=late(sb_qk, e_sqk))
            stream(pool_u, e_pu, sb_after, late(sb_v, e_sv))
            dve.wait_ge(bias_ready[1], 4)

            def pool_los(*groups):
                for g in groups:
                    dve.wait_ge(pool_hi, g + 1)
                    nc.vector.tensor_tensor(PS[:, 2 * g:2 * g + 2, 1], PQ[:, g], PS[:, 2 * g:2 * g + 2, 0].bitcast(F32),
                                            ALU.subtract).then_inc(pool_split, 1)

            def moba_v_after(i, c, first):
                sb_after(i + 2, c)
                if not first and c == 0:
                    pool_los(0, 1)
                if not first and c in (3, 7):
                    pool_los(2 if c == 3 else 3)

            stream(moba_v, e_mv, carried=late(pool_u, e_pu), steps=moba_v_after)
            stream(pool_w)

            def project(c):
                if c == 0:
                    late(moba_v, e_mv)(2)
                if c < 4:
                    dve.wait_ge(used, SPL + pool_w.units(0, c // 2))
                    m = nc.vector.tensor_reduce(PQ[:, c], ps[:, 2 * c:2 * c + 2].rearrange("p h (a n) -> p h n a", a=2), AX.X, ALU.add)
                    if c < 2:
                        m.then_inc(emptied, 1)
                    dve.drain()
                    dve.sem_inc(proj_sum, 1)
                if 2 <= c < 6:
                    g = c - 2
                    dve.wait_ge(proj_hi, g + 1)
                    for t in range(2):
                        m = nc.vector.scalar_tensor_tensor(YB[:, 2 * g + t, 1], PQ[:, g, t], v("pool_scale_2", 2 * g + t),
                                                           YB[:, 2 * g + t, 0].bitcast(F32), ALU.mult, ALU.subtract)
                    m.then_inc(pool_done, 1)

            def e_mqk(i, b):
                empty(moba_qk, i, b, MQK[:, ds(8 * b + 2 * i, 2)])

            stream(moba_qk, e_mqk, carried=project, steps=lambda i, c, first: None if first else moba_after(i - 1, c))

            def last_heads(c):
                late(moba_qk, e_mqk)(c)
                moba_after(3, c)

            def merge_after(i, c, first=False, tail=False):
                def logits_(i, g):
                    dve.drain()
                    empty(merge, i, 2 * g, GT)
                    dve.drain()
                    dve.sem_inc(mg_logit, 1)

                def gated(i, g):
                    dve.drain()
                    empty(merge, i, 2 * g + 1, BR)
                    dve.drain()
                    dve.wait_ge(mg_gate, 3 * i + g + 1)
                    nc.vector.tensor_tensor(BR if g else MA, BR, GS, ALU.mult)

                def add():
                    dve.drain()
                    return nc.vector.tensor_tensor(MA, MA, BR, ALU.add)

                if not first:
                    if c == 0:
                        logits_(i - 1, 2)
                    if c == 2:
                        gated(i - 1, 2)
                    if c == 3:
                        add().then_inc(mg_m, 1)
                    if c == 5:
                        dve.wait_ge(mg_hi, i)
                        nc.vector.tensor_tensor(MM[:, ds(2 * (i - 1), 2), 1], MA, MM[:, ds(2 * (i - 1), 2), 0].bitcast(F32),
                                                ALU.subtract).then_inc(mg_done, 1)
                if not tail:
                    if c == 6:
                        logits_(i, 0)
                    if c == 8:
                        gated(i, 0)
                    if c == 12:
                        logits_(i, 1)
                    if c == 14:
                        gated(i, 1)
                    if c == 15:
                        add()

            stream(merge, carried=last_heads, steps=merge_after)
            e_o2 = columns(out_2, Y3)
            stream(out_2, e_o2, carried=lambda c: merge_after(8, c, tail=True))

            def third_norm(c):
                late(out_2, e_o2)(c)
                if c == 2:
                    dve.drain()
                    dve.wait_ge(x_reloaded[2], 16)
                    nc.vector.tensor_tensor(X3, X3, Y3, ALU.add).then_inc(x_ready[2], 1)
                    dve.drain()
                    norm_dve(5, X3, xn3)
                    scale_dve(5, X3, xn3)
                    turn_dve(5)
                if c == 4:
                    dve.wait_ge(spilled[2], 16)

            stream(up2, carried=third_norm, steps=ff2_after)
            e_d2 = columns(down2, Yd)
            stream(down2, e_d2, carried=lambda c: ff2_after(FB, c, tail=True))
            finish(down2, e_d2)
            dve.drain()
            dve.wait_ge(x_reloaded[3], 16)
            dve.wait_ge(gain_in[2], 16)
            nc.vector.tensor_tensor(Xd, Xd, Yd, ALU.add).then_inc(y_ready[2], 1)
            dve.drain()
            norm_dve(6, Xd, fin)
            for a in range(2):
                nc.vector.scalar_tensor_tensor(fin[:, a], Xd[:, a], st[:, 24 + a:25 + a], gain2, ALU.mult, ALU.mult).then_inc(y_ready[3], 1)


_INS = ["x", "pre_mix_norm", "w_in", "lambda_q1", "lambda_k1", "lambda_q2", "lambda_k2", "diff_subln", "cmp_pos_k",
        "cmp_pos_v", "cmp_k_w1", "cmp_k_w2", "cmp_v_w1", "cmp_v_w2", "rel_bias", "w_out", "post_mix_norm",
        "pre_ffn_norm", "w_up", "conv_w", "conv_b", "w_down", "post_ffn_norm", "norm_mix_2", "norm_ffn_2", "w_in_2",
        "w_pool_2", "pool_scale_2", "w_br_a_2", "w_br_b_2", "w_br_c_2", "w_out_2", "w_gate_2", "w_up_2", "w_down_2",
        "rel_bias_2", "norm_final_2"]


def kernel(**inputs):
    import concourse.bacc as bacc
    from concourse.bass_utils import run_bass_kernel_spmd

    nc = bacc.Bacc("TRN2", target_bir_lowering=False, num_devices=1)
    arrays, w = {}, {}
    for name in _INS + ["consts"]:
        a = np.ascontiguousarray(shape_constants() if name == "consts" else inputs[name])
        arrays[f"in_{name}_dram"] = a
        w[name] = nc.dram_tensor(f"in_{name}_dram", a.shape, mybir.dt.from_np(a.dtype), kind="ExternalInput").ap()
    out = nc.dram_tensor("out_0_dram", (1, T, D), F32, kind="ExternalOutput").ap()
    two_blocks(nc, w, out)
    r = run_bass_kernel_spmd(nc, [arrays], core_ids=[0])
    return r.results[0]["out_0_dram"]
```

```python
import math
from contextlib import ExitStack

import numpy as np

import concourse.bass as bass
from concourse import mybir

F32 = mybir.dt.float32
F32R = mybir.dt.float32r
ACT = mybir.ActivationFunctionType
ALU = mybir.AluOpType
AX = mybir.AxisListType

P = 128
T = 256
D = 2048
NK = D // P
F = 5632
NF = F // P
NB = 256
FB = F // NB
KC = 4
RAW = 8
SPL = 4
HEADS = 8
NC = (T - 32) // 16 + 1
NEG = -1e30
TINY = 1e-30
EPS = 1e-6
LAM_INIT = 0.8 - 0.6 * math.exp(0.0)
COLS, TOKS = 0, 1
LAG = 3
KB = 1024

IDENT, FLIP, LOWER, ONES, SBMASK, CNT, CNEG, CONE, HOT1, HOT2 = np.cumsum([0, 128, 128, 128, 128, 384, 64, 2 * NC, 2 * NC, 256]).tolist()
NCONST = HOT2 + 256

VECS = [("pre_mix_norm", 16), ("pre_ffn_norm", 16), ("norm_mix_2", 16), ("norm_ffn_2", 16), ("pool_scale_2", 8),
        ("diff_subln", 1), ("conv_b", 88), ("conv_w0", 88), ("conv_w1", 88), ("conv_w2", 88), ("cmp_pos_k", 32), ("cmp_pos_v", 32)]
VEC_TILES = [[0, 1, 2, 3, 4, 5], [6], [7], [8], [9], [10, 11]]
VAT = dict(zip([n for n, _ in VECS], np.cumsum([0] + [n for _, n in VECS]).tolist()))
NVEC = sum(n for _, n in VECS)


def shape_constants():
    c = np.zeros((P, NCONST), np.float32)
    r = np.arange(P)
    c[r, IDENT + r] = 1
    c[r, FLIP + P - 1 - r] = 1
    c[:, LOWER:LOWER + P] = -(r[:, None] >= r[None, :]).astype(np.float32)
    c[:, ONES:ONES + P] = -1
    strict = np.where(r[:, None] < r[None, :], 0, NEG)
    c[:, SBMASK:SBMASK + P] = strict
    c[:, SBMASK + 2 * P:SBMASK + 3 * P] = strict
    for g in range(4):
        c[:, CNT + 16 * g:CNT + 16 * (g + 1)] = 1.0 / np.minimum(np.arange(16) + 1, 2 << g)
    for a in range(2):
        ok = (np.arange(NC) * 16 + 31)[None, :] <= (r + a * P)[:, None]
        c[:, CNEG + a * NC:CNEG + (a + 1) * NC] = np.where(ok, 0, NEG)
        c[:, CONE + a * NC:CONE + (a + 1) * NC] = ok
    for at, far in ((HOT1, 128), (HOT2, 2048)):
        d = T - 1 - np.arange(T)
        large = 16 + (np.log(np.maximum(d, 1) / 16) / math.log(far / 16) * 16).astype(np.int32)
        bucket = np.where(d < 16, d, np.minimum(large, 31))
        c[bucket, at + np.arange(T)] = 1
    return c


class Phase:

    unit = block = slot = 0
    loads = [0] * RAW

    @classmethod
    def reset(cls):
        cls.unit = cls.block = cls.slot = 0
        cls.loads = [0] * RAW

    def __init__(self, iters, blocks):
        self.iters, self.blocks = iters, blocks
        self.n = sum(blocks)
        self.nb = len(blocks)
        self.u0, self.b0, self.rot = Phase.unit, Phase.block, Phase.slot
        self.loads0 = list(Phase.loads)
        Phase.unit += iters * self.n
        Phase.block += iters * self.nb
        Phase.slot = (self.rot + self.n) % RAW
        self.per = [sum(self.slot_of(c) == s for c in range(self.n)) for s in range(RAW)]
        Phase.loads = [a + iters * b for a, b in zip(Phase.loads, self.per)]

    def slot_of(self, c):
        return (self.rot + c) % RAW

    def units(self, i, c):
        return self.u0 + i * self.n + c + 1

    def blocks_(self, i, b):
        return self.b0 + i * self.nb + b + 1

    def before(self, i, c, ring):
        if c >= ring or self.iters == 1:
            prev = c - ring
        else:
            prev = c + (self.n - 1 - c) // ring * ring - self.n
        return self.units(i, prev)

    def loaded(self, i, c):
        s = self.slot_of(c)
        nth = sum(self.slot_of(x) == s for x in range(c + 1))
        return 16 * (self.loads0[s] + i * self.per[s] + nth)

    def where(self, c):
        for b, k in enumerate(self.blocks):
            if c < k:
                return b, c
            c -= k

    def ends(self):
        out, e = [], -1
        for b, k in enumerate(self.blocks):
            e += k
            out.append(((e + LAG) % self.n if self.n > LAG else 0, b, e + LAG >= self.n))
        return out


def two_blocks(nc, w, out):
    Phase.reset()
    diff_qk = Phase(4, [4, 4])
    diff_v = Phase(2, [4, 4])
    nsa_q = Phase(3, [4, 4])
    nsa_k = Phase(1, [4, 4])
    squeeze = Phase(1, [8, 8])
    nsa_v = Phase(1, [4, 4])
    out_a = Phase(2, [2, 2, 2, 2])
    out_b = Phase(2, [2, 2, 2, 2])
    up1 = Phase(FB, [4, 4])
    down1 = Phase(2, [11, 11, 11, 11])
    sb_qk = Phase(4, [4, 4])
    sb_v = Phase(2, [4, 4])
    pool_u = Phase(2, [4, 4])
    moba_v = Phase(2, [4, 4])
    pool_w = Phase(1, [1, 1])
    moba_qk = Phase(4, [4, 4])
    merge = Phase(4, 2 * [4, 2, 4, 2, 4, 2])
    out_2 = Phase(4, [4, 4])
    up2 = Phase(FB, [4, 4])
    down2 = Phase(2, [11, 11, 11, 11])

    with ExitStack() as ctx:
        def sem(name):
            return ctx.enter_context(nc.semaphore(name))

        BASE = (nc.sbuf_base + 31) // 32 * 32
        at = [BASE]

        def fixed(name, shape, dt=F32):
            t = nc.alloc_sbuf_tensor_at(name, shape, dt, offset=at[0])
            at[0] += (int(np.prod(shape[1:])) * 4 + 31) // 32 * 32
            return t.ap() if hasattr(t, "ap") and callable(t.ap) else t

        raw = fixed("raw", [P, RAW, KC, NB])
        spl = fixed("spl", [P, SPL, KC, 2, NB], F32R)
        HA0 = at[0]
        HA = fixed("HA", [P, NK, 2, T], F32R)
        k1 = fixed("k1", [P, CNEG])
        vec = fixed("vec", [P, NVEC])
        st = fixed("st", [P, 128])
        gates = fixed("gates", [P, 2, 24])
        neg_lam = fixed("neg_lam", [P, 1])
        lsum = fixed("lsum", [P, 4])
        sums = fixed("sums", [P, 2, 8])
        sums2 = fixed("sums2", [P, 2, 2])
        G0 = at[0]

        def inG(name, kb, shape, dt=F32, base=G0):
            t = nc.alloc_sbuf_tensor_at(name, shape, dt, offset=int(base + kb * KB))
            assert base != G0 or kb * KB + int(np.prod(shape[1:])) * 4 <= 104 * KB, name
            return t.ap() if hasattr(t, "ap") and callable(t.ap) else t

        def inH(name, kb, shape, dt=F32):
            assert kb * KB + int(np.prod(shape[1:])) * 4 <= 32 * KB, name
            return inG(name, kb, shape, dt, HA0)

        x0 = inG("x0", 0, [P, 2, D])
        xn0 = inG("xn0", 16, [P, 2, D])
        rows = inG("rows", 32, [P, 6, P])
        k2 = inG("k2", 36, [P, NCONST - CNEG])
        tab1 = inG("tab1", 42, [P, 16])
        tab2 = inG("tab2", 42.25, [P, 8])
        rbias = inG("rbias", 42.5, [P, 2, 384])
        lamv = inG("lamv", 46, [P, 4, 64])
        lamp = inG("lamp", 47, [P, 2, 64])
        gw = inG("gw", 48, [P, NK, 24])
        gws = inG("gws", 50, [P, NK, 2, 24], F32R)
        gsum = inG("gsum", 53, [P, T])
        hank1 = inG("hank1", 54, [P, 16, T])
        QK = inG("QK", 0, [P, 16, T])
        DV = inG("DV", 16, [P, 2, 1024])
        NQ = inG("NQ", 24, [P, 12, T])
        NKs = inG("NKs", 36, [P, 4, T])
        NVs = inG("NVs", 40, [P, 2, 2, T])
        MIX = inG("MIX", 44, [P, NK, 2, T], F32R)
        OD = inG("OD", 60, [P, 2, HEADS, P])
        bias1 = inG("bias1", 76, [P, 16, T])
        LG = inG("LG", 92, [P, 2, 2, 384])
        PT = inG("PT", 98, [P, 2, 2, 384])
        kblk = inG("kblk", 68, [P, 32, 2 * NC])
        vblk = inG("vblk", 72, [P, 32, 2 * NC])
        ksp = inG("ksp", 0, [P, 32, 2, 2 * NC], F32R)
        vsp = inG("vsp", 8, [P, 32, 2, 2 * NC], F32R)
        PC = inG("PC", 16, [P, 2, HEADS, 32])
        PcT = inG("PcT", 18, [P, 2, T])
        vcr = inG("vcr", 20, [P, 2, P])
        kcT = inG("kcT", 21, [P, 2 * NC])
        hid_rows = inG("hid_rows", 21.25, [P, 2, NB])
        w2 = inG("w2", 32, [P, 2, 2, P])
        hid = inG("hid", 34, [P, 2, 2, 2 * NC])
        cmk = inG("cmk", 34.5, [P, 4, NC])
        cl = inG("cl", 34.75, [P, 2, HEADS, NC])
        Y1 = inG("Y1", 0, [P, 2, D])
        gain1 = inG("gain1", 32, [P, D])
        X1 = inG("X1", 88, [P, 2, D])
        xn1 = inG("xn1", 16, [P, 2, D])
        tmp1 = inG("tmp1", 40, [P, 2, 2, NB])
        FF = inG("FF", 0, [P, NF, 2, T], F32R)
        U = inG("U", 88, [P, 2, T])
        CV = inG("CV", 90, [P, 2, T])
        GL = inG("GL", 92, [P, 2, T])
        HF = inG("HF", 94, [P, 2, T])
        tmp2 = inG("tmp2", 88, [P, 2, 2, NB])
        junk = inG("junk", 92, [P, 2, NB])
        Yd = inH("Yd", 0, [P, 2, D])
        Xd = inH("Xd", 16, [P, 2, D])
        gain2 = inG("gain2", 96, [P, D])
        X2 = inG("X2", 48, [P, 2, D])
        xn2 = inG("xn2", 64, [P, 2, D])
        hank2 = inG("hank2", 88, [P, 8, T])
        SQK = inG("SQK", 0, [P, 16, T])
        SV = inG("SV", 16, [P, 2, 1024])
        UP = inG("UP", 24, [P, 8, T])
        PQ = inG("PQ", 32, [P, 4, 2, T])
        PD = inG("PD", 100, [P, 2, T])
        PS = inG("PS", 48, [P, 8, 2, T], F32R)
        MQK = inG("MQK", 16, [P, 16, T])
        MV = inG("MV", 40, [P, 2, 1024])
        YA = inG("YA", 48, [P, 8, 2, T], F32R)
        YC = inG("YC", 64, [P, 8, 2, T], F32R)
        bias2 = inG("bias2", 80, [P, 8, T])
        SZ = inG("SZ", 88, [P, 2, 4, 384])
        LM = inG("LM", 96, [P, 2, 384])
        PM = inG("PM", 99, [P, 2, 384])
        YB = inG("YB", 0, [P, 8, 2, T], F32R)
        MM = inG("MM", 16, [P, NK, 2, T], F32R)
        GT = inG("GT", 88, [P, 2, T])
        GS = inG("GS", 90, [P, 2, T])
        BR = inG("BR", 92, [P, 2, T])
        MA = inG("MA", 94, [P, 2, T])
        junk3 = inG("junk3", 48, [P, 2, NB])
        X3 = inG("X3", 64, [P, 2, D])
        xn3 = inG("xn3", 0, [P, 2, D])

        ps = ctx.enter_context(nc.psum_tensor("ps", [P, 8, 512], F32))
        table = nc.dram_tensor("table", [24, 384], F32, kind="Internal").ap()
        spill = nc.dram_tensor("spill", [3, T, D], F32, kind="Internal").ap()

        loaded = [sem(f"loaded{s}") for s in range(RAW)]
        hi_done = sem("hi_done")
        split = sem("split")
        used = sem("used")
        emptied = sem("emptied")

        x_in = [sem(f"x_in{a}") for a in range(2)]
        ident_in = sem("ident_in")
        warm_set = sem("warm_set")
        first_in = sem("first_in")
        const_in = sem("const_in")
        vec_in = sem("vec_in")
        vec_turned = sem("vec_turned")
        vec_ready = sem("vec_ready")
        lam_sums = sem("lam_sums")
        lam_exps = sem("lam_exps")
        gw_hi = sem("gw_hi")
        gw_split = sem("gw_split")
        gate_psum = sem("gate_psum")
        gate_part = sem("gate_part")
        gate_sum = sem("gate_sum")
        gate_ready = sem("gate_ready")
        table_psum = sem("table_psum")
        table_sb = sem("table_sb")
        table_out = sem("table_out")
        hank_in = [sem(f"hank_in{b}") for b in range(2)]
        flipped = [sem(f"flipped{b}") for b in range(2)]
        bias_ready = [sem(f"bias_ready{b}") for b in range(2)]
        NORM = ["sq", "var", "root", "rstd", "scaled_a", "scaled_d", "turned", "round", "done"]
        norm = {s: sem(f"norm_{s}") for s in NORM}
        x_reloaded = [sem(f"x_reloaded{n}") for n in range(4)]
        gain_in = [sem(f"gain_in{n}") for n in range(3)]
        spilled = [sem(f"spilled{n}") for n in range(3)]
        x_ready = [sem(f"x_ready{n}") for n in range(3)]
        part_in = sem("part_in")
        part_sq = sem("part_sq")
        result_a = sem("result_a")
        result_d = sem("result_d")
        scores = sem("scores")
        logits = sem("logits")
        exps = sem("exps")
        probs = sem("probs")
        probs_turned = sem("probs_turned")
        probs_copied = sem("probs_copied")
        head_out = sem("head_out")
        head_hi = sem("head_hi")
        head_free = sem("head_free")
        dn = {s: sem(f"dn_{s}") for s in ("var", "root", "scaled", "turned", "round", "done")}
        w2_in = sem("w2_in")
        blk_sum = sem("blk_sum")
        blk_hi = sem("blk_hi")
        blk_split = sem("blk_split")
        hid_sum = sem("hid_sum")
        hid_turned = sem("hid_turned")
        hid_gelu = sem("hid_gelu")
        hid_ready = sem("hid_ready")
        cmp_psum = sem("cmp_psum")
        cmp_sb = sem("cmp_sb")
        cs_psum = sem("cs_psum")
        cs_logit = sem("cs_logit")
        cs_exp = sem("cs_exp")
        cs_prob = sem("cs_prob")
        cs_turned = sem("cs_turned")
        cs_ready = sem("cs_ready")
        nsa_done = sem("nsa_done")
        ff_u = sem("ff_u")
        ff_c = sem("ff_c")
        ff_conv = sem("ff_conv")
        ff_gelu = sem("ff_gelu")
        ff_h = sem("ff_h")
        ff_hi = sem("ff_hi")
        ff_done = sem("ff_done")
        sz = {s: sem(f"sb_{s}") for s in ("z", "zm", "ln", "sp", "aft", "e", "a", "out", "hi", "free")}
        pooled = sem("pooled")
        pool_hi = sem("pool_hi")
        pool_split = sem("pool_split")
        proj_sum = sem("proj_sum")
        proj_hi = sem("proj_hi")
        pool_done = sem("pool_done")
        mg_logit = sem("mg_logit")
        mg_gate = sem("mg_gate")
        mg_m = sem("mg_m")
        mg_hi = sem("mg_hi")
        mg_done = sem("mg_done")
        stored = sem("stored")

        def chunks(name):
            return w[name][0].rearrange("(k p) n -> p k n", p=P)

        ident = k1[:, IDENT:IDENT + P]

        def ident_rows(n):
            return k1[0:n, IDENT:IDENT + n]

        def v(name, j=0, n=1):
            return vec[:, VAT[name] + j:VAT[name] + j + n]

        def vdyn(name, j):
            return vec[:, bass.ds(VAT[name] + j, 1)] if not isinstance(j, int) else v(name, j)

        def ds(a, n=1):
            return slice(a, a + n) if isinstance(a, int) else bass.ds(a, n)

        def flat(t):
            return t.rearrange("p a n -> p (a n)")

        NORMS = {0: (x0, xn0, "pre_mix_norm"), 2: (X1, xn1, "pre_ffn_norm"), 4: (X2, xn2, "norm_mix_2"), 5: (X3, xn3, "norm_ffn_2")}

        PIECES = {1: 0, 2: 8, 3: 12, 4: 20, 5: 24, 6: 32}
        HALF = [slice(0, D // 2), slice(D // 2, D)]
        QUARTER = [slice(D // 4 * k, D // 4 * (k + 1)) for k in range(4)]
        TURN = {0: 0, 2: 1, 4: 2, 5: 3}

        block = ctx.enter_context(nc.Block())

        @block.sync
        def _(sp):
            def load(ph, i, c, src):
                sp.wait_ge(split, RAW + ph.before(i, c, RAW))
                sp.dma_start(raw[:, ph.slot_of(c)], src).then_inc(loaded[ph.slot_of(c)], 16)

            def stream(ph, src):
                if ph.iters == 1:
                    for c in range(ph.n):
                        load(ph, 0, c, src(0, *ph.where(c)))
                else:
                    with sp.Fori(0, ph.iters) as i:
                        for c in range(ph.n):
                            load(ph, i, c, src(i, *ph.where(c)))

            def cols(name, block_of, k0=0):
                wv = chunks(name)
                return lambda i, b, k: wv[:, k0 + KC * k:k0 + KC * (k + 1), ds(NB * block_of(i, b), NB)]

            for a in range(2):
                sp.dma_start(x0[:, a], w["x"][0, a * P:(a + 1) * P, :]).then_inc(x_in[a], 16)
            sp.dma_start(k1[:, 0:LOWER], w["consts"][:, 0:LOWER]).then_inc(ident_in, 16)
            stream(diff_qk, cols("w_in", lambda i, b: 2 * i + b))
            stream(diff_v, cols("w_in", lambda i, b: 8 + 2 * i + b))
            stream(nsa_q, cols("w_in", lambda i, b: 12 + 2 * i + b))
            stream(nsa_k, cols("w_in", lambda i, b: 18 + 2 * b))
            squeezers = [chunks("cmp_k_w1"), chunks("cmp_v_w1")]
            stream(squeeze, lambda i, b, k: squeezers[b][:, KC * k:KC * (k + 1), :])
            stream(nsa_v, cols("w_in", lambda i, b: 19 + 2 * b))
            stream(out_a, cols("w_out", lambda i, b: 4 * i + b))
            stream(out_b, cols("w_out", lambda i, b: 4 * i + b, 8))
            stream(up1, cols("w_up", lambda i, b: i + FB * b))
            stream(down1, cols("w_down", lambda i, b: 4 * i + b))
            stream(sb_qk, cols("w_in_2", lambda i, b: 16 + 2 * i + b))
            stream(sb_v, cols("w_in_2", lambda i, b: 24 + 2 * i + b))
            stream(pool_u, cols("w_in_2", lambda i, b: 12 + 2 * i + b))
            stream(moba_v, cols("w_in_2", lambda i, b: 8 + 2 * i + b))
            wp = w["w_pool_2"][0].rearrange("(c g) (k p) n -> c p (g k) n", p=P, g=2)
            stream(pool_w, lambda i, b, k: wp[b])
            stream(moba_qk, cols("w_in_2", lambda i, b: i + 4 * b))
            gate = chunks("w_in_2")
            branch = [chunks(n) for n in ("w_br_a_2", "w_br_b_2", "w_br_c_2")]

            def merge_src(i, b, k):
                g, j = 2 - b % 6 // 2, 2 * i + b // 6
                if b % 2 == 0:
                    return gate[:, KC * k:KC * (k + 1), ds(NB * (28 + 8 * g + j), NB)]
                return branch[g][:, KC * k:KC * (k + 1), ds(NB * j, NB)]

            stream(merge, merge_src)
            stream(out_2, cols("w_out_2", lambda i, b: 2 * i + b))
            gu = [chunks("w_gate_2"), chunks("w_up_2")]
            stream(up2, lambda i, b, k: gu[b][:, KC * k:KC * (k + 1), ds(NB * i, NB)])
            stream(down2, cols("w_down_2", lambda i, b: 4 * i + b))
            oview = out[0].rearrange("(a p) d -> p a d", p=P)
            for half in range(2):
                for a, done in ((1, result_d), (0, result_a)):
                    sp.wait_ge(done, half + 1)
                    sp.dma_start(oview[:, a, HALF[half]], Yd[:, a, HALF[half]]).then_inc(stored, 16)
            sp.wait_ge(stored, 64)

        @block.gpsimd
        def _(pool):
            def rows_of(name, dst, src):
                pool.dma_start(dst, src).then_inc(vec_in, 16)

            r = 0
            for name, n in VECS[:6]:
                pool.dma_start(rows[r:r + n, 0, :], w[name][0].rearrange("(r p) -> r p", p=P)).then_inc(first_in, 16)
                r += n
            pool.dma_start(k1[:, LOWER:], w["consts"][:, LOWER:CNEG]).then_inc(const_in, 16)
            rows_of("conv_b", rows[0:88, 1, :], w["conv_b"][0].rearrange("(r p) -> r p", p=P))
            for j in range(3):
                rows_of("conv_w", rows[0:88, 2 + j, :], w["conv_w"][0, j].rearrange("(r p) -> r p", p=P))
            rows_of("pos", rows[0:32, 5, :], w["cmp_pos_k"][0])
            rows_of("pos", rows[32:64, 5, :], w["cmp_pos_v"][0])
            pool.dma_start(gw, chunks("w_in")[:, :, 5632:5656]).then_inc(const_in, 16)
            pool.dma_start(k2, w["consts"][:, CNEG:]).then_inc(const_in, 16)
            pool.dma_start(tab1[0:32, :], w["rel_bias"]).then_inc(const_in, 16)
            pool.dma_start(tab2[0:32, :], w["rel_bias_2"].rearrange("h b -> b h"), allow_slow_non_contiguous=True).then_inc(const_in, 16)
            for j, name in enumerate(("lambda_q1", "lambda_k1", "lambda_q2", "lambda_k2")):
                pool.dma_start(lamv[:, j, :], w[name].to_broadcast([P, 64])).then_inc(const_in, 16)

            pool.wait_ge(table_sb, 1)
            pool.dma_start(table[0:16], rbias[0:16, 0, :]).then_inc(table_out, 16)
            pool.dma_start(table[16:24], rbias[0:8, 1, :]).then_inc(table_out, 16)
            pool.wait_ge(table_out, 32)
            window = lambda h0, n: bass.AP(table.tensor, h0 * 384, [[1, P], [384, n], [1, T]])
            pool.dma_start(hank1, window(0, 16)).then_inc(hank_in[0], 16)

            pool.wait_ge(used, SPL + nsa_k.units(0, nsa_k.n - 1))
            for j, name in enumerate(("cmp_k_w2", "cmp_v_w2")):
                pool.dma_start(w2[:, j], w[name][0].rearrange("(k p) n -> p k n", p=P)).then_inc(w2_in, 16)
            cm = w["consts"][:, CNEG:CNEG + 4 * NC].rearrange("p (a c) -> p a c", c=NC)
            pool.dma_start(cmk, cm).then_inc(w2_in, 16)

            pool.wait_ge(nsa_done, 1)
            pool.dma_start(X1, w["x"][0].rearrange("(a p) d -> p a d", p=P)).then_inc(x_reloaded[0], 16)
            pool.dma_start(gain1, w["post_mix_norm"].to_broadcast([P, D])).then_inc(gain_in[0], 16)

            def keep(n, x):
                pool.wait_ge(x_ready[n], 1)
                pool.dma_start(spill[n].rearrange("(a p) d -> p a d", p=P), x).then_inc(spilled[n], 16)

            def reload(n, x, r):
                pool.dma_start(x, spill[n].rearrange("(a p) d -> p a d", p=P)).then_inc(x_reloaded[r], 16)

            keep(0, X1)
            pool.wait_ge(used, SPL + up1.units(FB - 1, up1.n - 1))
            pool.wait_ge(spilled[0], 16)
            reload(0, Xd, 1)
            pool.dma_start(gain2, w["post_ffn_norm"].to_broadcast([P, D])).then_inc(gain_in[1], 16)
            keep(1, X2)
            pool.dma_start(hank2, window(16, 8)).then_inc(hank_in[1], 16)
            for g in range(4):
                pool.wait_ge(emptied, 2 + pool_u.blocks_(g // 2, g % 2))
                src, q = UP[:, 2 * g:2 * g + 2], PQ[:, g]
                for n in range(g + 1):
                    dst, back = (PD, q)[(g - n) % 2], 1 << n
                    nc.gpsimd.tensor_copy(dst[:, :, 0:back], src[:, :, 0:back])
                    nc.gpsimd.tensor_tensor(dst[:, :, back:], src[:, :, back:], src[:, :, 0:T - back], ALU.add)
                    pool.drain()
                    src = dst
                cnt = k1[:, CNT + 16 * g:CNT + 16 * (g + 1)].unsqueeze(1).to_broadcast([P, 2, 16])
                nc.gpsimd.tensor_tensor(q[:, :, 0:16], src[:, :, 0:16], cnt, ALU.mult)
                nc.gpsimd.tensor_scalar(q[:, :, 16:], src[:, :, 16:], 1.0 / (2 << g), None, ALU.mult)
                pool.drain()
                nc.gpsimd.tensor_tensor(q, q, UP[:, 2 * g:2 * g + 2], ALU.subtract).then_inc(pooled, 1)
            pool.wait_ge(used, SPL + merge.units(3, merge.n - 1))
            pool.wait_ge(spilled[1], 16)
            reload(1, X3, 2)
            keep(2, X3)
            pool.wait_ge(used, SPL + up2.units(FB - 1, up2.n - 1))
            pool.wait_ge(spilled[2], 16)
            reload(2, Xd, 3)
            pool.dma_start(gain2, w["norm_final_2"].rearrange("(a d) -> a d", a=1).to_broadcast([P, D])).then_inc(gain_in[2], 16)
        @block.tensor
        def _(pe):
            def unit(ph, i, c, kinds, acts):
                b, k = ph.where(c)
                pe.wait_ge(split, RAW + ph.units(i, c))
                if k == 0:
                    pe.wait_ge(emptied, ph.blocks_(i, b))
                s = ph.slot_of(c) % SPL
                last_k = ph.blocks[b] * KC - 1
                for kk in range(KC):
                    act = acts(b, KC * k + kk)
                    wt = spl[:, s, kk]
                    n = act.shape[-1]
                    for h in range(2):
                        o = ps[:, 2 * (b % 2) + h]
                        first, last = KC * k + kk == 0, KC * k + kk == last_k
                        part = slice(h * P, (h + 1) * P)

                        def whole():
                            if kinds[b] == COLS:
                                return nc.tensor.matmul(o[:, 0:2 * n], wt[:, 0, part], flat(act), start=first, stop=last)
                            return nc.tensor.matmul(o, act[:, 0, part], flat(wt), start=first, stop=last)

                        def cross():
                            if kinds[b] == COLS:
                                return nc.tensor.matmul(o[:, n:2 * n], wt[:, 1, part], act[:, 0], start=False, stop=False)
                            return nc.tensor.matmul(o[:, NB:], act[:, 1, part], wt[:, 0], start=False, stop=False)

                        if first:
                            whole()
                            m = cross()
                        else:
                            cross()
                            m = whole()
                m.then_inc(used, 1)

            def stream(ph, kinds, acts, before=None, heads=False, ahead=None):
                peeled = ph.iters if heads else min(ph.iters, 1 if ahead or ph.iters == 1 else 0)
                for i in range(peeled):
                    for c in range(ph.n):
                        if ahead and i == 0:
                            ahead(c)
                        if before:
                            before(i, c)
                        unit(ph, i, c, kinds, acts)
                if peeled < ph.iters:
                    with pe.Fori(peeled, ph.iters) as i:
                        for c in range(ph.n):
                            if before:
                                before(i, c)
                            unit(ph, i, c, kinds, acts)

            def turn_norm(n, c):
                src, nth, s = NORMS[n][1], TURN[n], norm
                for q in {0: range(4), 1: range(4, 6), 2: range(6, 8)}.get(c, ()):
                    if q % 2 == 0:
                        pe.wait_ge(s["scaled_a"], 4 * nth + 1 + q // 2)
                        pe.wait_ge(s["scaled_d"], 4 * nth + 1 + q // 2)
                    if q >= 4:
                        pe.wait_ge(s["done"], 8 * nth + q - 3)
                    for k in range(2):
                        for a in range(2):
                            at_ = (k * 2 + a) * P
                            m = nc.tensor.transpose(ps[:, 4 + q % 4, at_:at_ + P], src[:, a, (2 * q + k) * P:(2 * q + k + 1) * P], ident)
                    m.then_inc(s["turned"], 1)
                if c < 4:
                    pe.wait_ge(s["done"], 8 * nth + 2 * c + 2)

            def head_scores(q, k, bank):
                S = ps[:, bank]
                nc.tensor.matmul(S[:, 0:P], q[:, 0:P], k[:, 0:P], start=True, stop=True)
                return nc.tensor.matmul(S[:, P:3 * P], q[:, P:T], k, start=True, stop=True)

            def turn(src, bank):
                for j in range(3):
                    m = nc.tensor.transpose(ps[:, bank, j * P:(j + 1) * P], src[:, j * P:(j + 1) * P], ident)
                return m

            def free_bank(h):
                pe.wait_ge(head_free, h + 1)

            def diff_scores(i, j):
                h = 2 * i + j
                free_bank(h)
                for m in range(2):
                    r = slice(64 * m, 64 * m + 64)
                    q = QK[r, ds(h)].rearrange("p a t -> p (a t)")
                    k = QK[r, ds(h + 8)].rearrange("p a t -> p (a t)")
                    last = head_scores(q, k, 4 + 2 * j + m)
                last.then_inc(scores, 1)

            def diff_turn(i, j):
                h = 2 * i + j
                pe.wait_ge(probs, h + 1)
                turn(LG[:, j, 0], 4 + 2 * j).then_inc(probs_turned, 1)

            def diff_out(i, j):
                h = 2 * i + j
                pe.wait_ge(probs_copied, h + 1)
                pe.wait_ge(emptied, 2 + diff_v.blocks_(1, 1))
                O = ps[:, 5 + 2 * j]
                vh = [DV[:, a, ds(P * h, P)] for a in range(2)]
                pt = PT[:, j, 0]
                nc.tensor.matmul(O[:, 0:P], pt[:, 0:P], vh[0], start=True, stop=True)
                nc.tensor.matmul(O[:, P:T], pt[:, P:T], vh[0], start=True, stop=False)
                nc.tensor.matmul(O[:, P:T], pt[:, T:3 * P], vh[1], start=False, stop=True).then_inc(head_out, 1)

            def diff_before(i, c):
                for j in range(2):
                    if c == 0:
                        diff_scores(i, j)
                    if c == 3 + j:
                        diff_turn(i, j)
                    if c == 5 + j:
                        diff_out(i, j)

            def diff_finish(c):
                if c == 3:
                    pe.wait_ge(dn["scaled"], 1)
                    for q in range(4):
                        for c_ in range(2):
                            for a in range(2):
                                at_ = (c_ * 2 + a) * P
                                m = nc.tensor.transpose(ps[:, 4 + q, at_:at_ + P], OD[:, a, 2 * q + c_], ident)
                        m.then_inc(dn["turned"], 1)

            def nsa_before(g, c):
                pair, c = c // 4, c % 4
                for j in range(2):
                    hg = 2 * pair + j
                    nh = 4 * g + hg
                    if c == 0:
                        free_bank(HEADS + nh)
                        q = NQ[:, ds(nh)].rearrange("p a t -> p (a t)")
                        for m in range(2):
                            k = NKs[:, ds(2 * m + g)].rearrange("p a t -> p (a t)")
                            last = head_scores(q, k, 4 + 2 * j + m)
                        last.then_inc(scores, 1)
                    if c == 2:
                        pe.wait_ge(probs, HEADS + nh + 1)
                        turn(LG[:, j, 0], 4 + 2 * j)
                        turn(LG[:, j, 1], 5 + 2 * j).then_inc(probs_turned, 1)
                    if c == 3:
                        pe.wait_ge(probs_copied, HEADS + nh + 1)
                        pe.wait_ge(emptied, nsa_v.blocks_(0, 1) + 2)
                        O = ps[:, 4 + 2 * j, 0:T]
                        for m in range(2):
                            for a in range(2):
                                vh = NVs[:, a, m, ds(P * g, P)]
                                o, pt = (O, PT[:, j, m, 0:T]) if a == 0 else (O[:, P:T], PT[:, j, m, T:3 * P])
                                nc.tensor.matmul(o, vh, pt, start=(m == 0 and a == 0), stop=False)
                        r = slice(32 * hg, 32 * hg + NC)
                        nc.tensor.matmul(O, vcr[r, ds(g)].rearrange("p a e -> p (a e)"), PcT[r, ds(g)].rearrange("p a t -> p (a t)"),
                                         start=False, stop=True).then_inc(head_out, 1)

            def sb_before(i, c):
                for j in range(2):
                    h = 2 * i + j
                    X, Yb = ps[:, 4 + 2 * j], ps[:, 5 + 2 * j]
                    if c == 0:
                        pe.wait_ge(sz["free"], h + 1)
                        q = SQK[:, ds(h)].rearrange("p a t -> p (a t)")
                        k = SQK[:, ds(h + 8)].rearrange("p a t -> p (a t)")
                        nc.tensor.matmul(X[:, 0:T], k[:, 0:P], q, start=True, stop=True)
                        nc.tensor.matmul(X[:, T:3 * P], k[:, P:T], q[:, P:T], start=True, stop=True).then_inc(sz["z"], 1)
                    if c == 3:
                        pe.wait_ge(sz["sp"], i + 1)
                        sp_ = SZ[:, j, 2]
                        low, one = k1[:, LOWER:LOWER + P], k1[:, ONES:ONES + P]
                        nc.tensor.matmul(Yb[:, 0:T], low, sp_[:, 0:T], start=True, stop=False)
                        nc.tensor.matmul(Yb[:, P:T], one, sp_[:, T:3 * P], start=False, stop=True)
                        nc.tensor.matmul(Yb[:, T:3 * P], low, sp_[:, T:3 * P], start=True, stop=True).then_inc(sz["aft"], 1)
                    if c == 5:
                        pe.wait_ge(sz["a"], i + 1)
                        pe.wait_ge(emptied, 2 + sb_v.blocks_(1, 1))
                        a_ = SZ[:, j, 3]
                        nc.tensor.matmul(X[:, 0:T], SV[:, 0, ds(P * h, P)], a_[:, 0:T], start=True, stop=False)
                        nc.tensor.matmul(X[:, P:T], SV[:, 1, ds(P * h, P)], a_[:, T:3 * P], start=False, stop=True).then_inc(sz["out"], 1)

            def moba_before(pair, c):
                for j in range(2):
                    h = 2 * pair + j
                    n = 2 * HEADS + h
                    X, Yb = 4 + 2 * j, 5 + 2 * j
                    if c == 1:
                        free_bank(n)
                        pe.wait_ge(emptied, 2 + moba_qk.blocks_(pair, 1))
                        q = MQK[:, ds(h)].rearrange("p a t -> p (a t)")
                        k = MQK[:, ds(h + 8)].rearrange("p a t -> p (a t)")
                        head_scores(q, k, X).then_inc(scores, 1)
                    if c == 3:
                        pe.wait_ge(probs, n + 1)
                        turn(LM[:, j], Yb).then_inc(probs_turned, 1)
                    if c == 5:
                        pe.wait_ge(probs_copied, n + 1)
                        O = ps[:, X]
                        nc.tensor.matmul(O[:, 0:T], MV[:, 0, ds(P * h, P)], PM[:, j, 0:T], start=True, stop=False)
                        nc.tensor.matmul(O[:, P:T], MV[:, 1, ds(P * h, P)], PM[:, j, T:3 * P], start=False, stop=True).then_inc(head_out, 1)

            nc.tensor.sem_inc(used, SPL)
            nc.tensor.sem_inc(bias_ready[0], 4)

            def turn_vectors(tiles_, bank):
                for j in tiles_:
                    n = sum(VECS[m][1] for m in VEC_TILES[j])
                    a = VAT[VECS[VEC_TILES[j][0]][0]]
                    m = nc.tensor.transpose(ps[:, bank, a:a + n], rows[0:n, j], ident_rows(n))
                m.then_inc(vec_turned, 1)

            pe.wait_ge(ident_in, 16)
            pe.wait_ge(first_in, 16 * 6)
            turn_vectors((0,), 0)

            def gate_logits(c):
                turn_norm(0, c)
                if c == 7:
                    pe.wait_ge(gate_part, 1)
                    for a in range(2):
                        m = nc.tensor.transpose(ps[:, 5, 48 * a:48 * (a + 1)], gsum[0:48, a * P:(a + 1) * P], ident_rows(48))
                    m.then_inc(gate_psum, 1)
                if c != 4:
                    return
                pe.wait_ge(const_in, 16 * 9)
                pe.wait_ge(vec_in, 16 * 6)
                turn_vectors(range(1, 6), 6)
                nc.tensor.matmul(ps[0:16, 7, 0:T], tab1[0:32], k2[0:32, HOT1 - CNEG:HOT1 - CNEG + T], start=True, stop=True)
                nc.tensor.matmul(ps[0:8, 7, T:2 * T], tab2[0:32], k2[0:32, HOT2 - CNEG:HOT2 - CNEG + T], start=True,
                                 stop=True).then_inc(table_psum, 1)
                pe.wait_ge(gw_split, 1)
                for k in range(NK):
                    m = nc.tensor.matmul(ps[0:48, 4], flat(gws[:, k]), flat(HA[:, k]), start=k == 0, stop=k == NK - 1)
                m.then_inc(gate_psum, 1)

            HAc = lambda b, k: HA[:, k]
            stream(diff_qk, [COLS, COLS], HAc, ahead=gate_logits)
            pe.wait_ge(gate_sum, 1)
            pe.wait_ge(table_sb, 1)
            pe.wait_ge(hank_in[0], 16)

            def bias_before(i, c):
                if c == 0:
                    pe.wait_ge(bias_ready[0], 4 * i + 4)
                    for q in range(4):
                        nc.tensor.matmul(ps[:, 4 + q], k1[:, FLIP:FLIP + P], hank1[:, ds(8 * i + 2 * q, 2)].rearrange("p h t -> p (h t)"),
                                         start=True, stop=True).then_inc(flipped[0], 1)

            stream(diff_v, [TOKS, TOKS], HAc, bias_before)
            pe.wait_ge(bias_ready[0], 12)
            stream(nsa_q, [COLS, COLS], HAc, diff_before, heads=True)
            stream(nsa_k, [COLS, COLS], HAc, lambda i, c: diff_before(3, c))
            pe.wait_ge(blk_split, 2)
            for c in range(squeeze.n):
                diff_finish(c)
                b, k = squeeze.where(c)
                pe.wait_ge(split, RAW + squeeze.units(0, c))
                if k == 0:
                    pe.wait_ge(emptied, squeeze.blocks_(0, b))
                o = ps[0:2 * NC, 2 * b]
                for kk in range(KC):
                    wt, act = spl[:, squeeze.slot_of(c) % SPL, kk], (ksp, vsp)[b][:, KC * k + kk]
                    first, last = KC * k + kk == 0, KC * k + kk == 31
                    if not first:
                        nc.tensor.matmul(o[:, NB:], act[:, 1], wt[:, 0], start=False, stop=False)
                    m = nc.tensor.matmul(o, act[:, 0], flat(wt), start=first, stop=last)
                    if first:
                        nc.tensor.matmul(o[:, NB:], act[:, 1], wt[:, 0], start=False, stop=False)
                m.then_inc(used, 1)

            def compressed(c):
                if c == 1:
                    pe.wait_ge(hid_gelu, 1)
                    pe.wait_ge(dn["done"], 4)
                    for b in range(2):
                        for k in range(2):
                            at_ = (2 * b + k) * 2 * NC
                            m = nc.tensor.transpose(ps[:, 7, at_:at_ + 2 * NC], hid_rows[0:2 * NC, b, k * P:(k + 1) * P], ident_rows(2 * NC))
                    m.then_inc(hid_turned, 1)
                if c == 2:
                    pe.wait_ge(hid_ready, 1)
                    pe.wait_ge(w2_in, 48)
                    for k in range(2):
                        nc.tensor.matmul(ps[:, 4, 0:2 * NC], w2[:, 0, k], hid[:, 0, k], start=k == 0, stop=k == 1)
                    for j in range(4):
                        for g in range(2):
                            for k in range(2):
                                m = nc.tensor.matmul(ps[32 * j:32 * j + NC, 5, g * P:(g + 1) * P], hid[:, 1, k, g * NC:(g + 1) * NC],
                                                     w2[:, 1, k], start=k == 0, stop=k == 1)
                    m.then_inc(cmp_psum, 1)
                if c == 3:
                    pe.wait_ge(cmp_sb, 1)
                    for a in range(2):
                        for h in range(HEADS):
                            m = nc.tensor.matmul(ps[:, 6 + a, h * NC:(h + 1) * NC], NQ[:, h, a * P:(a + 1) * P],
                                                 kcT[:, (h // 4) * NC:(h // 4 + 1) * NC], start=True, stop=True)
                    m.then_inc(cs_psum, 1)
                if c == 7:
                    pe.wait_ge(cs_prob, 1)
                    for g in range(2):
                        for a in range(2):
                            m = nc.tensor.transpose(ps[:, 4, (g * 2 + a) * P:(g * 2 + a + 1) * P],
                                                    PC[:, a, 4 * g:4 * g + 4].rearrange("p h c -> p (h c)"), ident)
                    m.then_inc(cs_turned, 1)

            stream(nsa_v, [TOKS, TOKS], HAc, lambda i, c: compressed(c))
            pe.wait_ge(cs_ready, 1)
            MIXc = lambda b, k: MIX[:, k]
            stream(out_a, [TOKS] * 4, MIXc, nsa_before, heads=True)
            pe.wait_ge(head_free, 2 + 2 * HEADS)
            stream(out_b, [TOKS] * 4, lambda b, k: MIX[:, 8 + k])
            stream(up1, [COLS, COLS], HAc, ahead=lambda c: turn_norm(2, c))

            def hidden_ready(n):
                def ahead(c):
                    if c == 0:
                        pe.wait_ge(ff_done, n * FB - 1)
                    if c == 10:
                        pe.wait_ge(ff_done, n * FB)
                return ahead

            FFc = lambda b, k: FF[:, k]
            stream(down1, [TOKS] * 4, FFc, ahead=hidden_ready(1))
            stream(sb_qk, [COLS, COLS], HAc, ahead=lambda c: turn_norm(4, c))
            pe.wait_ge(hank_in[1], 16)
            for q in range(4):
                nc.tensor.matmul(ps[:, 4 + q], k1[:, FLIP:FLIP + P], hank2[:, 2 * q:2 * q + 2].rearrange("p h t -> p (h t)"),
                                 start=True, stop=True).then_inc(flipped[1], 1)
            stream(sb_v, [TOKS, TOKS], HAc)
            pe.wait_ge(bias_ready[1], 4)
            stream(pool_u, [COLS, COLS], HAc, sb_before, heads=True)
            stream(moba_v, [TOKS, TOKS], HAc, lambda i, c: sb_before(i + 2, c), heads=True)
            pe.wait_ge(sz["free"], 2 + HEADS)
            for c in range(2):
                pe.wait_ge(split, RAW + pool_w.units(0, c))
                pe.wait_ge(pool_split, 2 * c + 2)
                for g in (2 * c, 2 * c + 1):
                    if c == 0:
                        pe.wait_ge(emptied, pool_w.blocks_(0, g))
                    for h in range(2):
                        o = ps[:, 2 * g + h]
                        for k in range(2):
                            wt, act = spl[:, pool_w.slot_of(c) % SPL, 2 * (g % 2) + k], PS[:, 2 * g + k]
                            part = slice(h * P, (h + 1) * P)
                            if k:
                                nc.tensor.matmul(o[:, T:], wt[:, 1, part], act[:, 0], start=False, stop=False)
                            m = nc.tensor.matmul(o, wt[:, 0, part], flat(act), start=k == 0, stop=k == 1)
                            if not k:
                                nc.tensor.matmul(o[:, T:], wt[:, 1, part], act[:, 0], start=False, stop=False)
                m.then_inc(used, 1)

            def moba_heads(i, c):
                if i == 1 and c == 0:
                    pe.wait_ge(pool_done, 4)
                if i > 0:
                    moba_before(i - 1, c)

            stream(moba_qk, [COLS, COLS], HAc, moba_heads, heads=True)
            ys = [YC, YB, YA]

            def last_heads(c):
                moba_before(3, c)
                if c == 16:
                    pe.wait_ge(head_free, 2 + 3 * HEADS)

            stream(merge, [COLS] * 12, lambda b, k: HA[:, k] if b % 2 == 0 else ys[b % 6 // 2][:, k], ahead=last_heads)
            stream(out_2, [TOKS, TOKS], lambda b, k: MM[:, k], ahead=lambda c: pe.wait_ge(mg_done, 2 * c + 2) if c < 4 else None)
            stream(up2, [COLS, COLS], HAc, ahead=lambda c: turn_norm(5, c))
            stream(down2, [TOKS] * 4, FFc, ahead=hidden_ready(2))

        @block.scalar
        def _(act):
            def round_unit(ph, i, c):
                s = ph.slot_of(c)
                act.wait_ge(loaded[s], ph.loaded(i, c))
                act.wait_ge(used, SPL + ph.before(i, c, SPL))
                nc.scalar.activation(spl[:, s % SPL, :, 0], raw[:, s], ACT.Copy).then_inc(hi_done, 1)

            def stream(ph, after=None, carried=None):
                def body(i, first):
                    for c in range(ph.n):
                        round_unit(ph, i, c)
                        if first and carried:
                            carried(c)
                        if after:
                            after(i, c, first)
                body(0, True)
                if ph.iters > 1:
                    with act.Fori(1, ph.iters) as i:
                        body(i, False)

            def root(n):
                act.wait_ge(norm["var"], n + 1)
                nc.scalar.activation(st[:, 4 * n + 2:4 * n + 4], st[:, 4 * n:4 * n + 2], ACT.Sqrt).then_inc(norm["root"], 1)

            def scale_act(n, src, dst):
                act.wait_ge(norm["rstd"], n + 1)
                for part in QUARTER:
                    nc.scalar.activation(dst[:, 0, part], src[:, 0, part], ACT.Copy, scale=st[:, 4 * n:4 * n + 1]).then_inc(norm["scaled_a"], 1)

            def warm(n):
                nc.scalar.activation(st[:, 120 + n:121 + n], ident[:, 0:1], ACT.Sqrt)

            def square(n, m, src, dst):
                act.drain()
                act.wait_ge(part_in, PIECES[n] + m + 1)
                for a in range(2):
                    e = nc.scalar.activation(dst[:, a], src[:, a], ACT.Square, accum_out=sums[:, a, ds(m)])
                e.then_inc(part_sq, 1)

            def squares(n, ph, src, dst):
                def after(i, c, first):
                    for e, b, is_late in ph.ends():
                        if c == e + 1 and not is_late:
                            square(n, ph.nb * i + b, src(i, b), dst)
                        if c == e + 1 and is_late and not first:
                            square(n, ph.nb * (i - 1) + b, src(i - 1, b), dst)
                return after

            def last_squares(n, ph, src, dst, c):
                for e, b, is_late in ph.ends():
                    if is_late and c == min(e + 1, 2):
                        square(n, ph.nb * (ph.iters - 1) + b, src(ph.iters - 1, b), dst)

            def squares_of_halves(n, src, dst):
                for k in range(2):
                    for a in range(2):
                        act.wait_ge(part_in, PIECES[n] + 2 * k + a + 1)
                        nc.scalar.activation(dst[:, a, HALF[k]], src[:, a, HALF[k]], ACT.Square, accum_out=sums2[:, a, k:k + 1]).then_inc(part_sq, 1)

            def turn_act(n, qs=range(8)):
                s, name = norm, NORMS[n][2]
                for q in qs:
                    act.wait_ge(s["turned"], 8 * TURN[n] + q + 1)
                    for c in range(2):
                        m = nc.scalar.activation(HA[:, 2 * q + c, 0], ps[:, 4 + q % 4, c * T:(c + 1) * T], ACT.Copy, scale=v(name, 2 * q + c))
                    m.then_inc(s["round"], 1)

            def softmax_exp(n, j, buf, maps):
                act.wait_ge(logits, n + 1)
                for a in range(2):
                    sl = slice(0, P) if a == 0 else slice(P, 3 * P)
                    for m in range(maps):
                        at_ = 32 + 16 * j + 2 * a + m
                        e = nc.scalar.activation(buf[:, m, sl], buf[:, m, sl], ACT.Exp, bias=st[:, at_:at_ + 1], accum_out=st[:, at_ + 4:at_ + 5])
                e.then_inc(exps, 1)

            def copy_turned(n, j, dst, bank, maps):
                act.wait_ge(probs_turned, n + 1)
                for m in range(maps):
                    cp = nc.scalar.activation(dst[:, m], ps[:, bank + m, 0:3 * P], ACT.Copy)
                cp.then_inc(probs_copied, 1)

            def head_round(n, j, dst, bank, ready=None, done=None):
                act.wait_ge(ready or head_out, n + 1)
                nc.scalar.activation(dst, ps[:, bank, 0:T], ACT.Copy).then_inc(done or head_hi, 1)

            def diff_after(i, c):
                for j in range(2):
                    h = 2 * i + j
                    if c == 2:
                        softmax_exp(h, j, LG[:, j], 2)
                    if c == 5 + j:
                        copy_turned(h, j, PT[:, j], 4 + 2 * j, 1)
                    if c == 7:
                        act.wait_ge(head_out, h + 1)
                        for a in range(2):
                            at_ = 64 + a * 8 + h
                            nc.scalar.activation(PT[:, j, 1, a * P:(a + 1) * P], ps[:, 5 + 2 * j, a * P:(a + 1) * P], ACT.Square, accum_out=st[:, ds(at_)])
                        nc.scalar.activation(OD[:, :, ds(h)].rearrange("p a h e -> p (a h) e"), ps[:, 5 + 2 * j, 0:T].rearrange("p (a e) -> p a e", a=2), ACT.Copy).then_inc(head_free, 1)

            def nsa_after(g, c, first):
                pair, c = c // 4, c % 4
                for j in range(2):
                    h = 4 * g + 2 * pair + j
                    if c == 1:
                        softmax_exp(HEADS + h, j, LG[:, j], 2)
                    if c == 2:
                        copy_turned(HEADS + h, j, PT[:, j], 4 + 2 * j, 2)
                    if c == 3:
                        head_round(HEADS + h, j, MIX[:, ds(8 + h), 0].rearrange("p a t -> p (a t)"), 4 + 2 * j)

            def moba_after(pair, c):
                for j in range(2):
                    h = 2 * pair + j
                    n = 2 * HEADS + h
                    if c == 4:
                        softmax_exp(n, j, LM[:, j:j + 1], 1)
                    if c == 6:
                        copy_turned(n, j, PM[:, j:j + 1], 5 + 2 * j, 1)
                    if c == 7:
                        head_round(n, j, YA[:, ds(h), 0].rearrange("p a t -> p (a t)"), 4 + 2 * j)

            def sb_after(i, c, first):
                z, e, a_ = (SZ[:, :, k] for k in (0, 1, 3))
                if c == 2:
                    act.wait_ge(sz["zm"], i + 1)
                    nc.scalar.activation(e, z, ACT.Abs)
                    act.drain()
                    nc.scalar.activation(e, e, ACT.Exp, scale=-1.0)
                    act.drain()
                    nc.scalar.activation(e, e, ACT.Ln, bias=1.0).then_inc(sz["ln"], 1)
                if c == 4:
                    act.wait_ge(sz["e"], i + 1)
                    nc.scalar.activation(a_, a_, ACT.Exp).then_inc(sz["a"], 1)
                if c == 7:
                    for j in range(2):
                        h = 2 * i + j
                        head_round(h, j, YC[:, ds(h), 0].rearrange("p a t -> p (a t)"), 4 + 2 * j, sz["out"], sz["hi"])

            def ff1_after(i, c, first=False, tail=False):
                def tap(i, b):
                    act.wait_ge(ff_u, 2 * i + b + 1)
                    for t in range(2):
                        j = 2 * i + 44 * b + t
                        m = nc.scalar.activation(CV[:, t], U[:, t], ACT.Identity, bias=vdyn("conv_b", j), scale=vdyn("conv_w2", j))
                    m.then_inc(ff_c, 1)
                if not first:
                    if c == 0:
                        act.wait_ge(ff_conv, i)
                        nc.scalar.activation(GL, CV, ACT.Gelu_apprx_tanh).then_inc(ff_gelu, 1)
                    if c == 3:
                        tap(i - 1, 1)
                    if c == 5:
                        act.wait_ge(ff_h, i)
                        nc.scalar.activation(FF[:, ds(2 * (i - 1), 2), 0], HF, ACT.Copy).then_inc(ff_hi, 1)
                if not tail and c == 7:
                    tap(i, 0)

            def ff2_after(i, c, first=False, tail=False):
                if not first:
                    if c == 4:
                        act.wait_ge(ff_h, FB + i)
                        nc.scalar.activation(FF[:, ds(2 * (i - 1), 2), 0], HF, ACT.Copy).then_inc(ff_hi, 1)
                if not tail and c == 7:
                    act.wait_ge(ff_u, 2 * FB + i + 1)
                    nc.scalar.activation(GL, U, ACT.Silu).then_inc(ff_gelu, 1)

            def merge_after(i, c, first=False, tail=False):
                second, c = c // 18, c % 18
                j = 2 * i + second

                def gate(j, g):
                    act.wait_ge(mg_logit, 3 * j + g + 1)
                    nc.scalar.activation(GS, GT, ACT.Sigmoid).then_inc(mg_gate, 1)
                if not first or second:
                    if c == 1:
                        gate(j - 1, 2)
                    if c == 4:
                        act.wait_ge(mg_m, j)
                        nc.scalar.activation(MM[:, ds(2 * (j - 1), 2), 0], MA, ACT.Copy).then_inc(mg_hi, 1)
                if not tail:
                    if c == 7:
                        gate(j, 0)
                    if c == 13:
                        gate(j, 1)

            act.sem_inc(part_sq, 2)
            act.wait_ge(warm_set, 1)
            nc.scalar.activation(st[:, 120:121], st[:, 120:121], ACT.Sqrt)
            act.wait_ge(x_in[0], 16)
            nc.scalar.activation(xn0[:, 0], x0[:, 0], ACT.Square, accum_out=st[:, 0:1])
            act.wait_ge(x_in[1], 16)
            nc.scalar.activation(xn0[:, 1, HALF[1]], x0[:, 1, HALF[1]], ACT.Square, accum_out=st[:, 117:118]).then_inc(norm["sq"], 1)
            root(0)
            scale_act(0, x0, xn0)

            def first_turn(c):
                if c == 0:
                    act.wait_ge(vec_ready, 1)
                if c < 4:
                    turn_act(0, (2 * c, 2 * c + 1))
                if c == 3:
                    act.wait_ge(const_in, 16 * 9)
                    nc.scalar.activation(gws[:, :, 0], gw, ACT.Copy).then_inc(gw_hi, 1)
                if c == 5:
                    act.wait_ge(lam_sums, 1)
                    nc.scalar.activation(lsum[:, 2:4], lsum[:, 0:2], ACT.Exp).then_inc(lam_exps, 1)

            def bias_after(i, c, first):
                if c == 3:
                    for q in range(4):
                        act.wait_ge(flipped[0], 4 * i + q + 1)
                        nc.scalar.activation(bias1[:, ds(8 * i + 2 * q, 2)].rearrange("p h t -> p (h t)"), ps[:, 4 + q],
                                             ACT.Copy).then_inc(bias_ready[0], 1)

            stream(diff_qk, None, first_turn)

            def gates_act(c):
                if c == 1:
                    act.wait_ge(gate_sum, 1)
                    nc.scalar.activation(gates, gates, ACT.Sigmoid).then_inc(gate_ready, 1)

            stream(diff_v, bias_after, gates_act)
            stream(nsa_q, lambda i, c, first: diff_after(i, c))

            def last_diff(i, c, first):
                diff_after(3, c)
                if c == 6:
                    for b, (src, dst) in enumerate(((kblk, ksp), (vblk, vsp))):
                        act.wait_ge(blk_sum, b + 1)
                        nc.scalar.activation(dst[:, :, 0], src, ACT.Copy).then_inc(blk_hi, 1)

            stream(nsa_k, last_diff)

            def finish_diff(i, c, first):
                if c == 1:
                    act.wait_ge(dn["var"], 1)
                    nc.scalar.activation(st[:, 80:96], st[:, 64:80], ACT.Sqrt).then_inc(dn["root"], 1)
                if c == 6:
                    for q in range(4):
                        act.wait_ge(dn["turned"], q + 1)
                        nc.scalar.activation(MIX[:, 2 * q:2 * q + 2, 0], ps[:, 4 + q].rearrange("p (c t) -> p c t", c=2), ACT.Copy,
                                             scale=st[:, 96:97]).then_inc(dn["round"], 1)

            stream(squeeze, finish_diff)

            def compressed(i, c, first):
                if c == 2:
                    act.wait_ge(hid_sum, 2)
                    nc.scalar.activation(hid_rows[0:2 * NC], hid_rows[0:2 * NC], ACT.Gelu_apprx_tanh).then_inc(hid_gelu, 1)
                if c == 4:
                    act.wait_ge(hid_turned, 1)
                    nc.scalar.activation(hid.rearrange("p b k n -> p (b k n)"), ps[:, 7, 0:8 * NC], ACT.Copy).then_inc(hid_ready, 1)
                if c == 5:
                    act.wait_ge(cmp_psum, 1)
                    nc.scalar.activation(kcT, ps[:, 4, 0:2 * NC], ACT.Copy)
                    for j in range(4):
                        r = slice(32 * j, 32 * j + NC)
                        m = nc.scalar.activation(vcr[r].rearrange("p g e -> p (g e)"), ps[r, 5, 0:T], ACT.Copy)
                    m.then_inc(cmp_sb, 1)
                if c == 6:
                    act.wait_ge(cs_logit, 1)
                    nc.scalar.activation(cl, cl, ACT.Exp).then_inc(cs_exp, 1)

            def turned_copy(c):
                if c == 0:
                    act.wait_ge(cs_turned, 1)
                    nc.scalar.activation(PcT.rearrange("p g t -> p (g t)"), ps[:, 4], ACT.Copy).then_inc(cs_ready, 1)

            stream(nsa_v, compressed)
            stream(out_a, nsa_after, turned_copy)
            src1, src3 = lambda i, b: tmp1[:, b % 2], lambda i, b: tmp2[:, b % 2]
            stream(out_b, squares(1, out_b, src1, xn1[:, :, 0:NB]))

            def second_norm(n, ph, src, sq, x, xn, c):
                if c == 1:
                    warm(n)
                last_squares(n, ph, src, sq, c)
                if c == 2:
                    root(n)
                    act.drain()
                    squares_of_halves(n + 1, x, xn)
                    root(n + 1)
                    scale_act(n + 1, x, xn)
                    turn_act(n + 1)

            stream(up1, ff1_after, lambda c: second_norm(1, out_b, src1, xn1[:, :, 0:NB], X1, xn1, c))
            stream(down1, squares(3, down1, src3, junk), lambda c: ff1_after(FB, c, tail=True))

            def bias2_after(c):
                if c == 5:
                    for q in range(4):
                        act.wait_ge(flipped[1], q + 1)
                        nc.scalar.activation(bias2[:, 2 * q:2 * q + 2].rearrange("p h t -> p (h t)"), ps[:, 4 + q], ACT.Copy).then_inc(bias_ready[1], 1)

            stream(sb_qk, None, lambda c: second_norm(3, down1, src3, junk, X2, xn2, c))
            stream(sb_v, None, bias2_after)
            stream(pool_u, sb_after)
            act.wait_ge(spilled[1], 16)

            def pool_round(*groups):
                for g in groups:
                    act.wait_ge(pooled, g + 1)
                    nc.scalar.activation(PS[:, 2 * g:2 * g + 2, 0], PQ[:, g], ACT.Copy).then_inc(pool_hi, 1)

            def moba_v_after(i, c, first):
                sb_after(i + 2, c, first)
                if first and c == 7:
                    pool_round(0, 1)
                if not first and c in (3, 6):
                    pool_round(2 if c == 3 else 3)

            stream(moba_v, moba_v_after)
            stream(pool_w)

            def proj_round(c):
                if 1 <= c <= 4:
                    g = c - 1
                    act.wait_ge(proj_sum, g + 1)
                    for t in range(2):
                        m = nc.scalar.activation(YB[:, 2 * g + t, 0], PQ[:, g, t], ACT.Copy, scale=v("pool_scale_2", 2 * g + t))
                    m.then_inc(proj_hi, 1)

            stream(moba_qk, lambda i, c, first: None if first else moba_after(i - 1, c), proj_round)
            stream(merge, merge_after, lambda c: moba_after(3, c))
            cols_of = lambda ph, x: lambda i, b: x[:, :, ds(NB * (ph.nb * i + b), NB)]
            stream(out_2, squares(5, out_2, cols_of(out_2, X3), junk3), lambda c: merge_after(4, c, tail=True))

            def third_norm(c):
                if c == 1:
                    warm(5)
                last_squares(5, out_2, cols_of(out_2, X3), junk3, c)
                if c == 2:
                    root(5)
                    scale_act(5, X3, xn3)
                    turn_act(5)

            stream(up2, ff2_after, third_norm)
            stream(down2, squares(6, down2, cols_of(down2, Xd), junk), lambda c: ff2_after(FB, c, tail=True))
            warm(6)
            last_squares(6, down2, cols_of(down2, Xd), junk, 2)
            root(6)
            act.wait_ge(norm["rstd"], 7)
            for half in HALF:
                nc.scalar.activation(Yd[:, 0, half], Yd[:, 0, half], ACT.Copy, scale=st[:, 24:25]).then_inc(result_a, 1)

        @block.vector
        def _(dve):
            def split_unit(ph, i, c):
                s = ph.slot_of(c)
                dve.wait_ge(hi_done, ph.units(i, c))
                nc.vector.tensor_tensor(spl[:, s % SPL, :, 1], raw[:, s], spl[:, s % SPL, :, 0].bitcast(F32),
                                        ALU.subtract).then_inc(split, 1)

            def empty(ph, i, b, dst, n=NB):
                dve.wait_ge(used, SPL + ph.units(i, sum(ph.blocks[:b + 1]) - 1))
                src = ps[:, 2 * (b % 2):2 * (b % 2) + 2, 0:2 * n].rearrange("p h (a n) -> p h n a", a=2)
                nc.vector.tensor_reduce(dst, src, AX.X, ALU.add).then_inc(emptied, 1)

            def stream(ph, emptyb=None, after=None, carried=None, steps=None):
                def body(i, first):
                    for c in range(ph.n):
                        split_unit(ph, i, c)
                        if first and carried:
                            carried(c)
                        for e, b, is_late in ph.ends():
                            if emptyb and c == e and not is_late:
                                emptyb(i, b)
                            if emptyb and c == e and is_late and not first:
                                emptyb(i - 1, b)
                        if after:
                            after(i, c)
                        if steps:
                            steps(i, c, first)
                body(0, True)
                if ph.iters > 1:
                    with dve.Fori(1, ph.iters) as i:
                        body(i, False)

            def late(ph, emptyb):
                def carried(c):
                    for e, b, is_late in ph.ends():
                        if is_late and c == e:
                            emptyb(ph.iters - 1, b)
                return carried

            def finish(ph, emptyb):
                for e, b, is_late in ph.ends():
                    if is_late:
                        emptyb(ph.iters - 1, b)

            def tiles(ph, dst):
                return lambda i, b: empty(ph, i, b, dst[:, ds(ph.nb * 2 * i + 2 * b, 2)])

            def columns(ph, dst):
                return lambda i, b: empty(ph, i, b, dst[:, :, ds(NB * (ph.nb * i + b), NB)])

            def rstd(n):
                q = 4 * n
                dve.drain()
                nc.vector.tensor_scalar(st[:, q:q + 2], st[:, q:q + 2], 1.0 / D, EPS, ALU.mult, ALU.add).then_inc(norm["var"], 1)
                dve.wait_ge(norm["root"], n + 1)
                nc.vector.reciprocal(st[:, q:q + 2], st[:, q + 2:q + 4]).then_inc(norm["rstd"], 1)
                dve.drain()

            def rstd_of(n, parts_, count):
                dve.wait_ge(part_sq, 2 + PIECES[n] + count)
                nc.vector.tensor_reduce(st[:, 4 * n:4 * n + 2], parts_, AX.X, ALU.add)
                rstd(n)

            def scale_dve(n, src, dst):
                for part in QUARTER:
                    nc.vector.tensor_scalar(dst[:, 1, part], src[:, 1, part], st[:, 4 * n + 1:4 * n + 2], None, ALU.mult).then_inc(norm["scaled_d"], 1)

            def turn_dve(n, qs=range(8)):
                s, name = norm, NORMS[n][2]
                for q in qs:
                    dve.wait_ge(s["round"], 8 * TURN[n] + q + 1)
                    for c in range(2):
                        k = 2 * q + c
                        m = nc.vector.scalar_tensor_tensor(HA[:, k, 1], ps[:, 4 + q % 4, c * T:(c + 1) * T], v(name, k),
                                                           HA[:, k, 0].bitcast(F32), ALU.mult, ALU.subtract)
                    m.then_inc(s["done"], 1)

            def gained(ph, n, tmp, y, gain, gain_ready, add=False):
                def emptyb(i, b):
                    m = ph.nb * i + b
                    t, yb, cols = tmp[:, b % 2], y[:, :, ds(NB * m, NB)], ds(NB * m, NB)
                    dve.drain()
                    dve.wait_ge(part_sq, PIECES[n] + m + 1)
                    empty(ph, i, b, t)
                    dve.drain()
                    if add:
                        nc.vector.tensor_tensor(t, t, yb, ALU.add)
                        dve.drain()
                    dve.sem_inc(part_in, 1)
                    dve.wait_ge(gain_ready, 16)
                    nc.vector.tensor_tensor(yb, t, gain[:, cols].unsqueeze(1).to_broadcast([P, 2, NB]), ALU.mult)
                return emptyb

            def added(ph, x, x_in_, y=None, gain=None, gain_ready=None):
                def emptyb(i, b):
                    m = ph.nb * i + b
                    cols = ds(NB * m, NB)
                    xb, t = x[:, :, cols], tmp2[:, b % 2]
                    dve.drain()
                    empty(ph, i, b, t)
                    dve.drain()
                    dve.wait_ge(x_in_, 16)
                    nc.vector.tensor_tensor(xb, xb, t, ALU.add).then_inc(part_in, 1)
                    if gain is not None:
                        dve.drain()
                        dve.wait_ge(gain_ready, 16)
                        nc.vector.tensor_tensor(y[:, :, cols], xb, gain[:, cols].unsqueeze(1).to_broadcast([P, 2, NB]), ALU.mult)
                return emptyb

            TILE = [slice(0, P), slice(P, 3 * P)]

            def softmax_logits(n, j, bank, maps, buf, scale, bias, h):
                dve.wait_ge(scores, n + 1)
                for a in range(2):
                    w_ = P * (a + 1)
                    bt = bias[:, ds(h), T - w_:T].to_broadcast([P, maps, w_]) if maps > 1 else bias[:, ds(h), T - w_:T]
                    nc.vector.scalar_tensor_tensor(buf[:, 0:maps, TILE[a]], ps[:, bank:bank + maps, TILE[a]], scale, bt, ALU.mult, ALU.add)
                dve.drain()
                for a in range(2):
                    at_ = 32 + 16 * j + 2 * a
                    m = nc.vector.tensor_reduce(st[:, at_:at_ + maps], buf[:, 0:maps, TILE[a]], AX.X, ALU.max, negate=True)
                m.then_inc(logits, 1)

            def softmax_sums(n, j, maps, guard=True):
                dve.wait_ge(exps, n + 1)
                sv = st[:, 36 + 16 * j:40 + 16 * j].rearrange("p (a m) -> p a m", m=2)[:, :, 0:maps]
                r = st[:, 40 + 16 * j:44 + 16 * j].rearrange("p (a m) -> p a m", m=2)[:, :, 0:maps]
                if guard:
                    nc.vector.tensor_scalar(sv, sv, TINY, None, ALU.max)
                    dve.drain()
                nc.vector.reciprocal(r, sv)
                dve.drain()
                return r

            def scale_probs(buf, r, maps):
                for a in range(2):
                    for m in range(maps):
                        t = nc.vector.tensor_scalar(buf[:, m, TILE[a]], buf[:, m, TILE[a]], r[:, a, m:m + 1], None, ALU.mult)
                return t

            def diff_after(i, c):
                if c != 2:
                    return
                for j in range(2):
                    softmax_logits(2 * i + j, j, 4 + 2 * j, 2, LG[:, j], 64 ** -0.5, bias1, 2 * i + j)
                for j in range(2):
                    r = softmax_sums(2 * i + j, j, 2)
                    nc.vector.tensor_scalar(r[:, :, 1], r[:, :, 1], neg_lam, None, ALU.mult)
                    dve.drain()
                    for a in range(2):
                        nc.vector.tensor_scalar(LG[:, j, 1, TILE[a]], LG[:, j, 1, TILE[a]], r[:, a, 1:2], None, ALU.mult)
                    dve.drain()
                    for a in range(2):
                        m = nc.vector.scalar_tensor_tensor(LG[:, j, 0, TILE[a]], LG[:, j, 0, TILE[a]], r[:, a, 0:1], LG[:, j, 1, TILE[a]],
                                                           ALU.mult, ALU.add)
                    m.then_inc(probs, 1)

            def head_split(n, j, dst):
                dve.wait_ge(head_hi, n - HEADS + 1)
                nc.vector.tensor_tensor(dst[1], ps[:, 4 + 2 * j, 0:T], dst[0].bitcast(F32), ALU.subtract).then_inc(head_free, 1)

            def parts(t, h):
                return [t[:, ds(h), k].rearrange("p a t -> p (a t)") for k in range(2)]

            def nsa_after(g, c):
                pair, c = c // 4, c % 4
                hs = [4 * g + 2 * pair + j for j in range(2)]
                if c == 1:
                    for j, h in enumerate(hs):
                        softmax_logits(HEADS + h, j, 4 + 2 * j, 2, LG[:, j], 128 ** -0.5, bias1, 8 + h)
                    for j, h in enumerate(hs):
                        r = softmax_sums(HEADS + h, j, 2)
                        nc.vector.tensor_tensor(r, r, gates[:, :, ds(3 * h + 1, 2)], ALU.mult)
                        dve.drain()
                        scale_probs(LG[:, j], r, 2).then_inc(probs, 1)
                if c == 3:
                    for j, h in enumerate(hs):
                        head_split(HEADS + h, j, parts(MIX, 8 + h))

            def moba_after(pair, c):
                hs = [2 * pair + j for j in range(2)]
                if c == 4:
                    for j, h in enumerate(hs):
                        softmax_logits(2 * HEADS + h, j, 4 + 2 * j, 1, LM[:, j:j + 1], 128 ** -0.5, bias2, h)
                    for j, h in enumerate(hs):
                        r = softmax_sums(2 * HEADS + h, j, 1, guard=False)
                        scale_probs(LM[:, j:j + 1], r, 1).then_inc(probs, 1)
                if c == 7:
                    for j, h in enumerate(hs):
                        head_split(2 * HEADS + h, j, parts(YA, h))

            def sb_after(i, c):
                if c == 2:
                    for j in range(2):
                        dve.wait_ge(sz["z"], 2 * i + j + 1)
                        m = nc.vector.scalar_tensor_tensor(SZ[:, j, 0], ps[:, 4 + 2 * j, 0:3 * P], 128 ** -0.5, k1[:, SBMASK:SBMASK + 3 * P],
                                                           ALU.mult, ALU.add)
                    m.then_inc(sz["zm"], 1)
                if c == 3:
                    dve.wait_ge(sz["ln"], i + 1)
                    nc.vector.scalar_tensor_tensor(SZ[:, :, 2], SZ[:, :, 0], 0.0, SZ[:, :, 1], ALU.max, ALU.add).then_inc(sz["sp"], 1)
                if c == 4:
                    for j in range(2):
                        dve.wait_ge(sz["aft"], 2 * i + j + 1)
                        m = nc.vector.tensor_tensor(SZ[:, j, 3], SZ[:, j, 0], ps[:, 5 + 2 * j, 0:3 * P], ALU.add)
                    m.then_inc(sz["e"], 1)
                if c == 7:
                    for j in range(2):
                        h = 2 * i + j
                        dve.wait_ge(sz["hi"], h + 1)
                        d = parts(YC, h)
                        nc.vector.tensor_tensor(d[1], ps[:, 4 + 2 * j, 0:T], d[0].bitcast(F32), ALU.subtract).then_inc(sz["free"], 1)

            def split_hidden(n, i):
                dve.wait_ge(ff_hi, n + 1)
                nc.vector.tensor_tensor(FF[:, ds(2 * i, 2), 1], HF, FF[:, ds(2 * i, 2), 0].bitcast(F32), ALU.subtract).then_inc(ff_done, 1)

            def empty_u(ph, i, b):
                dve.drain()
                empty(ph, i, b, U)
                dve.drain()
                dve.sem_inc(ff_u, 1)

            def ff1_after(i, c, first=False, tail=False):
                def taps(i, b):
                    dve.wait_ge(ff_c, 2 * i + b + 1)
                    for back in (1, 2):
                        for t in range(2):
                            cw = vdyn(f"conv_w{2 - back}", 2 * i + 44 * b + t)
                            m = nc.vector.scalar_tensor_tensor(CV[:, t, back:], U[:, t, 0:T - back], cw, CV[:, t, back:], ALU.mult, ALU.add)
                        if back == 1:
                            dve.drain()
                    return m
                if not first:
                    if c == 2:
                        empty_u(up1, i - 1, 1)
                    if c == 3:
                        taps(i - 1, 1)
                    if c == 4:
                        dve.drain()
                        dve.wait_ge(ff_gelu, i)
                        nc.vector.tensor_tensor(HF, GL, CV, ALU.mult).then_inc(ff_h, 1)
                    if c == 6:
                        split_hidden(i - 1, i - 1)
                if not tail:
                    if c == 6:
                        empty_u(up1, i, 0)
                    if c == 7:
                        taps(i, 0).then_inc(ff_conv, 1)

            def ff2_after(i, c, first=False, tail=False):
                if not first:
                    if c == 2:
                        dve.drain()
                        empty(up2, i - 1, 1, CV)
                    if c == 3:
                        dve.drain()
                        dve.wait_ge(ff_gelu, FB + i)
                        nc.vector.tensor_tensor(HF, GL, CV, ALU.mult).then_inc(ff_h, 1)
                    if c == 5:
                        split_hidden(FB + i - 1, i - 1)
                if not tail and c == 6:
                    empty_u(up2, i, 0)

            nc.vector.sem_inc(split, RAW)
            nc.vector.sem_inc(emptied, 2)
            nc.vector.sem_inc(head_free, 2)
            nc.vector.sem_inc(sz["free"], 2)
            nc.vector.memset(st[:, 120:121], 1.0).then_inc(warm_set, 1)
            dve.wait_ge(x_in[1], 16)
            nc.vector.tensor_tensor_reduce(out=xn0[:, 1, HALF[0]], in0=x0[:, 1, HALF[0]], in1=x0[:, 1, HALF[0]], scale=1.0, scalar=0.0,
                                           op0=ALU.mult, op1=ALU.add, accum_out=st[:, 1:2])
            dve.drain()
            dve.wait_ge(norm["sq"], 1)
            nc.vector.tensor_tensor(st[:, 1:2], st[:, 1:2], st[:, 117:118], ALU.add)
            rstd(0)
            scale_dve(0, x0, xn0)
            dve.wait_ge(vec_turned, 1)
            nc.vector.tensor_copy(vec[:, 0:VAT["conv_b"]], ps[:, 0, 0:VAT["conv_b"]])
            dve.drain()
            nc.vector.tensor_scalar(st[:, 96:97], v("diff_subln"), 1.0 - LAM_INIT, None, ALU.mult).then_inc(vec_ready, 1)

            def first_turn(c):
                if c < 4:
                    turn_dve(0, (2 * c, 2 * c + 1))
                if c == 3:
                    dve.wait_ge(gw_hi, 1)
                    nc.vector.tensor_tensor(gws[:, :, 1], gw, gws[:, :, 0].bitcast(F32), ALU.subtract).then_inc(gw_split, 1)
                if c == 4:
                    lv = lamv.rearrange("p (a b) n -> p a b n", b=2)
                    nc.vector.tensor_tensor(lamp, lv[:, :, 0], lv[:, :, 1], ALU.mult)
                    dve.drain()
                    nc.vector.tensor_reduce(lsum[:, 0:2], lamp, AX.X, ALU.add).then_inc(lam_sums, 1)
                if c == 5:
                    dve.wait_ge(lam_exps, 1)
                    nc.vector.scalar_tensor_tensor(neg_lam, lsum[:, 3:4], -LAM_INIT, lsum[:, 2:3], ALU.add, ALU.subtract)
                if c == 7:
                    dve.wait_ge(vec_turned, 2)
                    nc.vector.tensor_copy(vec[:, VAT["conv_b"]:], ps[:, 6, VAT["conv_b"]:NVEC])
                    dve.wait_ge(table_psum, 1)
                    nc.vector.tensor_copy(rbias[0:16, 0, 0:T], ps[0:16, 7, 0:T])
                    nc.vector.tensor_copy(rbias[0:8, 1, 0:T], ps[0:8, 7, T:2 * T])
                    nc.vector.memset(rbias[0:16, :, T:384], NEG).then_inc(table_sb, 1)
                    dve.wait_ge(gate_psum, 1)
                    nc.vector.tensor_reduce(gsum[0:48], ps[0:48, 4].rearrange("p (a n) -> p n a", a=2), AX.X, ALU.add).then_inc(gate_part, 1)

            e_qk, e_v, e_q = tiles(diff_qk, QK), columns(diff_v, DV), tiles(nsa_q, NQ)
            stream(diff_qk, e_qk, carried=first_turn)

            def gates_dve(c):
                late(diff_qk, e_qk)(c)
                if c == 0:
                    dve.wait_ge(gate_psum, 2)
                    nc.vector.tensor_reduce(gates, ps[:, 5, 0:96].rearrange("p (h a n) -> p h n a", h=2, a=2), AX.X, ALU.add).then_inc(gate_sum, 1)

            stream(diff_v, e_v, carried=gates_dve)
            dve.wait_ge(bias_ready[0], 12)
            dve.wait_ge(gate_ready, 1)
            stream(nsa_q, e_q, diff_after, late(diff_v, e_v))
            e_k = lambda i, b: empty(nsa_k, i, b, NKs[:, 2 * b:2 * b + 2])
            e_nv = lambda i, b: empty(nsa_v, i, b, NVs[:, :, b])

            def last_diff(i, c):
                diff_after(3, c)
                if c == 4:
                    dve.drain()
                    for b, (dst, name) in enumerate(((kblk, "cmp_pos_k"), (vblk, "cmp_pos_v"))):
                        pos = v(name, 0, 32).unsqueeze(2).to_broadcast([P, 32, NC])
                        for g in range(2):
                            src = NQ[:, 8 + 2 * b + g]
                            win = bass.AP(src.tensor, src.offset, [src.ap[0], [1, 32], [16, NC]])
                            m = nc.vector.tensor_tensor(dst[:, :, g * NC:(g + 1) * NC], win, pos, ALU.add)
                        m.then_inc(blk_sum, 1)
                if c == 7:
                    for b, (src, dst) in enumerate(((kblk, ksp), (vblk, vsp))):
                        dve.wait_ge(blk_hi, b + 1)
                        nc.vector.tensor_tensor(dst[:, :, 1], src, dst[:, :, 0].bitcast(F32), ALU.subtract).then_inc(blk_split, 1)

            stream(nsa_k, e_k, last_diff, late(nsa_q, e_q))

            def between(i, c):
                if c == 0:
                    dve.wait_ge(head_free, 2 + HEADS)
                    nc.vector.tensor_scalar(st[:, 64:80], st[:, 64:80], 1.0 / P, EPS, ALU.mult, ALU.add).then_inc(dn["var"], 1)
                if c == 1:
                    dve.wait_ge(dn["root"], 1)
                    nc.vector.reciprocal(st[:, 64:80], st[:, 80:96])
                    dve.drain()
                    od = OD.rearrange("p a h e -> p (a h) e")
                    nc.vector.tensor_tensor(od, od, st[:, 64:80].unsqueeze(2).to_broadcast([P, 16, P]), ALU.mult).then_inc(dn["scaled"], 1)
                if c == 6:
                    for q in range(4):
                        dve.wait_ge(dn["round"], q + 1)
                        nc.vector.scalar_tensor_tensor(MIX[:, 2 * q:2 * q + 2, 1], ps[:, 4 + q].rearrange("p (c t) -> p c t", c=2),
                                                       st[:, 96:97], MIX[:, 2 * q:2 * q + 2, 0].bitcast(F32), ALU.mult,
                                                       ALU.subtract).then_inc(dn["done"], 1)

            def e_sq(i, b):
                dve.wait_ge(used, SPL + squeeze.units(0, 8 * b + 7))
                nc.vector.tensor_reduce(hid_rows[0:2 * NC, b], ps[0:2 * NC, 2 * b].rearrange("p (a n) -> p n a", a=2), AX.X, ALU.add).then_inc(emptied, 1)
                dve.drain()
                dve.sem_inc(hid_sum, 1)

            stream(squeeze, e_sq, between, late(nsa_k, e_k))
            ah = cl.rearrange("p a h c -> p (a h) c")
            cm = st[:, 100:116]
            cmb = cm.unsqueeze(2).to_broadcast([P, 16, NC])

            def compressed(i, c):
                if c == 6:
                    dve.wait_ge(w2_in, 48)
                    dve.wait_ge(cs_psum, 1)
                    for a in range(2):
                        nc.vector.scalar_tensor_tensor(cl[:, a], ps[:, 6 + a, 0:HEADS * NC].rearrange("p (h c) -> p h c", c=NC), 128 ** -0.5,
                                                       cmk[:, a:a + 1].to_broadcast([P, HEADS, NC]), ALU.mult, ALU.add)
                    dve.drain()
                    nc.vector.tensor_reduce(cm, ah, AX.X, ALU.max)
                    dve.drain()
                    nc.vector.tensor_tensor(ah, ah, cmb, ALU.subtract).then_inc(cs_logit, 1)
                if c == 7:
                    dve.wait_ge(cs_exp, 1)
                    for a in range(2):
                        nc.vector.tensor_tensor(cl[:, a], cl[:, a], cmk[:, 2 + a:3 + a].to_broadcast([P, HEADS, NC]), ALU.mult)
                    nc.vector.memset(PC, 0.0)
                    dve.drain()
                    nc.vector.tensor_reduce(cm, ah, AX.X, ALU.add)
                    dve.drain()
                    nc.vector.tensor_scalar(cm, cm, TINY, None, ALU.max)
                    dve.drain()
                    nc.vector.reciprocal(cm, cm)
                    dve.drain()
                    cm2 = cm.rearrange("p (a h) -> p a h", a=2)
                    nc.vector.tensor_tensor(cm2, cm2, gates.rearrange("p a (h c) -> p a h c", c=3)[:, :, :, 0], ALU.mult)
                    dve.drain()
                    nc.vector.tensor_tensor(PC.rearrange("p a h c -> p (a h) c")[:, :, 0:NC], ah, cmb, ALU.mult).then_inc(cs_prob, 1)

            stream(nsa_v, e_nv, compressed, late(squeeze, e_sq))
            e_oa = columns(out_a, Y1)

            e_ob = gained(out_b, 1, tmp1, Y1, gain1, gain_in[0], add=True)

            stream(out_a, e_oa, nsa_after, late(nsa_v, e_nv))
            dve.drain()
            dve.sem_inc(nsa_done, 1)
            stream(out_b, e_ob, carried=late(out_a, e_oa))

            def second_norm(n, ph, e, y, x, xn, c, x_in_, dst):
                late(ph, e)(c)
                if c == 2:
                    rstd_of(n, sums, 8)
                    dve.wait_ge(x_in_, 16)
                    for half in HALF:
                        for a in range(2):
                            nc.vector.scalar_tensor_tensor(dst[:, a, half], y[:, a, half], st[:, 4 * n + a:4 * n + a + 1], x[:, a, half],
                                                           ALU.mult, ALU.add).then_inc(part_in, 1)
                    dve.drain()
                    dve.sem_inc(x_ready[n // 2], 1)
                    rstd_of(n + 1, sums2, 4)
                    scale_dve(n + 1, dst, xn)
                    turn_dve(n + 1)

            def up1_carried(c):
                second_norm(1, out_b, e_ob, Y1, X1, xn1, c, x_reloaded[0], X1)
                if c == 4:
                    dve.wait_ge(spilled[0], 16)

            stream(up1, carried=up1_carried, steps=ff1_after)
            e_d1 = gained(down1, 3, tmp2, Yd, gain2, gain_in[1])
            stream(down1, e_d1, carried=lambda c: ff1_after(FB, c, tail=True))
            e_sqk, e_sv = tiles(sb_qk, SQK), columns(sb_v, SV)
            e_pu, e_mv = tiles(pool_u, UP), columns(moba_v, MV)
            stream(sb_qk, e_sqk, carried=lambda c: second_norm(3, down1, e_d1, Yd, Xd, xn2, c, x_reloaded[1], X2))
            stream(sb_v, e_sv, carried=late(sb_qk, e_sqk))
            stream(pool_u, e_pu, sb_after, late(sb_v, e_sv))
            dve.wait_ge(bias_ready[1], 4)

            def pool_los(*groups):
                for g in groups:
                    dve.wait_ge(pool_hi, g + 1)
                    nc.vector.tensor_tensor(PS[:, 2 * g:2 * g + 2, 1], PQ[:, g], PS[:, 2 * g:2 * g + 2, 0].bitcast(F32),
                                            ALU.subtract).then_inc(pool_split, 1)

            def moba_v_after(i, c, first):
                sb_after(i + 2, c)
                if not first and c == 0:
                    pool_los(0, 1)
                if not first and c in (3, 7):
                    pool_los(2 if c == 3 else 3)

            stream(moba_v, e_mv, carried=late(pool_u, e_pu), steps=moba_v_after)
            stream(pool_w)

            def project(c):
                if c == 0:
                    late(moba_v, e_mv)(2)
                if c < 4:
                    dve.wait_ge(used, SPL + pool_w.units(0, c // 2))
                    m = nc.vector.tensor_reduce(PQ[:, c], ps[:, 2 * c:2 * c + 2].rearrange("p h (a n) -> p h n a", a=2), AX.X, ALU.add)
                    if c < 2:
                        m.then_inc(emptied, 1)
                    dve.drain()
                    dve.sem_inc(proj_sum, 1)
                if 2 <= c < 6:
                    g = c - 2
                    dve.wait_ge(proj_hi, g + 1)
                    for t in range(2):
                        m = nc.vector.scalar_tensor_tensor(YB[:, 2 * g + t, 1], PQ[:, g, t], v("pool_scale_2", 2 * g + t),
                                                           YB[:, 2 * g + t, 0].bitcast(F32), ALU.mult, ALU.subtract)
                    m.then_inc(pool_done, 1)

            def e_mqk(i, b):
                empty(moba_qk, i, b, MQK[:, ds(8 * b + 2 * i, 2)])

            stream(moba_qk, e_mqk, carried=project, steps=lambda i, c, first: None if first else moba_after(i - 1, c))

            def last_heads(c):
                late(moba_qk, e_mqk)(c)
                moba_after(3, c)

            def merge_after(i, c, first=False, tail=False):
                second, c = c // 18, c % 18
                j = 2 * i + second
                this, that = (i, 6 * second), (i - 1 + second, 6 - 6 * second)

                def logits_(at_, g):
                    dve.drain()
                    empty(merge, at_[0], at_[1] + 2 * g, GT)
                    dve.drain()
                    dve.sem_inc(mg_logit, 1)

                def gated(at_, j, g):
                    dve.drain()
                    empty(merge, at_[0], at_[1] + 2 * g + 1, BR)
                    dve.drain()
                    dve.wait_ge(mg_gate, 3 * j + g + 1)
                    nc.vector.tensor_tensor(BR if g else MA, BR, GS, ALU.mult)

                def add():
                    dve.drain()
                    return nc.vector.tensor_tensor(MA, MA, BR, ALU.add)

                if not first or second:
                    if c == 0:
                        logits_(that, 2)
                    if c == 2:
                        gated(that, j - 1, 2)
                    if c == 3:
                        add().then_inc(mg_m, 1)
                    if c == 5:
                        dve.wait_ge(mg_hi, j)
                        nc.vector.tensor_tensor(MM[:, ds(2 * (j - 1), 2), 1], MA, MM[:, ds(2 * (j - 1), 2), 0].bitcast(F32),
                                                ALU.subtract).then_inc(mg_done, 1)
                if not tail:
                    if c == 6:
                        logits_(this, 0)
                    if c == 8:
                        gated(this, j, 0)
                    if c == 12:
                        logits_(this, 1)
                    if c == 14:
                        gated(this, j, 1)
                    if c == 15:
                        add()

            stream(merge, carried=last_heads, steps=merge_after)
            e_o2 = added(out_2, X3, x_reloaded[2])
            stream(out_2, e_o2, carried=lambda c: merge_after(4, c, tail=True))

            def third_norm(c):
                late(out_2, e_o2)(c)
                if c == 2:
                    rstd_of(5, sums, 8)
                    dve.sem_inc(x_ready[2], 1)
                    scale_dve(5, X3, xn3)
                    turn_dve(5)
                if c == 4:
                    dve.wait_ge(spilled[2], 16)

            stream(up2, carried=third_norm, steps=ff2_after)
            e_d2 = added(down2, Xd, x_reloaded[3], Yd, gain2, gain_in[2])
            stream(down2, e_d2, carried=lambda c: ff2_after(FB, c, tail=True))
            finish(down2, e_d2)
            rstd_of(6, sums, 8)
            for half in HALF:
                nc.vector.tensor_scalar(Yd[:, 1, half], Yd[:, 1, half], st[:, 25:26], None, ALU.mult).then_inc(result_d, 1)


_INS = ["x", "pre_mix_norm", "w_in", "lambda_q1", "lambda_k1", "lambda_q2", "lambda_k2", "diff_subln", "cmp_pos_k",
        "cmp_pos_v", "cmp_k_w1", "cmp_k_w2", "cmp_v_w1", "cmp_v_w2", "rel_bias", "w_out", "post_mix_norm",
        "pre_ffn_norm", "w_up", "conv_w", "conv_b", "w_down", "post_ffn_norm", "norm_mix_2", "norm_ffn_2", "w_in_2",
        "w_pool_2", "pool_scale_2", "w_br_a_2", "w_br_b_2", "w_br_c_2", "w_out_2", "w_gate_2", "w_up_2", "w_down_2",
        "rel_bias_2", "norm_final_2"]


def kernel(**inputs):
    import concourse.bacc as bacc
    from concourse.bass_utils import run_bass_kernel_spmd

    nc = bacc.Bacc("TRN2", target_bir_lowering=False, num_devices=1)
    arrays, w = {}, {}
    for name in _INS + ["consts"]:
        a = np.ascontiguousarray(shape_constants() if name == "consts" else inputs[name])
        arrays[f"in_{name}_dram"] = a
        w[name] = nc.dram_tensor(f"in_{name}_dram", a.shape, mybir.dt.from_np(a.dtype), kind="ExternalInput").ap()
    out = nc.dram_tensor("out_0_dram", (1, T, D), F32, kind="ExternalOutput").ap()
    two_blocks(nc, w, out)
    r = run_bass_kernel_spmd(nc, [arrays], core_ids=[0])
    return r.results[0]["out_0_dram"]
```
